# Optimizing a Trainium2 kernel written in Bass

```python
import jax, jax.numpy as jnp
from jax import lax
import numpy as np

D_MODEL = 1024
BATCH = 1
SEQ = 1024
DEPTH = 1
DEC_BATCH = 8
DEC_SEQ = 4
PAST_LEN = 8192
PAGE_SIZE = 128

N_META = 16
CONV_CH = D_MODEL // 2
SCONV_K = 3
GDN_HEADS = 4
GDN_DK = 128
GDN_DV = 128
GDN_CONV_K = 4
CHUNK = 64
FFN_HIDDEN = 4 * D_MODEL
EPS = 1e-6

QKV_W = GDN_HEADS * (2 * GDN_DK + GDN_DV)
O_B = 0
O_C = O_B + CONV_CH
O_H = O_C + CONV_CH
O_QKV = O_H + CONV_CH
O_G = O_QKV + QKV_W
O_A = O_G + GDN_HEADS * GDN_DV
O_BETA = O_A + GDN_HEADS
IN_W = O_BETA + GDN_HEADS
MIX_W = CONV_CH + GDN_HEADS * GDN_DV

kernel_name = 'hymba_shortconv_gated_deltanet_step'

def rmsnorm(x, g):
    xf = x.astype(jnp.float32)
    y = xf * lax.rsqrt(jnp.mean(xf * xf, axis=-1, keepdims=True) + EPS)
    return (y * g.astype(jnp.float32)).astype(x.dtype)

def l2norm(x):
    return x * lax.rsqrt(jnp.sum(x * x, axis=-1, keepdims=True) + EPS)

def causal_dwconv(x, buf, w):
    xp = jnp.concatenate([buf.astype(x.dtype), x], axis=1)
    y = lax.conv_general_dilated(xp, w[:, None, :].astype(x.dtype), window_strides=(1,), padding='VALID',
                                 dimension_numbers=('NWC', 'WIO', 'NWC'), feature_group_count=x.shape[-1])
    return y, xp[:, xp.shape[1] - (w.shape[0] - 1):]

def chunk_len(t):
    return CHUNK if t % CHUNK == 0 else t

def gated_delta_chunked(q, k, v, g, beta, state, chunk):
    b, t, h, _ = q.shape
    dv = v.shape[-1]
    n = t // chunk

    def blocks(a):
        a = a.reshape((b, n, chunk, h) + a.shape[3:])
        return jnp.moveaxis(jnp.moveaxis(a, 1, 0), 2, 3)

    qc, kc, vc, gc, bc = blocks(q), blocks(k), blocks(v), blocks(g), blocks(beta)
    G = jnp.cumsum(gc, axis=-1)
    idx = jnp.arange(chunk)
    causal = idx[:, None] >= idx[None, :]
    strict = idx[:, None] > idx[None, :]
    decay = jnp.exp(jnp.where(causal, G[..., :, None] - G[..., None, :], -jnp.inf))
    kb = kc * bc[..., None]
    lower = jnp.where(strict, jnp.einsum('nbhid,nbhjd->nbhij', kb, kc) * decay, 0.0)
    eye = jnp.eye(chunk, dtype=jnp.float32)
    rhs = jnp.concatenate([vc * bc[..., None], kb * jnp.exp(G)[..., None]], axis=-1)
    sol = lax.linalg.triangular_solve(eye + lower, rhs, left_side=True, lower=True)
    u, w = sol[..., :dv], sol[..., dv:]
    qk = jnp.einsum('nbhid,nbhjd->nbhij', qc, kc) * decay
    q_dec = qc * jnp.exp(G)[..., None]
    g_last = G[..., -1]
    k_dec = kc * jnp.exp(g_last[..., None] - G)[..., None]

    def step(S, xs):
        u_i, w_i, qk_i, qd_i, kd_i, gl_i = xs
        v_new = u_i - jnp.einsum('bhcd,bhde->bhce', w_i, S)
        o_i = jnp.einsum('bhcd,bhde->bhce', qd_i, S) + jnp.einsum('bhij,bhje->bhie', qk_i, v_new)
        S = S * jnp.exp(gl_i)[..., None, None] + jnp.einsum('bhcd,bhce->bhde', kd_i, v_new)
        return S, o_i

    S, o = lax.scan(step, state, (u, w, qk, q_dec, k_dec, g_last))
    o = jnp.moveaxis(jnp.moveaxis(o, 3, 2), 0, 1).reshape(b, t, h, dv)
    return o, S

def hybrid_layer(h, buf_a, buf_qkv, ssm, segments, norm_mix, w_in, conv_a_w, conv_qkv_w, a_log, dt_bias,
                 gdn_norm, w_out, norm_ffn, w_up, w_down):
    f32 = jnp.float32
    bsz, t, _ = h.shape
    xn = rmsnorm(h, norm_mix)
    z = xn @ w_in
    conv_out, new_a = causal_dwconv(z[..., O_C:O_H] * z[..., O_H:O_QKV], buf_a, conv_a_w)
    y_a = z[..., O_B:O_C] * conv_out
    qkv, new_qkv = causal_dwconv(z[..., O_QKV:O_G], buf_qkv, conv_qkv_w)
    qkv = jax.nn.silu(qkv.astype(f32))
    nq = GDN_HEADS * GDN_DK
    q = l2norm(qkv[..., :nq].reshape(bsz, t, GDN_HEADS, GDN_DK)) * (GDN_DK ** -0.5)
    k = l2norm(qkv[..., nq:2 * nq].reshape(bsz, t, GDN_HEADS, GDN_DK))
    v = qkv[..., 2 * nq:].reshape(bsz, t, GDN_HEADS, GDN_DV)
    g = -jnp.exp(a_log.astype(f32)) * jax.nn.softplus(z[..., O_A:O_BETA].astype(f32) + dt_bias.astype(f32))
    beta = jax.nn.sigmoid(z[..., O_BETA:IN_W].astype(f32))
    S = ssm.astype(f32)
    outs = []
    start = 0
    for seg in segments:
        sl = slice(start, start + seg)
        o_s, S = gated_delta_chunked(q[:, sl], k[:, sl], v[:, sl], g[:, sl], beta[:, sl], S, chunk_len(seg))
        outs.append(o_s)
        start += seg
    o = jnp.concatenate(outs, axis=1)
    gate = z[..., O_G:O_A].reshape(bsz, t, GDN_HEADS, GDN_DV).astype(f32)
    o = rmsnorm(o, gdn_norm) * jax.nn.silu(gate)
    y_b = o.reshape(bsz, t, GDN_HEADS * GDN_DV).astype(h.dtype)
    h = h + jnp.concatenate([y_a, y_b], axis=-1) @ w_out
    u = jax.nn.relu(rmsnorm(h, norm_ffn) @ w_up)
    h = h + (u * u) @ w_down
    return h, new_a, new_qkv, S.astype(ssm.dtype)

def setup_inputs(seed: int = 0) -> dict:
    key = jax.random.key(seed)
    ks = jax.random.split(key, 20)
    nrm = jax.random.normal
    f32 = jnp.float32
    x_prompt = nrm(ks[0], (BATCH, SEQ, D_MODEL), f32)
    x_sample = nrm(ks[1], (DEC_BATCH, DEC_SEQ, D_MODEL), f32)
    state_conv_a = nrm(ks[2], (DEPTH, DEC_BATCH, SCONV_K - 1, CONV_CH), f32)
    state_conv_qkv = nrm(ks[3], (DEPTH, DEC_BATCH, GDN_CONV_K - 1, QKV_W), f32)
    state_ssm = 0.3 * nrm(ks[4], (DEPTH, DEC_BATCH, GDN_HEADS, GDN_DK, GDN_DV), f32)
    meta_tokens = nrm(ks[5], (N_META, D_MODEL), f32)
    norm_mix = 1.0 + 0.02 * nrm(ks[6], (DEPTH, D_MODEL), f32)
    w_in = nrm(ks[7], (DEPTH, D_MODEL, IN_W), f32) * D_MODEL ** -0.5
    conv_a_w = nrm(ks[8], (DEPTH, SCONV_K, CONV_CH), f32) * SCONV_K ** -0.5
    conv_qkv_w = nrm(ks[9], (DEPTH, GDN_CONV_K, QKV_W), f32) * GDN_CONV_K ** -0.5
    a_log = jnp.log(jax.random.uniform(ks[10], (DEPTH, GDN_HEADS), f32, 1.0, 16.0))
    dt = jnp.exp(jax.random.uniform(ks[11], (DEPTH, GDN_HEADS), f32, np.log(1e-3), np.log(1e-1)))
    dt_bias = dt + jnp.log(-jnp.expm1(-dt))
    gdn_norm = 1.0 + 0.02 * nrm(ks[12], (DEPTH, GDN_DV), f32)
    w_out = nrm(ks[13], (DEPTH, MIX_W, D_MODEL), f32) * MIX_W ** -0.5
    norm_ffn = 1.0 + 0.02 * nrm(ks[14], (DEPTH, D_MODEL), f32)
    w_up = nrm(ks[15], (DEPTH, D_MODEL, FFN_HIDDEN), f32) * D_MODEL ** -0.5
    w_down = nrm(ks[16], (DEPTH, FFN_HIDDEN, D_MODEL), f32) * FFN_HIDDEN ** -0.5
    norm_final = 1.0 + 0.02 * nrm(ks[17], (D_MODEL,), f32)
    return {'x_prompt': x_prompt, 'x_sample': x_sample, 'state_conv_a': state_conv_a,
            'state_conv_qkv': state_conv_qkv, 'state_ssm': state_ssm, 'meta_tokens': meta_tokens,
            'norm_mix': norm_mix, 'w_in': w_in, 'conv_a_w': conv_a_w, 'conv_qkv_w': conv_qkv_w,
            'a_log': a_log, 'dt_bias': dt_bias, 'gdn_norm': gdn_norm, 'w_out': w_out,
            'norm_ffn': norm_ffn, 'w_up': w_up, 'w_down': w_down, 'norm_final': norm_final}

def reference(x_prompt, x_sample, state_conv_a, state_conv_qkv, state_ssm, meta_tokens, norm_mix, w_in,
              conv_a_w, conv_qkv_w, a_log, dt_bias, gdn_norm, w_out, norm_ffn, w_up, w_down, norm_final):
    bp, tp, _ = x_prompt.shape
    bs, ts, _ = x_sample.shape
    meta = jnp.broadcast_to(meta_tokens[None].astype(x_prompt.dtype), (bp, N_META, D_MODEL))
    hp = jnp.concatenate([meta, x_prompt], axis=1)
    hs = x_sample
    pa, pq, ps, sa, sq, ss = [], [], [], [], [], []
    for l in range(DEPTH):
        lw = (norm_mix[l], w_in[l], conv_a_w[l], conv_qkv_w[l], a_log[l], dt_bias[l], gdn_norm[l],
              w_out[l], norm_ffn[l], w_up[l], w_down[l])
        hp, a_p, q_p, s_p = hybrid_layer(
            hp, jnp.zeros((bp, SCONV_K - 1, CONV_CH), x_prompt.dtype),
            jnp.zeros((bp, GDN_CONV_K - 1, QKV_W), x_prompt.dtype),
            jnp.zeros((bp, GDN_HEADS, GDN_DK, GDN_DV), state_ssm.dtype), (N_META, tp), *lw)
        hs, a_s, q_s, s_s = hybrid_layer(hs, state_conv_a[l], state_conv_qkv[l], state_ssm[l], (ts,), *lw)
        pa.append(a_p); pq.append(q_p); ps.append(s_p)
        sa.append(a_s.astype(state_conv_a.dtype)); sq.append(q_s.astype(state_conv_qkv.dtype)); ss.append(s_s)
    y_prompt = rmsnorm(hp, norm_final)[:, N_META:]
    y_sample = rmsnorm(hs, norm_final)
    return (y_prompt, y_sample, jnp.stack(pa), jnp.stack(pq), jnp.stack(ps), jnp.stack(sa), jnp.stack(sq), jnp.stack(ss))


_drawn_inputs = setup_inputs


def setup_inputs(seed=0):
    import zlib

    import numpy as np

    out = dict(_drawn_inputs(seed))
    spreads = {}
    factors = {'gdn_norm': 8.0, 'norm_ffn': 3.591, 'norm_final': 2.87}
    for name, (base, spread) in spreads.items():
        noise = np.random.default_rng([zlib.crc32(name.encode()), seed]).standard_normal(out[name].shape)
        drawn = base * np.exp(spread * noise) if base else spread * noise
        out[name] = __import__('jax').numpy.asarray(drawn.astype(out[name].dtype))
    for name, factor in factors.items():
        out[name] = (out[name] * factor).astype(out[name].dtype)
    return out
```

```python
from contextlib import ExitStack

import numpy as np

import concourse.bass as bass
from concourse import mybir

ALU = mybir.AluOpType
ACT = mybir.ActivationFunctionType
AX = mybir.AxisListType
F32 = mybir.dt.float32
F32R = mybir.dt.float32r

P = 128
D = 1024
KT = D // P
SEQ, META, NSEQ, LSEQ = 1024, 16, 8, 4
NH = 4
CONV = D // 2
QKVW = NH * 3 * P
FFN = 4 * D
EPS = 1e-6
NS = NSEQ * LSEQ
C0 = NS + META
NT = 1 + SEQ // P
TOK = C0 + SEQ
PRM = TOK - NS
GROUPS = [(0, C0 + 2 * P), (C0 + 2 * P, 3 * P), (C0 + 5 * P, 3 * P)]
GTILES = [(0, 1, 2), (3, 4, 5), (6, 7, 8)]
O_B, O_C, O_H, O_QKV = 0, CONV, 2 * CONV, 3 * CONV
O_G = O_QKV + QKVW
O_A = O_G + NH * P
SMALL_LEVELS, LEVELS = 4, 7

IN_TILES = ([("k", h, O_QKV + NH * P + P * h) for h in range(NH)] + [("q", h, O_QKV + P * h) for h in range(NH)]
            + [("v", h, O_QKV + 2 * NH * P + P * h) for h in range(NH)] + [("gate", h, O_G + P * h) for h in range(NH)]
            + [x for i in range(CONV // P) for x in (("C", i, O_C + P * i), ("H", i, O_H + P * i), ("B", i, O_B + P * i))])
N_IN = len(IN_TILES)
N_OUT = D // P
N_MIX = N_IN + N_OUT
FG = FFN // D


def tile_cols(t):
    return (0, C0) if t == 0 else (C0 + (t - 1) * P, P)


def constants():
    j, i = np.arange(P)[:, None], np.arange(P)[None, :]
    seq = np.where(np.arange(C0) < NS, np.arange(C0) // LSEQ, NSEQ)
    same = seq[:, None] == seq[None, :]
    up = (j <= i)
    main = np.zeros((P, 2 * P + 2 * C0 + 2 * NH), np.float32)
    main[:, 0:P] = j == i
    main[:, P:2 * P] = up
    main[:C0, 2 * P:2 * P + C0] = same & up[:C0, :C0]
    main[:C0, 2 * P + C0:2 * P + 2 * C0] = same
    main[:16, 2 * P + 2 * C0:] = np.tile(np.eye(8), (2, 1))
    g = [((i == j + 1) & (j % 2 == 0)).astype(np.float32)]
    for c, levels in ((P, LEVELS), (C0, SMALL_LEVELS)):
        for k in range(1, levels):
            b = 2 ** k
            first = np.arange(c // 2) // b
            m = np.zeros((P, c // 2), np.float32)
            r = np.arange(c)
            m[:c] = (r[:, None] // (2 * b) == first[None, :]) & (r[:, None] % (2 * b) >= b)
            g.append(m)
    own = np.zeros((P, NSEQ + 1), np.float32)
    own[np.arange(C0), seq] = 1
    g.append(own)
    cols = np.zeros((NSEQ, C0), np.float32)
    for b in range(NSEQ):
        cols[b, b * LSEQ:(b + 1) * LSEQ] = 1
    g.append(np.tile(cols.reshape(1, -1), (P, 1)))
    return main, np.concatenate(g, axis=1).astype(np.float32)


def build(nc, x_prompt, x_sample, state_conv_a, state_conv_qkv, state_ssm, meta_tokens, norm_mix, w_in,
          conv_a_w, conv_qkv_w, a_log, dt_bias, gdn_norm, w_out, norm_ffn, w_up, w_down, norm_final,
          c_main, c_gdn, y_prompt, y_sample, new_a_prompt, new_qkv_prompt, new_ssm_prompt,
          new_a_sample, new_qkv_sample, new_ssm_sample):
    ctx = ExitStack()
    with ctx:
        SLOT = TOK * 4
        R1 = 16512
        RK = R1 + 16 * SLOT
        RYA = RK + 8 * SLOT
        RQ = RK + 16 * SLOT
        RG = RK + 20 * SLOT
        RING = RK + 24 * SLOT
        RZ = RING + 6 * 4096
        ZB = 4448
        RS = RZ + 2 * ZB
        at = {"small": RS}

        def place(name, shape, dt, offset):
            return nc.alloc_sbuf_tensor_at(name, shape, dt, offset=offset)

        def small(name, shape):
            size = 4
            for s in shape[1:]:
                size *= s
            t = place(name, shape, F32, at["small"])
            at["small"] += (size + 31) // 32 * 32
            assert at["small"] <= 229368, name
            return t

        def sem(name):
            return ctx.enter_context(nc.semaphore(name))

        ps = [ctx.enter_context(nc.psum_tensor(f"bank{i}", [P, 512], F32)) for i in range(8)]

        xh = place("xn_high", [P, KT, TOK], F32R, R1)
        xl = place("xn_low", [P, KT, TOK], F32R, R1 + KT * SLOT)
        kf = place("k_feat", [P, NH, TOK], F32, RK)
        vf = place("v_feat", [P, NH, TOK], F32, RK + 4 * SLOT)
        qf = place("q_feat", [P, NH, TOK], F32, RQ)
        gate = place("gate_feat", [P, NH, TOK], F32, RG)
        ya_h = place("ya_high", [P, NH, TOK], F32R, RYA)
        ya_l = place("ya_low", [P, NH, TOK], F32R, RYA + 4 * SLOT)
        yb_h = place("yb_high", [P, NH, TOK], F32R, RK + 4 * SLOT)
        yb_l = place("yb_low", [P, NH, TOK], F32R, RK)
        hT = place("hT", [P, KT, TOK], F32, RQ)
        hg_h = place("hg_high", [P, KT, TOK], F32R, R1)
        hg_l = place("hg_low", [P, KT, TOK], F32R, R1 + KT * SLOT)
        u_h = place("u_high", [P, KT, TOK], F32R, RK)
        u_l = place("u_low", [P, KT, TOK], F32R, RK + KT * SLOT)
        w_raw = [place(f"w_raw{i}", [P, KT, P], F32, RING + 4096 * i) for i in range(2)]
        w_h = [place(f"w_high{i}", [P, KT, P], F32R, RING + 4096 * (2 + i)) for i in range(2)]
        w_l = [place(f"w_low{i}", [P, KT, P], F32R, RING + 4096 * (4 + i)) for i in range(2)]
        z = [place(f"conv_row{i}", [P, ZB // 4], F32, RZ + ZB * i) for i in range(2)]

        x_big = place("x_tok", [P, NT - 1, D], F32, RYA)
        x_small = place("x_tok0", [P, D], F32, RZ)
        square_out = place("square_out", [P, D], F32, RK)
        rows_q = place("rows_q", [28, QKVW], F32, RG)
        rows_a = place("rows_a", [19, CONV], F32, RG + 6144)
        rows_n = place("rows_n", [16, P], F32, RG + 8192)
        ab_raw = place("ab_raw", [P, KT, 8], F32, RG + 3 * SLOT)
        ab_w = place("ab_w", [P, KT, 16], F32R, RG + 3 * SLOT + 256)
        abT = place("abT", [16, TOK], F32, RZ + ZB)

        cm = small("c_main", [P, 2 * P + 2 * C0 + 2 * NH])
        eye, upper = cm[:, 0:P], cm[:, P:2 * P]
        upper_s, same_s = cm[0:C0, 2 * P:2 * P + C0], cm[0:C0, 2 * P + C0:2 * P + 2 * C0]
        fold_ab = cm[0:16, 2 * P + 2 * C0:]
        one = small("one", [P, 1])
        mhalf = small("minus_half", [P, 1])
        tq = small("tq", [P, QKVW // P, 28])
        ta = small("ta", [P, CONV // P, 19])
        tn = small("tn", [P, 16])
        gn = small("gdn_norm_col", [P, 1])
        al = small("a_log_b", [P, NH])
        dtb = small("dt_bias_b", [P, NH])
        last_in = [small(f"last_in{i}", [P, 27]) for i in range(2)]
        last_out = [small(f"last_out{i}", [27, P]) for i in range(2)]
        ssx = small("ssx", [P, NT])
        rx = small("rx", [P, NT])
        ab = small("ab", [P, NT, 2 * NH])
        sc = {n: small(n, [P, NT, NH]) for n in
              ("g", "beta", "gneg", "eg", "egl", "eglb", "nk", "rk", "c", "p", "kd_s", "rq_s", "sso", "fo", "tmp")}
        g_seq = small("g_seq", [P, NSEQ, NH])
        eg_seq = small("eg_seq", [P, NSEQ, NH])

        HB = NH * P * 4
        SET = ("Y", "wn", "vn", "kd", "qk")
        gd = [{n: place(f"{n}_{s}", [P, NH * P], F32, R1 + (5 * s + m) * HB) for m, n in enumerate(SET)} for s in range(4)]
        TB = R1 + 20 * HB
        tmpb = [{n: place(f"{n}_{s}", [P, NH * P], F32, TB + (3 * s + m) * HB) for m, n in enumerate(("kg", "At", "X"))}
                for s in range(2)]
        pb = [[place(f"pairs_{s}{i}", [P, NH * P], F32, TB + (6 + 2 * s + i) * HB) for i in range(2)] for s in range(2)]
        S = place("S", [P, NH * P], F32, TB + 10 * HB)
        cg = place("c_gdn", [P, c_gdn.shape[1]], F32, TB + 11 * HB)
        assert TB + 11 * HB + 4 * c_gdn.shape[1] <= RK
        m0 = cg[:, 0:P]
        off = P
        lev_big = [None]
        for k in range(1, LEVELS):
            lev_big.append(cg[:, off:off + P // 2])
            off += P // 2
        lev_small = [None]
        for k in range(1, SMALL_LEVELS):
            lev_small.append(cg[:, off:off + C0 // 2])
            off += C0 // 2
        own = cg[:, off:off + NSEQ + 1]
        off += NSEQ + 1
        own_cols = cg[:, off:off + NSEQ * C0]
        SSs = place("S_sample", [P, NH, NSEQ, P], F32, R1 + 5 * HB)
        vm = place("v_masked", [C0, NSEQ + 1, P], F32, R1 + 13 * HB)
        wm = place("w_masked", [P, NSEQ, C0], F32, R1 + 16 * HB)
        qm = place("q_masked", [P, NSEQ, C0], F32, R1 + 17 * HB)
        assert NSEQ * C0 * 4 <= HB and (NSEQ + 1) * P * 4 <= 3 * HB
        ob = place("o_tok", [P, NH * P], F32, RZ)
        t1 = place("qs_scaled", [P, NH * P], F32, RZ + HB)
        vnew = place("v_new", [P, NH * P], F32, RZ + 2 * HB)
        ybt = place("yb_full", [P, NH, P], F32, RZ + 3 * HB)

        xs = place("x_slice", [P, NT, P], F32, RZ)
        hsq = place("h_squares", [P, TOK], F32, RZ + NT * P * 4)
        ut = [place(f"u_work{i}", [P, 3 * P], F32, RZ + 3 * P * 4 * i) for i in range(2)]
        nfin = place("norm_final_b", [P, D], F32, R1)
        yt = [place(f"y_tok{i}", [P, D], F32, R1 + 4096 * (1 + i)) for i in range(3)]

        s_row = sem("s_row"); s_xin = [sem(f"s_xin{i}") for i in range(3)]; s_const = sem("s_const")
        x_sq = sem("x_sq"); x_pow = sem("x_pow"); x_ms = sem("x_ms"); x_scaled = sem("x_scaled")
        x_turned = sem("x_turned"); x_high = sem("x_high"); x_low = sem("x_low")
        set_ones = sem("set_ones"); rows_turned = sem("rows_turned"); rows_kept = sem("rows_kept")
        ab_hi = sem("ab_hi"); ab_lo = sem("ab_lo"); ab_made = sem("ab_made"); ab_kept = sem("ab_kept")
        ab_turned = sem("ab_turned"); ab_tok = sem("ab_tok"); ab_act = sem("ab_act"); g_ready = sem("g_ready")
        g_summed = sem("g_summed"); g_kept = sem("g_kept"); g_exp = sem("g_exp")
        w_load = [sem("w_load0"), sem("w_load1")]
        w_high = sem("w_high"); w_low = sem("w_low"); acc_done = sem("acc_done")
        acc_read_act = sem("acc_read_act"); acc_read_dve = sem("acc_read_dve")
        z_hist = sem("z_hist"); conv_done = sem("conv_done"); silu_done = sem("silu_done")
        last_cols = sem("last_cols"); last_turned = sem("last_turned"); last_kept = sem("last_kept")
        last_sent = [sem("last_sent0"), sem("last_sent1")]
        ya_high_s = sem("ya_high_s")
        ya_low_s = sem("ya_low_s")
        sq_done = sem("sq_done"); ss_done = sem("ss_done"); norms_done = sem("norms_done"); norms_mid = sem("norms_mid")
        s_gdn = sem("s_gdn"); s_states = sem("s_states")
        kv_turned = sem("kv_turned"); kv_kept = sem("kv_kept"); g_rows = sem("g_rows"); g_diff = sem("g_diff")
        d_exp = sem("d_exp"); d_mask = sem("d_mask"); kk_made = sem("kk_made"); kk_kept = sem("kk_kept")
        y_first = sem("y_first"); x_first_t = sem("x_first_t"); x_first = sem("x_first")
        pair_zero = [sem("pair_zero0"), sem("pair_zero1")]
        p_made = [sem("p_made0"), sem("p_made1")]; p_kept = [sem("p_kept0"), sem("p_kept1")]
        xy_made = [sem("xy_made0"), sem("xy_made1")]; xy_kept = [sem("xy_kept0"), sem("xy_kept1")]
        w_made = sem("w_made"); w_kept = sem("w_kept")
        v_made = sem("v_made"); v_kept = sem("v_kept"); qs_kept = sem("qs_kept")
        os_made = sem("os_made"); s_kept = sem("s_kept"); o_kept = sem("o_kept"); o_sq = sem("o_sq"); o_ms = sem("o_ms")
        o_pow = sem("o_pow"); o_normed = sem("o_normed"); o_turned = sem("o_turned"); yb_full_s = sem("yb_full_s")
        yb_high_s = sem("yb_high_s"); yb_low_s = sem("yb_low_s")
        wm_made = sem("wm_made"); vm_made = sem("vm_made"); ss_made = sem("ss_made"); ss_kept = sem("ss_kept")
        x_slice = sem("x_slice"); x_slice_t = sem("x_slice_t"); x_slice_kept = sem("x_slice_kept")
        hg_high_s = sem("hg_high_s"); hg_low_s = sem("hg_low_s"); h_sq = sem("h_sq")
        h_sum = sem("h_sum"); rstd_b = sem("rstd_b"); rstd_mid = sem("rstd_mid")
        u_full = sem("u_full"); u_high_s = sem("u_high_s"); u_low_s = sem("u_low_s")
        fin_const = sem("fin_const"); fin_turned = sem("fin_turned"); fin_sq = sem("fin_sq"); fin_ms = sem("fin_ms")
        fin_pow = sem("fin_pow"); fin_y = sem("fin_y"); fin_sent = [sem(f"fin_sent{i}") for i in range(3)]
        out_sent = sem("out_sent"); dve_step = sem("dve_step"); pool_step = sem("pool_step")

        act_reads = [k in ("k", "q", "v", "gate", "C") for k, _, _ in IN_TILES]

        def acc_free(pe, n, g):
            if n < N_IN and act_reads[n]:
                pe.wait_ge(acc_read_act, 3 * sum(act_reads[:n]) + g + 1)
            else:
                pe.wait_ge(acc_read_dve, dve_reads_to(n) + g + 1)

        def dve_reads_to(n):
            return 3 * (sum(not a for a in act_reads[:n]) + max(0, n - N_IN))

        def has_last(n):
            return IN_TILES[n][0] in ("k", "q", "v", "H")

        N_LAST = sum(has_last(n) for n in range(N_IN))

        def last_index(n):
            return sum(has_last(m) for m in range(n))

        def x_tile(t):
            return x_small[0:C0, :] if t == 0 else x_big[:, t - 1, :]

        def x_arrived(eng, t):
            if t == 0:
                eng.wait_ge(s_xin[0], 32)
            elif t <= 2:
                eng.wait_ge(s_xin[1], 16)
            else:
                eng.wait_ge(s_xin[2], 16)

        def rows(t):
            return C0 if t == 0 else P

        def heads(tile, c):
            return tile[0:c, 0:NH * c]

        def first(ap, b):
            return ap.rearrange("p (n two b) -> p n two b", two=2, b=b)[:, :, 0, :]

        def second(ap, b):
            return ap.rearrange("p (n two b) -> p n two b", two=2, b=b)[:, :, 1, :]

        def per_head(ap, c, w):
            return ap.unsqueeze(2).to_broadcast([c, NH, w])

        def over_heads(ap, c, w):
            return ap.unsqueeze(1).to_broadcast([c, NH, w])

        def parity(t):
            return 0 if t == 0 else (t - 1) % 2

        def cset(t):
            return 0 if t == 0 else (t - 1) % 4

        def level_at(t, k):
            if t == 0:
                return k
            return (SMALL_LEVELS - 1 if parity(t) == 0 else 0) + (LEVELS - 1) * ((t - 1) // 2) + k

        def tiles_before(t):
            return t

        pairs = [(1 + 2 * i, 2 + 2 * i) for i in range((NT - 1) // 2)]
        w_up_v = w_up.rearrange("l (k p) n -> l p k n", p=P)[0]
        w_down_v = w_down.rearrange("l (k p) n -> l p k n", p=P)[0]
        w_in_v = w_in.rearrange("l (k p) n -> l p k n", p=P)[0]
        w_out_v = w_out.rearrange("l (k p) n -> l p k n", p=P)[0]
        xp_v = x_prompt.rearrange("b (t p) n -> (b p) t n", p=P)
        xs_v = x_sample.rearrange("b s n -> (b s) n")
        ssm_v = state_ssm.rearrange("l b h d e -> l d h b e")[0]
        ssm_out_v = new_ssm_sample.rearrange("l b h d e -> l d h b e")[0]

        block = ctx.enter_context(nc.Block())

        @block.sync
        def _(sp):
            sp.dma_start(x_small[0:NS, :], xs_v).then_inc(s_xin[0], 16)
            sp.dma_start(x_small[NS:C0, :], meta_tokens).then_inc(s_xin[0], 16)
            sp.dma_start(x_big[:, 0:2, :], xp_v[:, 0:2, :]).then_inc(s_xin[1], 16)
            sp.dma_start(x_big[:, 2:8, :], xp_v[:, 2:8, :]).then_inc(s_xin[2], 16)

            def load(n):
                if n >= 2:
                    sp.wait_ge(w_low, n - 1)
                if n < N_IN:
                    c = IN_TILES[n][2]
                    src = w_in_v[:, :, c:c + P]
                elif n < N_MIX:
                    src = w_out_v[:, :, P * (n - N_IN):P * (n - N_IN + 1)]
                sp.dma_start(w_raw[n % 2][:, :, :], src).then_inc(w_load[n % 2], 16)

            def send_last(n):
                kind, i, _ = IN_TILES[n]
                m = last_index(n)
                sp.wait_ge(last_kept, m + 1)
                if kind == "H":
                    sp.dma_start(new_a_sample.rearrange("l b r c -> (l b r) c")[:, P * i:P * i + P],
                                 last_out[m % 2][0:16, :]).then_inc(last_sent[m % 2], 16)
                    sp.dma_start(new_a_prompt.rearrange("l b r c -> (l b r) c")[:, P * i:P * i + P],
                                 last_out[m % 2][16:18, :]).then_inc(last_sent[m % 2], 16)
                else:
                    c = {"q": 0, "k": NH * P, "v": 2 * NH * P}[kind] + P * i
                    sp.dma_start(new_qkv_sample.rearrange("l b r c -> (l b r) c")[:, c:c + P],
                                 last_out[m % 2][0:24, :]).then_inc(last_sent[m % 2], 16)
                    sp.dma_start(new_qkv_prompt.rearrange("l b r c -> (l b r) c")[:, c:c + P],
                                 last_out[m % 2][24:27, :]).then_inc(last_sent[m % 2], 16)

            def slice_x(f):
                if f == 0:
                    sp.wait_ge(yb_low_s, NT)
                else:
                    sp.wait_ge(x_slice_t, 3 * f)
                cols = slice(P * f, P * f + P)
                sp.dma_start(xs[0:NS, 0, :], xs_v[:, cols]).then_inc(x_slice, 16)
                sp.dma_start(xs[NS:C0, 0, :], meta_tokens[:, cols]).then_inc(x_slice, 16)
                sp.dma_start(xs[:, 1:NT, :], xp_v[:, :, cols]).then_inc(x_slice, 16)

            for n in range(N_MIX):
                if n == N_IN + 3:
                    sp.wait_ge(ss_kept, 2 * NH)
                    for h in range(NH):
                        sp.dma_start(ssm_out_v[:, h, :, :], SSs[:, h, :, :]).then_inc(out_sent, 16)
                    sp.wait_ge(s_kept, NT)
                    sp.dma_start(new_ssm_prompt.rearrange("l b h d e -> d (l b h) e"),
                                 S[:, :].rearrange("p (h e) -> p h e", h=NH)).then_inc(out_sent, 16)
                if n >= N_IN + 3:
                    slice_x(n - N_IN - 3)
                load(n)
                if n >= 4 and n - 4 < N_IN and has_last(n - 4):
                    send_last(n - 4)
                if n == N_IN:
                    sp.wait_ge(acc_done, 3 * N_IN)
                    sp.dma_start(cg[:, :], c_gdn).then_inc(s_gdn, 16)
                    for h in range(NH):
                        sp.dma_start(SSs[:, h, :, :], ssm_v[:, h, :, :]).then_inc(s_states, 16)
            for f in range(N_MIX - N_IN - 3, N_OUT):
                slice_x(f)

            with sp.Fori(0, FG) as g:
                for i in range(2 * KT):
                    n = N_MIX + i
                    sp.wait_ge(w_low, g * (2 * KT) + (n - 1))
                    if i < KT:
                        src = w_up_v[:, :, bass.ds(g * D + P * i, P)]
                    else:
                        src = w_down_v[:, bass.ds(g * KT, KT), P * (i - KT):P * (i - KT) + P]
                    sp.dma_start(w_raw[n % 2][:, :, :], src).then_inc(w_load[n % 2], 16)
            sp.wait_ge(acc_done, 3 * (N_MIX + 2 * KT * FG - KT))
            sp.dma_start(nfin[:, :], norm_final.rearrange("(a n) -> a n", a=1).to_broadcast([P, D])).then_inc(fin_const, 16)
            for t in range(NT):
                sp.wait_ge(fin_y, t + 1)
                if t == 0:
                    sp.dma_start(y_sample.rearrange("b s n -> (b s) n"), yt[0][0:NS, :]).then_inc(fin_sent[0], 16)
                else:
                    sp.dma_start(y_prompt[0, P * (t - 1):P * t, :], yt[t % 3][:, :]).then_inc(fin_sent[t % 3], 16)
            for i in range(3):
                sp.wait_ge(fin_sent[i], 16 * len(range(i, NT, 3)))
            sp.wait_ge(out_sent, 16 * (NH + 1))
            for i in range(2):
                sp.wait_ge(last_sent[i], 32 * len(range(i, N_LAST, 2)))

        @block.gpsimd
        def _(pool):
            pool.memset(one[:, :], 1.0).then_inc(set_ones, 1)
            pool.memset(mhalf[:, :], -0.5).then_inc(set_ones, 1)
            pool.memset(ab[:, :, :], 0.0).then_inc(set_ones, 1)
            pool.wait_ge(set_ones, 3)
            for t in range(NT):
                pool.wait_ge(x_ms, t + 1)
                pool.tensor_tensor(rx[0:rows(t), t:t + 1], ssx[0:rows(t), t:t + 1], mhalf[0:rows(t), :],
                                   ALU.pow).then_inc(x_pow, 1)
            pool.wait_ge(ab_hi, 1)
            pool.tensor_tensor(ab_w[:, :, 8:16], ab_raw[:, :, :], ab_w[:, :, 0:8].bitcast(F32),
                               ALU.subtract).then_inc(ab_lo, 1)

            def split_low(n, g=0):
                pool.wait_ge(w_high, g * (2 * KT) + (n + 1))
                if n >= 2:
                    pool.wait_ge(acc_done, g * (6 * KT) + 3 * (n - 1))
                pool.tensor_tensor(w_l[n % 2][:, :, :], w_raw[n % 2][:, :, :], w_h[n % 2][:, :, :].bitcast(F32),
                                   ALU.subtract).then_inc(w_low, 1)

            split_low(0)
            for n in range(N_IN):
                kind, i, _ = IN_TILES[n]
                if kind in ("k", "q", "v"):
                    f = {"q": 0, "k": NH, "v": 2 * NH}[kind] + i
                    if n == 0:
                        pool.wait_ge(x_turned, 24)
                        pool.wait_ge(rows_kept, 3)
                    elif n == 1:
                        pool.wait_ge(ab_turned, 1)
                    else:
                        pool.wait_ge(conv_done, n - 1)
                    zb = z[n % 2]
                    pool.tensor_copy(zb[:, 0:56].rearrange("p (b r) -> p b r", r=7)[:, :, 0:3],
                                     tq[:, f, 0:24].rearrange("p (b r) -> p b r", r=3))
                    pool.memset(zb[:, 56:59], 0.0).then_inc(z_hist, 1)
                if kind == "H":
                    if i == 0:
                        pool.wait_ge(ss_done, 2 * NH)
                    else:
                        pool.wait_ge(ya_low_s, i)
                    pool.tensor_copy(z[1][:, 0:48].rearrange("p (b r) -> p b r", r=6)[:, :, 0:2],
                                     ta[:, i, 0:16].rearrange("p (b r) -> p b r", r=2))
                    pool.memset(z[1][:, 48:50], 0.0).then_inc(z_hist, 1)
                split_low(n + 1)
                if has_last(n):
                    m = last_index(n)
                    if m >= 2:
                        pool.wait_ge(last_turned, m - 1)
                    if kind == "H":
                        pool.wait_ge(acc_read_dve, dve_reads_to(n) + 3)
                        pool.tensor_copy(last_in[m % 2][:, 0:16].rearrange("p (b r) -> p b r", r=2),
                                         z[1][:, 0:48].rearrange("p (b r) -> p b r", r=6)[:, :, 4:6])
                        pool.tensor_copy(last_in[m % 2][:, 16:18], z[1][:, 50 + PRM - 2:50 + PRM]).then_inc(last_cols, 1)
                    else:
                        pool.wait_ge(acc_read_act, 3 * n + 3)
                        pool.tensor_copy(last_in[m % 2][:, 0:24].rearrange("p (b r) -> p b r", r=3),
                                         z[n % 2][:, 0:56].rearrange("p (b r) -> p b r", r=7)[:, :, 4:7])
                        pool.tensor_copy(last_in[m % 2][:, 24:27], z[n % 2][:, 59 + PRM - 3:59 + PRM]).then_inc(last_cols, 1)

            def decay_mask(t):
                c, st = rows(t), gd[cset(t)]
                pool.wait_ge(d_exp, t + 1)
                m = upper_s if t == 0 else upper
                d = heads(st["wn"], c).rearrange("p (h i) -> p h i", h=NH)
                pool.tensor_tensor(d, d, over_heads(m[0:c, 0:c], c, c), ALU.mult).then_inc(d_mask, 1)

            def first_level(t):
                c, st, tb = rows(t), gd[cset(t)], tmpb[parity(t)]
                pool.wait_ge(kk_kept, t + 1)
                if t >= 5:
                    pool.wait_ge(v_made, t - 4)
                y = heads(st["Y"], c).rearrange("p (h i) -> p h i", h=NH)
                pool.tensor_tensor(y, heads(tb["At"], c).rearrange("p (h i) -> p h i", h=NH),
                                   over_heads(m0[0:c, 0:c], c, c), ALU.mult).then_inc(pool_step, 1)
                pool.wait_ge(pool_step, pst(t))
                pool.tensor_tensor(y, over_heads(eye[0:c, 0:c], c, c), y, ALU.subtract).then_inc(y_first, 1)

            def pst(t):
                return t + 1

            def zero_pairs(t, k):
                c, par = rows(t), parity(t)
                at_level = level_at(t, k)
                if at_level >= 3:
                    pool.wait_ge(xy_made[par], at_level - 2)
                pool.memset(heads(pb[par][at_level % 2], c), 0.0).then_inc(pair_zero[par], 1)

            def power(t):
                c = rows(t)
                pool.wait_ge(o_ms, t + 1)
                pool.tensor_tensor(sc["fo"][0:c, t, :], sc["tmp"][0:c, t, :], mhalf[0:c, :].to_broadcast([c, NH]),
                                   ALU.pow).then_inc(o_pow, 1)

            pool.wait_ge(acc_done, 3 * N_IN)
            pool.wait_ge(s_gdn, 16)
            decay_mask(0)
            zero_pairs(0, 1)
            zero_pairs(0, 2)
            first_level(0)
            zero_pairs(0, 3)
            for h in range(NH):
                if h:
                    pool.wait_ge(ss_made, h)
                oc = own_cols.rearrange("p (b i) -> p b i", b=NSEQ)
                pool.tensor_tensor(qm[:, :, :], qf[:, h, 0:C0].unsqueeze(1).to_broadcast([P, NSEQ, C0]), oc,
                                   ALU.mult).then_inc(wm_made, 1)
                pool.wait_ge(w_kept, 1)
                pool.tensor_tensor(wm[:, :, :], gd[0]["wn"][:, C0 * h:C0 * h + C0].unsqueeze(1).to_broadcast([P, NSEQ, C0]),
                                   oc, ALU.mult).then_inc(wm_made, 1)
            power(0)
            pool.wait_ge(os_made, 1)
            for n, (a, b) in enumerate(pairs):
                for t in (a, b):
                    decay_mask(t)
                for t in (a, b):
                    zero_pairs(t, 1)
                    zero_pairs(t, 2)
                    first_level(t)
                for k in range(1, LEVELS):
                    if n and k == 3:
                        power(pairs[n - 1][0])
                    if n and k == 5:
                        power(pairs[n - 1][1])
                    for t in (a, b):
                        if k + 2 < LEVELS:
                            zero_pairs(t, k + 2)
            for t in pairs[-1]:
                power(t)

            for n in range(N_IN + 1, N_MIX + 1):
                split_low(n)
            with pool.Fori(0, FG - 1) as g:
                for i in range(2 * KT):
                    split_low(N_MIX + 1 + i, g)
            for i in range(2 * KT - 1):
                split_low(N_MIX + 1 + i, FG - 1)
            for t in range(NT):
                c = rows(t)
                pool.wait_ge(fin_ms, t + 1)
                pool.tensor_tensor(rx[0:c, t:t + 1], ssx[0:c, t:t + 1], mhalf[0:c, :], ALU.pow).then_inc(fin_pow, 1)

        @block.scalar
        def _(act):
            act.dma_start(cm[:, :], c_main).then_inc(s_const, 16)
            act.dma_start(rows_n[0:8, :], norm_mix.rearrange("l (k p) -> (l k) p", p=P)).then_inc(s_row, 16)
            act.dma_start(rows_n[8:16, :], norm_ffn.rearrange("l (k p) -> (l k) p", p=P)).then_inc(s_row, 16)
            act.dma_start(ab_raw[:, :, :], w_in_v[:, :, O_A:O_A + 8]).then_inc(s_row, 16)
            act.dma_start(rows_q[0:24, :], state_conv_qkv.rearrange("l b r c -> (l b r) c")).then_inc(s_row, 16)
            act.dma_start(rows_q[24:28, :], conv_qkv_w[0]).then_inc(s_row, 16)
            act.dma_start(rows_a[0:16, :], state_conv_a.rearrange("l b r c -> (l b r) c")).then_inc(s_row, 16)
            act.dma_start(rows_a[16:19, :], conv_a_w[0]).then_inc(s_row, 16)
            act.dma_start(gn[:, :], gdn_norm.rearrange("l (p a) -> (l p) a", a=1)).then_inc(s_row, 16)
            act.dma_start(al[:, :], a_log.to_broadcast([P, NH])).then_inc(s_row, 16)
            act.dma_start(dtb[:, :], dt_bias.to_broadcast([P, NH])).then_inc(s_row, 16)
            for t in range(NT):
                x_arrived(act, t)
                if t:
                    act.wait_ge(x_sq, t)
                act.activation(square_out[0:rows(t), :], x_tile(t), ACT.Square,
                               accum_out=ssx[0:rows(t), t:t + 1]).then_inc(x_sq, 1)
            act.wait_ge(s_row, 160)
            act.activation(ab_w[:, :, 0:8], ab_raw[:, :, :], ACT.Copy).then_inc(ab_hi, 1)

            def split_high(n, g=0):
                act.wait_ge(w_load[n % 2], g * (16 * KT) + 16 * (n // 2 + 1))
                if n >= 2:
                    act.wait_ge(acc_done, g * (6 * KT) + 3 * (n - 1))
                act.activation(w_h[n % 2][:, :, :], w_raw[n % 2][:, :, :], ACT.Copy).then_inc(w_high, 1)

            split_high(0)
            act.wait_ge(rows_kept, 1)
            for g, (c0, w) in enumerate(GROUPS):
                for k in range(KT):
                    act.wait_ge(x_turned, KT * g + k + 1)
                    act.activation(xh[:, k, c0:c0 + w], ps[k][:, 0:w], ACT.Copy, scale=tn[:, k:k + 1]).then_inc(x_high, 1)
            for g, (c0, w) in enumerate(GROUPS):
                act.wait_ge(ab_made, g + 1)
                act.activation(abT[:, c0:c0 + w], ps[3 + g][0:16, 0:w], ACT.Copy).then_inc(ab_kept, 1)
            act.wait_ge(ab_tok, 2)
            act.activation(sc["tmp"][:, :, :], sc["eg"][:, :, :], ACT.Exp, scale=-1.0).then_inc(ab_act, 1)
            act.activation(sc["beta"][:, :, :], ab[:, :, NH:2 * NH], ACT.Exp, scale=-1.0).then_inc(ab_act, 1)
            act.activation(al[:, :], al[:, :], ACT.Exp).then_inc(ab_act, 1)
            act.wait_ge(ab_act, 3)
            act.activation(sc["tmp"][:, :, :], sc["tmp"][:, :, :], ACT.Ln, bias=one[:, 0:1]).then_inc(ab_act, 1)

            def silu(n):
                kind, i, _ = IN_TILES[n]
                dst = {"k": kf, "q": qf, "v": vf}[kind][:, i, :]
                act.wait_ge(conv_done, n + 1)
                act.activation(dst, dst, ACT.Silu).then_inc(silu_done, 1)

            def square_kq(j):
                src = (kf if j < NH else qf)[:, j % NH, :]
                act.wait_ge(silu_done, j + 1)
                if j < 2:
                    act.wait_ge(conv_done, 12)
                    act.wait_ge(last_cols, 12)
                else:
                    act.wait_ge(ss_done, j - 1)
                act.activation(z[j % 2][:, 0:TOK], src, ACT.Square).then_inc(sq_done, 1)

            for n in range(N_IN):
                kind, i, _ = IN_TILES[n]
                split_high(n + 1)
                if kind in ("k", "q", "v"):
                    zb = z[n % 2]
                    if n == 0:
                        act.wait_ge(x_turned, 24)
                    elif n == 1:
                        act.wait_ge(ab_turned, 1)
                    else:
                        act.wait_ge(conv_done, n - 1)
                        act.wait_ge(last_cols, n - 1)
                    for g, (c0, w) in enumerate(GROUPS):
                        act.wait_ge(acc_done, 3 * n + g + 1)
                        bank = ps[(n % 2) * 3 + g]
                        if g == 0:
                            act.activation(zb[:, 0:56].rearrange("p (b r) -> p b r", r=7)[:, :, 3:7],
                                           bank[:, 0:NS].rearrange("p (b r) -> p b r", r=LSEQ), ACT.Copy)
                            act.activation(zb[:, 59:59 + w - NS], bank[:, NS:w], ACT.Copy).then_inc(acc_read_act, 1)
                        else:
                            act.activation(zb[:, 59 + c0 - NS:59 + c0 - NS + w], bank[:, 0:w],
                                           ACT.Copy).then_inc(acc_read_act, 1)
                    if n:
                        silu(n - 1)
                if kind == "gate":
                    for g, (c0, w) in enumerate(GROUPS):
                        act.wait_ge(acc_done, 3 * n + g + 1)
                        if i == 0 and g == 0:
                            act.wait_ge(rows_kept, 3)
                            act.wait_ge(ab_made, 3)
                        act.activation(gate[:, i, c0:c0 + w], ps[(n % 2) * 3 + g][:, 0:w], ACT.Silu).then_inc(acc_read_act, 1)
                    if i == 0:
                        silu(n - 1)
                    square_kq(2 * i)
                    square_kq(2 * i + 1)
                if kind == "C":
                    if i == 0:
                        act.wait_ge(ss_done, 2 * NH)
                    else:
                        act.wait_ge(acc_read_dve, dve_reads_to(n))
                    for g, (c0, w) in enumerate(GROUPS):
                        act.wait_ge(acc_done, 3 * n + g + 1)
                        act.activation(z[0][:, c0:c0 + w], ps[(n % 2) * 3 + g][:, 0:w], ACT.Copy).then_inc(acc_read_act, 1)
                if kind == "B":
                    for g, (c0, w) in enumerate(GROUPS):
                        act.wait_ge(acc_read_dve, dve_reads_to(n) + g + 1)
                        act.activation(ya_h[:, i, c0:c0 + w], z[1][:, c0:c0 + w], ACT.Copy).then_inc(ya_high_s, 1)
                if n == 1:
                    act.wait_ge(g_kept, 4)
                    act.activation(sc["eg"][:, :, :], sc["gneg"][:, :, :], ACT.Exp, scale=-1.0).then_inc(g_exp, 1)
                    act.activation(sc["egl"][:, :, :], sc["egl"][:, :, :], ACT.Exp).then_inc(g_exp, 1)
                    act.activation(sc["eglb"][:, :, :], sc["eglb"][:, :, :], ACT.Exp).then_inc(g_exp, 1)
                    act.activation(eg_seq[:, :, :], eg_seq[:, :, :], ACT.Exp).then_inc(g_exp, 1)
                if n == N_IN - 1:
                    act.wait_ge(norms_mid, 1)
                    act.activation(sc["nk"][:, :, :], sc["nk"][:, :, :], ACT.Sqrt).then_inc(norms_mid, 1)
                    act.activation(sc["rq_s"][:, :, :], sc["rq_s"][:, :, :], ACT.Sqrt).then_inc(norms_mid, 1)

            def decay_exp(t):
                c, st = rows(t), gd[cset(t)]
                act.wait_ge(g_diff, t + 1)
                act.activation(heads(st["wn"], c), heads(st["wn"], c), ACT.Exp).then_inc(d_exp, 1)

            def keep_x(t):
                c, tb = rows(t), tmpb[parity(t)]
                act.wait_ge(x_first_t, t + 1)
                act.activation(heads(tb["X"], c), ps[2 * parity(t)][0:c, 0:NH * c], ACT.Copy).then_inc(x_first, 1)

            def keep_w(t):
                c, st = rows(t), gd[cset(t)]
                act.wait_ge(w_made, t + 1)
                act.activation(st["wn"][:, 0:NH * c], ps[2 * parity(t)][:, 0:NH * c], ACT.Copy, scale=-1.0).then_inc(w_kept, 1)

            def o_square(t):
                c = rows(t)
                act.wait_ge(o_kept, t + 1)
                for h in range(NH):
                    ins = act.activation(t1[0:c, P * h:P * h + P], ob[0:c, P * h:P * h + P], ACT.Square,
                                         scale=sc["rq_s"][0:c, t, h:h + 1], accum_out=sc["sso"][0:c, t, h:h + 1])
                ins.then_inc(o_sq, 1)

            def yb_high(t):
                c0, c = tile_cols(t)
                act.wait_ge(yb_full_s, t + 1)
                act.activation(yb_h[:, :, c0:c0 + c], ybt[:, :, 0:c], ACT.Copy).then_inc(yb_high_s, 1)

            decay_exp(0)
            keep_x(0)
            keep_w(0)
            o_square(0)
            yb_high(0)
            for n, pr in enumerate(pairs):
                for t in pr:
                    decay_exp(t)
                for t in pr:
                    keep_x(t)
                if n:
                    for t in pairs[n - 1]:
                        o_square(t)
                        yb_high(t)
                for t in pr:
                    keep_w(t)
            for t in pairs[-1]:
                o_square(t)
                yb_high(t)

            act.wait_ge(out_sent, 16 * (NH + 1))
            for f in range(N_OUT):
                n = N_IN + f
                split_high(n + 1)
                for g, (c0, w) in enumerate(GROUPS):
                    act.wait_ge(acc_read_dve, dve_reads_to(n) + g + 1)
                    act.activation(hg_h[:, f, c0:c0 + w], hT[:, f, c0:c0 + w], ACT.Copy,
                                   scale=tn[:, 8 + f:9 + f]).then_inc(hg_high_s, 1)

            act.wait_ge(rstd_mid, 3)
            act.activation(hsq[:, :], hsq[:, :], ACT.Sqrt).then_inc(rstd_b, 1)

            def up_high(g, i):
                for m, (c0, w) in enumerate(GROUPS):
                    act.wait_ge(u_full, g * (3 * KT) + 3 * i + m + 1)
                    if i == 0 and m == 0:
                        act.wait_ge(acc_done, g * (6 * KT) + 3 * N_MIX)
                    act.activation(u_h[:, i, c0:c0 + w], ut[(3 * i + m) % 2][:, 0:w], ACT.Copy).then_inc(u_high_s, 1)

            with act.Fori(0, FG - 1) as g:
                for i in range(KT):
                    split_high(N_MIX + 1 + i, g)
                    up_high(g, i)
                for i in range(KT):
                    split_high(N_MIX + KT + 1 + i, g)
            for i in range(KT):
                split_high(N_MIX + 1 + i, FG - 1)
                up_high(FG - 1, i)
            for i in range(KT - 1):
                split_high(N_MIX + KT + 1 + i, FG - 1)
            for t in range(NT):
                c = rows(t)
                act.wait_ge(fin_turned, t + 1)
                if t == 0:
                    act.wait_ge(acc_done, 3 * (N_MIX + 2 * KT * FG))
                if t >= 3:
                    act.wait_ge(fin_sent[t % 3], 16 * (t // 3))
                for half in range(2):
                    ins = act.activation(yt[t % 3][0:c, 512 * half:512 * half + 512], ps[4 * (t % 2) + half][0:c, :],
                                         ACT.Square, accum_out=sc["sso"][0:c, t, half:half + 1])
                ins.then_inc(fin_sq, 1)

        @block.tensor
        def _(pe):
            pe.wait_ge(s_const, 16)
            pe.wait_ge(s_row, 160)
            pe.transpose(ps[0][:, 0:16], rows_n[:, :], eye[0:16, 0:16]).then_inc(rows_turned, 1)
            for f in range(QKVW // P):
                ins = pe.transpose(ps[1][:, 28 * f:28 * f + 28], rows_q[:, P * f:P * f + P], eye[0:28, 0:28])
            for f in range(CONV // P):
                ins = pe.transpose(ps[2][:, 19 * f:19 * f + 19], rows_a[:, P * f:P * f + P], eye[0:19, 0:19])
            ins.then_inc(rows_turned, 1)
            for g, (c0, w) in enumerate(GROUPS):
                for k in range(KT):
                    if g == 0 and k == 0:
                        pe.wait_ge(rows_kept, 3)
                    if g:
                        pe.wait_ge(x_low, KT * (g - 1) + k + 1)
                    for t in GTILES[g]:
                        o, c = tile_cols(t)
                        if k == 0:
                            pe.wait_ge(x_scaled, t + 1)
                        ins = pe.transpose(ps[k][:, o - c0:o - c0 + c], x_tile(t)[:, P * k:P * k + P], eye[0:c, 0:c])
                    ins.then_inc(x_turned, 1)
            pe.wait_ge(ab_lo, 1)
            for g, (c0, w) in enumerate(GROUPS):
                pe.wait_ge(x_low, KT * (g + 1))
                if g == 0:
                    pe.wait_ge(x_low, 2 * KT + 6)
                for k in range(KT):
                    pe.matmul(ps[3 + g][0:16, 0:w], ab_w[:, k, 0:16], xh[:, k, c0:c0 + w], start=(k == 0), stop=False)
                for k in range(KT):
                    ins = pe.matmul(ps[3 + g][0:16, 0:w], ab_w[:, k, 0:16], xl[:, k, c0:c0 + w], start=False,
                                    stop=(k == KT - 1))
                ins.then_inc(ab_made, 1)

            def dense(n, rhs, g0=0, order=range(KT), prepare=None):
                for g, (c0, w) in enumerate(GROUPS):
                    if g == 0:
                        pe.wait_ge(w_low, g0 * (2 * KT) + (n + 1))
                    if prepare:
                        prepare(g)
                    bank = ps[(n % 2) * 3 + g]
                    for m, k in enumerate(order):
                        hi, lo = rhs(k)
                        pe.matmul(bank[:, 0:w], w_h[n % 2][:, k, :], hi[:, c0:c0 + w], start=(m == 0), stop=False)
                        pe.matmul(bank[:, 0:w], w_h[n % 2][:, k, :], lo[:, c0:c0 + w], start=False, stop=False)
                        ins = pe.matmul(bank[:, 0:w], w_l[n % 2][:, k, :], hi[:, c0:c0 + w], start=False,
                                        stop=(m == KT - 1))
                    ins.then_inc(acc_done, 1)

            def turn_last(n):
                m = last_index(n)
                r = 18 if IN_TILES[n][0] == "H" else 27
                pe.wait_ge(last_cols, m + 1)
                if m:
                    pe.wait_ge(last_kept, m)
                pe.transpose(ps[6][0:r, 0:P], last_in[m % 2][:, 0:r], eye).then_inc(last_turned, 1)

            def sum_squares(j):
                pe.wait_ge(sq_done, j + 1)
                for t in range(NT):
                    o, c = tile_cols(t)
                    col = t * 2 * NH + j
                    ins = pe.matmul(ps[7][0:c, col:col + 1], z[j % 2][:, o:o + c], one[:, :], start=True, stop=True)
                ins.then_inc(ss_done, 1)

            for n in range(N_IN):
                def prepare(g, n=n):
                    if n >= 2:
                        acc_free(pe, n - 2, g)
                    elif n == 0:
                        pe.wait_ge(x_low, 3 * KT)
                    else:
                        pe.wait_ge(ab_kept, g + 1)
                dense(n, lambda k: (xh[:, k, :], xl[:, k, :]), prepare=prepare)
                if n == 0:
                    pe.wait_ge(ab_kept, 3)
                    for t in range(NT):
                        o, c = tile_cols(t)
                        ins = pe.matmul(ps[6][0:c, 8 * t:8 * t + 8], abT[:, o:o + c], fold_ab, start=True, stop=True)
                    ins.then_inc(ab_turned, 1)
                    pe.wait_ge(g_ready, 2)
                    big = sc["g"][:, 1:NT, :]
                    small_g = sc["g"][0:C0, 0, :]
                    pe.matmul(ps[7][:, 0:32], upper, big, start=True, stop=True)
                    pe.matmul(ps[7][0:C0, 32:36], upper_s, small_g, start=True, stop=True)
                    pe.matmul(ps[7][:, 64:96], one[:, 0:1].to_broadcast([P, P]), big, start=True, stop=True)
                    pe.matmul(ps[7][0:C0, 96:100], same_s, small_g, start=True, stop=True)
                    pe.matmul(ps[7][:, 128:160], one[0:C0, 0:1].to_broadcast([C0, P]), g_seq[0:C0, :, :],
                              start=True, stop=True).then_inc(g_summed, 1)
                if n and has_last(n - 1):
                    if n == 1:
                        pe.wait_ge(ab_tok, 1)
                    turn_last(n - 1)
                if IN_TILES[n][0] == "gate" and IN_TILES[n][1]:
                    sum_squares(2 * IN_TILES[n][1] - 2)
                    sum_squares(2 * IN_TILES[n][1] - 1)
                if n == 4 * NH:
                    sum_squares(2 * NH - 2)
                    sum_squares(2 * NH - 1)

            def turn_kv(t):
                o, c = tile_cols(t)
                b = ps[2 * parity(t)], ps[2 * parity(t) + 1]
                if t == 1:
                    pe.wait_ge(ss_kept, 2 * NH)
                if t >= 3:
                    pe.wait_ge(w_kept, t - 1)
                for i, src in enumerate((kf, vf)):
                    for h in range(NH):
                        ins = pe.transpose(b[i][0:c, P * h:P * h + P], src[:, h, o:o + c], eye)
                ins.then_inc(kv_turned, 1)

            def decay_rows(t):
                c = rows(t)
                pe.wait_ge(kv_kept, t + 1)
                u = upper_s if t == 0 else upper
                for h in range(NH):
                    ins = pe.matmul(ps[2 * parity(t)][0:c, c * h:c * h + c],
                                    sc["g"][0:c, t, h:h + 1].to_broadcast([c, c]), u, start=True, stop=True)
                ins.then_inc(g_rows, 1)

            def products(t):
                o, c = tile_cols(t)
                pe.wait_ge(g_diff, t + 1)
                for i, rhs in enumerate((kf, qf)):
                    for h in range(NH):
                        ins = pe.matmul(ps[2 * parity(t) + i][0:c, c * h:c * h + c], kf[:, h, o:o + c],
                                        rhs[:, h, o:o + c], start=True, stop=True)
                ins.then_inc(kk_made, 1)

            def turn_y(t):
                c, st = rows(t), gd[cset(t)]
                pe.wait_ge(y_first, t + 1)
                for h in range(NH):
                    ins = pe.transpose(ps[2 * parity(t)][0:c, c * h:c * h + c], st["Y"][0:c, c * h:c * h + c],
                                       eye[0:c, 0:c])
                ins.then_inc(x_first_t, 1)

            def level_p(t, k):
                c, tb, par = rows(t), tmpb[parity(t)], parity(t)
                if k == 1:
                    pe.wait_ge(x_first, t + 1)
                else:
                    pe.wait_ge(xy_kept[par], level_at(t, k) - 1)
                for h in range(NH):
                    ins = pe.matmul(ps[2 * par][0:c, c // 2 * h:c // 2 * (h + 1)], tb["At"][0:c, c * h:c * h + c],
                                    first(tb["X"][0:c, c * h:c * h + c], 2 ** k), start=True, stop=True)
                ins.then_inc(p_made[par], 1)

            def level_xy(t, k):
                c, tb, st, par = rows(t), tmpb[parity(t)], gd[cset(t)], parity(t)
                at_level, last = level_at(t, k), k == (SMALL_LEVELS if t == 0 else LEVELS) - 1
                pk = pb[par][at_level % 2]
                pe.wait_ge(p_kept[par], at_level)
                for h in range(NH):
                    hs = slice(c * h, c * h + c)
                    if not last:
                        pe.matmul(ps[2 * par + 1][0:c, c // 2 * h:c // 2 * (h + 1)], st["Y"][0:c, hs],
                                  first(pk[0:c, hs], 2 ** k), start=True, stop=True)
                    ins = pe.matmul(ps[2 * par + 1][0:c, 256 + c // 2 * h:256 + c // 2 * (h + 1)], pk[0:c, hs],
                                    second(st["Y"][0:c, hs], 2 ** k), start=True, stop=True)
                ins.then_inc(xy_made[par], 1)

            def make_w(t):
                c, st, tb = rows(t), gd[cset(t)], tmpb[parity(t)]
                pe.wait_ge(xy_kept[parity(t)], level_at(t, (SMALL_LEVELS if t == 0 else LEVELS) - 1))
                for h in range(NH):
                    ins = pe.matmul(ps[2 * parity(t)][:, c * h:c * h + c], tb["kg"][0:c, P * h:P * h + P],
                                    st["Y"][0:c, c * h:c * h + c], start=True, stop=True)
                ins.then_inc(w_made, 1)

            def use_state(t):
                o, c = tile_cols(t)
                st = gd[cset(t)]
                pe.wait_ge(w_kept, t + 1)
                pe.wait_ge(s_kept, t)
                pe.wait_ge(v_kept, t)
                pe.wait_ge(qs_kept, t)
                pe.wait_ge(yb_full_s, t - 1 + t % 2)
                for h in range(NH):
                    hs = slice(P * h, P * h + P)
                    pe.matmul(ps[4][:, hs], st["Y"][:, hs], st["vn"][:, hs], start=True, stop=False)
                    pe.matmul(ps[4][:, hs], st["wn"][:, hs], S[:, hs], start=False, stop=True)
                for h in range(NH):
                    hs = slice(P * h, P * h + P)
                    ins = pe.matmul(ps[5][:, hs], qf[:, h, o:o + c], S[:, hs], start=True, stop=True)
                ins.then_inc(v_made, 1)

            def next_state(t):
                c, st = rows(t), gd[cset(t)]
                pe.wait_ge(v_kept, t + 1)
                pe.wait_ge(o_kept, t)
                for h in range(NH):
                    hs = slice(P * h, P * h + P)
                    pe.matmul(ps[7][:, hs], st["kd"][0:c, hs], vnew[0:c, hs],
                              start=True, stop=True)
                for h in range(NH):
                    ins = pe.matmul(ps[6][0:c, P * h:P * h + P], st["qk"][0:c, c * h:c * h + c],
                                    vnew[0:c, P * h:P * h + P], start=True, stop=True)
                ins.then_inc(os_made, 1)

            def turn_o(t):
                c = rows(t)
                pe.wait_ge(o_normed, t + 1)
                pe.wait_ge(qs_kept, t + 1 + (t % 2))
                if t:
                    pe.wait_ge(yb_full_s, t)
                for h in range(NH):
                    ins = pe.transpose(ps[5][:, c * h:c * h + c], ob[0:c, P * h:P * h + P], eye[0:c, 0:c])
                ins.then_inc(o_turned, 1)

            def chain_step(k, a, b):
                if k == 1:
                    use_state(a)
                if k == 2:
                    next_state(a)
                if k == 3:
                    use_state(b)
                if k == 4:
                    turn_o(a)
                    next_state(b)
                if k == 6:
                    turn_o(b)

            pe.wait_ge(norms_done, 1)
            turn_kv(0)
            decay_rows(0)
            products(0)
            turn_y(0)
            for k in range(1, SMALL_LEVELS):
                level_p(0, k)
                level_xy(0, k)
            make_w(0)
            pe.wait_ge(s_states, 16 * NH)
            for h in range(NH):
                hs, cs = slice(P * h, P * h + P), slice(C0 * h, C0 * h + C0)
                pe.wait_ge(wm_made, 2 * h + 2)
                pe.matmul(ps[4][0:C0, hs], gd[0]["Y"][0:C0, cs], gd[0]["vn"][0:C0, hs], start=True, stop=False)
                for b in range(NSEQ):
                    pe.matmul(ps[4][0:C0, hs], wm[:, b, :], SSs[:, h, b, :], start=False, stop=(b == NSEQ - 1))
                for b in range(NSEQ):
                    ins = pe.matmul(ps[5][0:C0, hs], qm[:, b, :], SSs[:, h, b, :], start=(b == 0), stop=(b == NSEQ - 1))
                ins.then_inc(ss_made, 1)
            for h in range(NH):
                pe.wait_ge(vm_made, h + 1)
                if h:
                    pe.wait_ge(ss_kept, 2 * h)
                for half in range(2):
                    ins = pe.matmul(ps[half][:, :], gd[0]["kd"][0:C0, P * h:P * h + P], vm[:, 4 * half:4 * half + 4, :],
                                    start=True, stop=True)
                ins = pe.matmul(ps[7][:, P * h:P * h + P], gd[0]["kd"][0:C0, P * h:P * h + P], vm[:, NSEQ, :],
                                start=True, stop=True)
                ins.then_inc(ss_made, 1)
            for h in range(NH):
                ins = pe.matmul(ps[6][0:C0, P * h:P * h + P], gd[0]["qk"][0:C0, C0 * h:C0 * h + C0],
                                vnew[0:C0, P * h:P * h + P], start=True, stop=True)
            ins.then_inc(os_made, 1)
            turn_o(0)
            for n, pr in enumerate(pairs):
                for step in (turn_kv, decay_rows, products, turn_y):
                    for t in pr:
                        step(t)
                for k in range(1, LEVELS):
                    for t in pr:
                        level_p(t, k)
                    if n:
                        chain_step(k, *pairs[n - 1])
                    for t in pr:
                        level_xy(t, k)
                for t in pr:
                    make_w(t)
            for k in range(1, LEVELS):
                chain_step(k, *pairs[-1])

            for f in range(N_OUT):
                n = N_IN + f

                def prepare(g, f=f, n=n):
                    m = 3 * f + g
                    pe.wait_ge(x_slice, 48 * (f + 1))
                    if m >= 2:
                        pe.wait_ge(h_sq, m - 1)
                    if m == 1:
                        pe.wait_ge(s_kept, NT)
                    for t in GTILES[g]:
                        o, c = tile_cols(t)
                        ins = pe.transpose(ps[6 + m % 2][:, o - GROUPS[g][0]:o - GROUPS[g][0] + c], xs[0:c, t, :],
                                           eye[0:c, 0:c])
                    ins.then_inc(x_slice_t, 1)
                    if f >= 2:
                        acc_free(pe, n - 2, g)

                if f == 0:
                    pe.wait_ge(yb_low_s, NT)
                    pe.wait_ge(ya_low_s, NH)
                dense(n, lambda k: (ya_h[:, k, :], ya_l[:, k, :]) if k < NH else (yb_h[:, k - NH, :], yb_l[:, k - NH, :]),
                      prepare=prepare)
            pe.wait_ge(h_sq, 3 * N_OUT)
            for g, (c0, w) in enumerate(GROUPS):
                if g == 0:
                    pe.wait_ge(x_slice_kept, 3 * N_OUT)
                if g == 2:
                    pe.wait_ge(rstd_mid, 1)
                pe.matmul(ps[6 + g % 2][:, 0:w], one[:, 0:1].to_broadcast([P, P]), hsq[:, c0:c0 + w], start=True,
                          stop=True).then_inc(h_sum, 1)

            def up(g, i):
                n = N_MIX + i

                def prepare(m):
                    pe.wait_ge(acc_read_dve, g * (6 * KT) + dve_reads_to(n - 2) + m + 1)
                    if i == 0:
                        pe.wait_ge(hg_low_s, 3 * N_OUT)
                dense(n, lambda k: (hg_h[:, k, :], hg_l[:, k, :]), g0=g, prepare=prepare)

            def down(g, i):
                n = N_MIX + KT + i

                def prepare(m):
                    pe.wait_ge(acc_read_dve, g * (6 * KT) + dve_reads_to(n - 2) + m + 1)
                    if i == 0:
                        pe.wait_ge(u_low_s, g * (3 * KT) + 3 * (KT - 1) + m + 1)
                dense(n, lambda k: (u_h[:, k, :], u_l[:, k, :]), g0=g, prepare=prepare)

            with pe.Fori(0, FG) as g:
                for i in range(KT):
                    up(g, i)
                for i in range(KT):
                    down(g, i)
            for t in range(NT):
                o, c = tile_cols(t)
                if t == 0:
                    pe.wait_ge(acc_read_dve, dve_reads_to(N_MIX + 2 * KT * FG))
                if t >= 2:
                    pe.wait_ge(fin_y, t - 1)
                for k in range(KT):
                    ins = pe.transpose(ps[4 * (t % 2) + k // 4][0:c, P * (k % 4):P * (k % 4) + P], hT[:, k, o:o + c], eye)
                ins.then_inc(fin_turned, 1)

        @block.vector
        def _(dve):
            steps = [0]

            def link(ins):
                steps[0] += 1
                ins.then_inc(dve_step, 1)
                dve.wait_ge(dve_step, steps[0])

            for t in range(NT):
                dve.wait_ge(x_sq, t + 1)
                dve.tensor_scalar(ssx[0:rows(t), t:t + 1], ssx[0:rows(t), t:t + 1], 1.0 / D, EPS, ALU.mult,
                                  ALU.add).then_inc(x_ms, 1)
                if t == 0:
                    dve.wait_ge(rows_turned, 2)
                    dve.tensor_copy(tn[:, :], ps[0][:, 0:16]).then_inc(rows_kept, 1)
                    dve.tensor_copy(tq[:, :, :], ps[1][:, 0:336].rearrange("p (f r) -> p f r", r=28)).then_inc(rows_kept, 1)
                    dve.tensor_copy(ta[:, :, :], ps[2][:, 0:76].rearrange("p (f r) -> p f r", r=19)).then_inc(rows_kept, 1)
                if t:
                    dve.wait_ge(x_pow, t)
                    dve.tensor_scalar(x_tile(t - 1), x_tile(t - 1), rx[0:rows(t - 1), t - 1:t], None,
                                      ALU.mult).then_inc(x_scaled, 1)
            dve.wait_ge(x_pow, NT)
            dve.tensor_scalar(x_tile(NT - 1), x_tile(NT - 1), rx[:, NT - 1:NT], None, ALU.mult).then_inc(x_scaled, 1)
            for g, (c0, w) in enumerate(GROUPS):
                for k in range(KT):
                    dve.wait_ge(x_high, KT * g + k + 1)
                    dve.scalar_tensor_tensor(out=xl[:, k, c0:c0 + w], in0=ps[k][:, 0:w], scalar=tn[:, k:k + 1],
                                             in1=xh[:, k, c0:c0 + w].bitcast(F32), op0=ALU.mult,
                                             op1=ALU.subtract).then_inc(x_low, 1)
            dve.wait_ge(ab_turned, 1)
            dve.wait_ge(set_ones, 3)
            dve.tensor_copy(ab[0:C0, 0, :], ps[6][0:C0, 0:8])
            dve.tensor_copy(ab[:, 1:NT, :], ps[6][:, 8:8 * NT].rearrange("p (t j) -> p t j", j=8)).then_inc(ab_tok, 1)
            dve.wait_ge(ab_tok, 1)
            link(dve.tensor_tensor(sc["g"][:, :, :], ab[:, :, 0:NH], dtb[:, :].unsqueeze(1).to_broadcast([P, NT, NH]), ALU.add))
            link(dve.tensor_scalar(sc["eg"][:, :, :], sc["g"][:, :, :], -1.0, None, ALU.mult))
            dve.tensor_tensor(sc["eg"][:, :, :], sc["eg"][:, :, :], sc["g"][:, :, :], ALU.max).then_inc(ab_tok, 1)
            dve.wait_ge(ab_act, 4)
            link(dve.tensor_scalar(sc["g"][:, :, :], sc["g"][:, :, :], 0.0, None, ALU.max))
            link(dve.tensor_tensor(sc["g"][:, :, :], sc["g"][:, :, :], sc["tmp"][:, :, :], ALU.add))
            link(dve.tensor_tensor(sc["g"][:, :, :], sc["g"][:, :, :], al[:, :].unsqueeze(1).to_broadcast([P, NT, NH]), ALU.mult))
            link(dve.tensor_scalar(sc["g"][:, :, :], sc["g"][:, :, :], -1.0, None, ALU.mult))
            link(dve.tensor_scalar(sc["beta"][:, :, :], sc["beta"][:, :, :], 1.0, None, ALU.add))
            dve.reciprocal(sc["beta"][:, :, :], sc["beta"][:, :, :]).then_inc(g_ready, 1)
            dve.tensor_tensor(g_seq[0:C0, :, :], sc["g"][0:C0, 0, :].unsqueeze(1).to_broadcast([C0, NSEQ, NH]),
                              same_s[:, 0:NS:LSEQ].unsqueeze(2).to_broadcast([C0, NSEQ, NH]), ALU.mult).then_inc(g_ready, 1)

            def conv(zr, r, samp_w, pre, wt, taps, dst):
                zs = zr[:, 0:NSEQ * samp_w].rearrange("p (b r) -> p b r", r=samp_w)
                ds = dst[:, 0:NS].rearrange("p (b r) -> p b r", r=LSEQ)
                for j in range(taps):
                    w = wt[:, j:j + 1]
                    main = zr[:, pre + j:pre + j + PRM]
                    if j == 0:
                        dve.tensor_scalar(dst[:, NS:TOK], main, w, None, ALU.mult)
                        link(dve.tensor_scalar(ds, zs[:, :, j:j + LSEQ], w, None, ALU.mult))
                    else:
                        dve.scalar_tensor_tensor(out=dst[:, NS:TOK], in0=main, scalar=w, in1=dst[:, NS:TOK],
                                                 op0=ALU.mult, op1=ALU.add)
                        ins = dve.scalar_tensor_tensor(out=ds, in0=zs[:, :, j:j + LSEQ], scalar=w, in1=ds,
                                                       op0=ALU.mult, op1=ALU.add)
                        if j < taps - 1:
                            link(ins)
                return ins

            def keep_last(m, r):
                dve.wait_ge(last_turned, m + 1)
                if m >= 2:
                    dve.wait_ge(last_sent[m % 2], 32 * (m // 2))
                dve.tensor_copy(last_out[m % 2][0:r, :], ps[6][0:r, 0:P]).then_inc(last_kept, 1)

            for n in range(N_IN):
                kind, i, _ = IN_TILES[n]
                if kind in ("k", "q", "v"):
                    f = {"q": 0, "k": NH, "v": 2 * NH}[kind] + i
                    dst = {"k": kf, "q": qf, "v": vf}[kind][:, i, :]
                    dve.wait_ge(acc_read_act, 3 * n + 3)
                    dve.wait_ge(z_hist, n + 1)
                    if n == 0:
                        dve.wait_ge(x_sq, NT)
                    conv(z[n % 2], 3, 7, 56, tq[:, f, 24:28], 4, dst).then_inc(conv_done, 1)
                if kind == "H":
                    bank = [ps[(n % 2) * 3 + g] for g in range(3)]
                    dve.wait_ge(z_hist, 3 * NH + i + 1)
                    for g, (c0, w) in enumerate(GROUPS):
                        dve.wait_ge(acc_done, 3 * n + g + 1)
                        dve.wait_ge(acc_read_act, 3 * sum(act_reads[:n]))
                        if i and g == 0:
                            dve.wait_ge(last_cols, 3 * NH + i)
                        if g == 0:
                            dve.tensor_tensor(z[1][:, 0:48].rearrange("p (b r) -> p b r", r=6)[:, :, 2:6],
                                              bank[0][:, 0:NS].rearrange("p (b r) -> p b r", r=LSEQ),
                                              z[0][:, 0:NS].rearrange("p (b r) -> p b r", r=LSEQ), ALU.mult)
                            dve.tensor_tensor(z[1][:, 50:50 + w - NS], bank[0][:, NS:w], z[0][:, NS:w],
                                              ALU.mult).then_inc(acc_read_dve, 1)
                        else:
                            ins = dve.tensor_tensor(z[1][:, 50 + c0 - NS:50 + c0 - NS + w], bank[g][:, 0:w],
                                                    z[0][:, c0:c0 + w], ALU.mult)
                            ins.then_inc(acc_read_dve, 1)
                    dve.wait_ge(acc_read_dve, dve_reads_to(n) + 3)
                    conv(z[1], 2, 6, 48, ta[:, i, 16:19], 3, z[0]).then_inc(conv_done, 1)
                if kind == "B":
                    dve.wait_ge(conv_done, 3 * NH + i + 1)
                    dve.wait_ge(last_cols, 3 * NH + i + 1)
                    for g, (c0, w) in enumerate(GROUPS):
                        dve.wait_ge(acc_done, 3 * n + g + 1)
                        dve.tensor_tensor(z[1][:, c0:c0 + w], ps[(n % 2) * 3 + g][:, 0:w], z[0][:, c0:c0 + w],
                                          ALU.mult).then_inc(acc_read_dve, 1)
                    dve.wait_ge(ya_high_s, 3 * i + 3)
                    dve.tensor_tensor(ya_l[:, i, :], z[1][:, 0:TOK], ya_h[:, i, :].bitcast(F32),
                                      ALU.subtract).then_inc(ya_low_s, 1)
                if n == 0:
                    dve.wait_ge(g_summed, 1)
                    dve.memset(sc["gneg"][:, 0, :], 0.0)
                    link(dve.memset(sc["egl"][:, 0, :], 0.0))
                    dve.memset(sc["eglb"][:, 0, :], 0.0)
                    g3 = lambda ap: ap.rearrange("p (t h) -> p t h", h=NH)
                    dve.tensor_scalar(sc["gneg"][:, 1:NT, :], g3(ps[7][:, 0:32]), -1.0, None, ALU.mult)
                    link(dve.tensor_scalar(sc["gneg"][0:C0, 0, :], ps[7][0:C0, 32:36], -1.0, None, ALU.mult))
                    dve.tensor_tensor(sc["egl"][:, 1:NT, :], g3(ps[7][:, 64:96]), sc["gneg"][:, 1:NT, :],
                                      ALU.add).then_inc(g_kept, 1)
                    dve.tensor_tensor(sc["egl"][0:C0, 0, :], ps[7][0:C0, 96:100], sc["gneg"][0:C0, 0, :],
                                      ALU.add).then_inc(g_kept, 1)
                    dve.tensor_copy(sc["eglb"][:, 1:NT, :], g3(ps[7][:, 64:96])).then_inc(g_kept, 1)
                    dve.tensor_copy(eg_seq[:, :, :], ps[7][:, 128:160].rearrange("p (b h) -> p b h", h=NH)).then_inc(g_kept, 1)
                if n and has_last(n - 1):
                    keep_last(last_index(n - 1), 18 if IN_TILES[n - 1][0] == "H" else 27)

            nk, rk, c_, p_ = sc["nk"], sc["rk"], sc["c"], sc["p"]
            dve.wait_ge(ss_done, 2 * NH)
            dve.memset(nk[:, 0, :], 1.0)
            link(dve.memset(sc["rq_s"][:, 0, :], 1.0))
            s4 = ps[7][:, 0:2 * NH * NT].rearrange("p (t j) -> p t j", j=2 * NH)
            dve.tensor_scalar(nk[:, 1:NT, :], s4[:, 1:NT, 0:NH], EPS, None, ALU.add)
            dve.tensor_scalar(nk[0:C0, 0, :], s4[0:C0, 0, 0:NH], EPS, None, ALU.add)
            dve.tensor_scalar(sc["rq_s"][:, 1:NT, :], s4[:, 1:NT, NH:2 * NH], EPS, None, ALU.add)
            dve.tensor_scalar(sc["rq_s"][0:C0, 0, :], s4[0:C0, 0, NH:2 * NH], EPS, None, ALU.add).then_inc(norms_mid, 1)
            dve.wait_ge(norms_mid, 3)
            dve.wait_ge(g_exp, 4)
            dve.reciprocal(rk[:, :, :], nk[:, :, :])
            link(dve.reciprocal(sc["rq_s"][:, :, :], sc["rq_s"][:, :, :]))
            dve.tensor_scalar(sc["rq_s"][:, :, :], sc["rq_s"][:, :, :], float(P) ** -0.5, None, ALU.mult)
            dve.tensor_tensor(sc["kd_s"][:, :, :], rk[:, :, :], sc["egl"][:, :, :], ALU.mult)
            link(dve.tensor_tensor(c_[:, :, :], rk[:, :, :], sc["beta"][:, :, :], ALU.mult))
            dve.tensor_tensor(p_[:, :, :], c_[:, :, :], rk[:, :, :], ALU.mult).then_inc(norms_done, 1)
            dve.wait_ge(norms_done, 1)

            h3 = lambda ap: ap.rearrange("p (h i) -> p h i", h=NH)

            def keep_kv(t):
                c, st, tb = rows(t), gd[cset(t)], tmpb[parity(t)]
                b0, b1 = ps[2 * parity(t)][0:c, :], ps[2 * parity(t) + 1][0:c, :]
                dve.wait_ge(kv_turned, t + 1)
                if t == 2:
                    dve.wait_ge(out_sent, 16 * NH)
                if t >= 3:
                    dve.wait_ge(w_made, t - 1)
                if t >= 5:
                    dve.wait_ge(os_made, t - 3)
                dve.tensor_tensor(h3(tb["kg"][0:c, :]), h3(b0), per_head(sc["eg"][0:c, t, :], c, P), ALU.mult)
                dve.tensor_tensor(h3(st["kd"][0:c, :]), h3(b0), per_head(sc["kd_s"][0:c, t, :], c, P), ALU.mult)
                dve.tensor_tensor(h3(st["vn"][0:c, :]), h3(b1), per_head(nk[0:c, t, :], c, P), ALU.mult).then_inc(kv_kept, 1)

            def decay_diff(t):
                c, st = rows(t), gd[cset(t)]
                dve.wait_ge(g_rows, t + 1)
                for h in range(NH):
                    ins = dve.tensor_scalar(st["wn"][0:c, c * h:c * h + c], ps[2 * parity(t)][0:c, c * h:c * h + c],
                                            sc["gneg"][0:c, t, h:h + 1], 0.0, ALU.add, ALU.min)
                ins.then_inc(g_diff, 1)

            def keep_products(t):
                c, st, tb = rows(t), gd[cset(t)], tmpb[parity(t)]
                dve.wait_ge(kk_made, t + 1)
                dve.wait_ge(d_mask, t + 1)
                for i, (dst, s) in enumerate(((tb["At"], p_), (st["qk"], rk))):
                    for h in range(NH):
                        cs = slice(c * h, c * h + c)
                        ins = dve.scalar_tensor_tensor(out=dst[0:c, cs], in0=ps[2 * parity(t) + i][0:c, cs],
                                                       scalar=s[0:c, t, h:h + 1], in1=st["wn"][0:c, cs], op0=ALU.mult,
                                                       op1=ALU.mult)
                ins.then_inc(kk_kept, 1)

            def keep_p(t, k):
                c, par, b = rows(t), parity(t), 2 ** k
                at_level = level_at(t, k)
                dve.wait_ge(p_made[par], at_level)
                dve.wait_ge(pair_zero[par], at_level)
                m = (lev_small if t == 0 else lev_big)[k][0:c, :]
                src = h3(ps[2 * par][0:c, 0:NH * c // 2]).rearrange("p h (n b) -> p h n b", b=b)
                dst = heads(pb[par][at_level % 2], c).rearrange("p (h n two b) -> p h n two b", h=NH, two=2, b=b)[:, :, :, 0, :]
                mask = m.rearrange("p (n b) -> p n b", b=b).unsqueeze(1).to_broadcast([c, NH, c // 2 // b, b])
                dve.tensor_tensor(dst, src, mask, ALU.mult).then_inc(p_kept[par], 1)

            def keep_xy(t, k):
                c, st, tb, par, b = rows(t), gd[cset(t)], tmpb[parity(t)], parity(t), 2 ** k
                at_level, last = level_at(t, k), k == (SMALL_LEVELS if t == 0 else LEVELS) - 1
                dve.wait_ge(xy_made[par], at_level)
                n3 = lambda ap: ap.rearrange("p (n b) -> p n b", b=b)
                if not last:
                    xf = first(heads(tb["X"], c), b)
                    dve.tensor_tensor(xf, xf, n3(ps[2 * par + 1][0:c, 0:NH * c // 2]), ALU.subtract)
                ys = second(heads(st["Y"], c), b)
                dve.tensor_tensor(ys, ys, n3(ps[2 * par + 1][0:c, 256:256 + NH * c // 2]),
                                  ALU.subtract).then_inc(xy_kept[par], 1)

            def keep_v(t):
                c = rows(t)
                dve.wait_ge(v_made, t)
                dve.wait_ge(os_made, t)
                dve.tensor_tensor(h3(vnew[0:c, :]), h3(ps[4][0:c, :]), per_head(c_[0:c, t, :], c, P),
                                  ALU.mult).then_inc(v_kept, 1)
                if t:
                    dve.wait_ge(o_sq, t)
                dve.tensor_tensor(h3(t1[0:c, :]), h3(ps[5][0:c, :]), per_head(sc["eg"][0:c, t, :], c, P),
                                  ALU.mult).then_inc(qs_kept, 1)

            def keep_state(t):
                dve.wait_ge(os_made, t + 1)
                for h in range(NH):
                    hs = slice(P * h, P * h + P)
                    ins = dve.scalar_tensor_tensor(out=S[:, hs], in0=S[:, hs], scalar=sc["eglb"][:, t, h:h + 1],
                                                   in1=ps[7][:, hs], op0=ALU.mult, op1=ALU.add)
                ins.then_inc(s_kept, 1)

            def keep_o(t):
                c = rows(t)
                dve.wait_ge(qs_kept, t + 1)
                if t:
                    dve.wait_ge(o_turned, t)
                dve.tensor_tensor(ob[0:c, :], ps[6][0:c, :], t1[0:c, :], ALU.add).then_inc(o_kept, 1)

            def norm_o(t):
                c = rows(t)
                dve.wait_ge(o_sq, t + 1)
                dve.tensor_scalar(sc["tmp"][0:c, t, :], sc["sso"][0:c, t, :], 1.0 / P, EPS, ALU.mult,
                                  ALU.add).then_inc(o_ms, 1)
                dve.wait_ge(o_pow, t + 1)
                link(dve.tensor_tensor(sc["fo"][0:c, t, :], sc["fo"][0:c, t, :], sc["rq_s"][0:c, t, :], ALU.mult))
                dve.tensor_tensor(h3(ob[0:c, :]), h3(ob[0:c, :]), per_head(sc["fo"][0:c, t, :], c, P),
                                  ALU.mult).then_inc(o_normed, 1)

            def gate_o(t):
                o, c = tile_cols(t)
                dve.wait_ge(o_turned, t + 1)
                dve.scalar_tensor_tensor(out=ybt[:, :, 0:c], in0=h3(ps[5][:, 0:NH * c]), scalar=gn[:, 0:1],
                                         in1=gate[:, :, o:o + c], op0=ALU.mult, op1=ALU.mult).then_inc(yb_full_s, 1)
                dve.wait_ge(yb_high_s, t + 1)
                dve.tensor_tensor(yb_l[:, :, o:o + c], ybt[:, :, 0:c], yb_h[:, :, o:o + c].bitcast(F32),
                                  ALU.subtract).then_inc(yb_low_s, 1)

            def chain_step(k, a, b):
                if k == 1:
                    keep_v(a)
                if k == 2:
                    keep_state(a)
                    keep_o(a)
                if k == 3:
                    keep_v(b)
                    norm_o(a)
                if k == 4:
                    gate_o(a)
                    keep_state(b)
                    keep_o(b)
                if k == 5:
                    norm_o(b)
                if k == 6:
                    gate_o(b)

            dve.wait_ge(acc_done, 3 * N_IN)
            keep_kv(0)
            decay_diff(0)
            keep_products(0)
            for k in range(1, SMALL_LEVELS):
                keep_p(0, k)
                keep_xy(0, k)
            dve.wait_ge(ss_made, NH)
            dve.tensor_tensor(h3(vnew[0:C0, :]), h3(ps[4][0:C0, :]), per_head(c_[0:C0, 0, :], C0, P),
                              ALU.mult).then_inc(v_kept, 1)
            dve.tensor_tensor(h3(t1[0:C0, :]), h3(ps[5][0:C0, :]), per_head(sc["eg"][0:C0, 0, :], C0, P),
                              ALU.mult).then_inc(qs_kept, 1)
            dve.wait_ge(v_kept, 1)
            for h in range(NH):
                if h:
                    dve.wait_ge(ss_made, NH + h)
                dve.tensor_tensor(vm[:, :, :], vnew[0:C0, P * h:P * h + P].unsqueeze(1).to_broadcast([C0, NSEQ + 1, P]),
                                  own[0:C0, :].unsqueeze(2).to_broadcast([C0, NSEQ + 1, P]), ALU.mult).then_inc(vm_made, 1)
                link(dve.tensor_tensor(SSs[:, h, :, :], SSs[:, h, :, :],
                                       eg_seq[:, :, h:h + 1].to_broadcast([P, NSEQ, P]), ALU.mult))
                dve.wait_ge(ss_made, NH + h + 1)
                for half in range(2):
                    sh = SSs[:, h, 4 * half:4 * half + 4, :]
                    dve.tensor_tensor(sh, sh, ps[half][:, :].rearrange("p (b e) -> p b e", b=4), ALU.add).then_inc(ss_kept, 1)
            dve.tensor_copy(S[:, :], ps[7][:, :]).then_inc(s_kept, 1)
            dve.wait_ge(os_made, 1)
            keep_o(0)
            norm_o(0)
            gate_o(0)
            for n, pr in enumerate(pairs):
                for step in (keep_kv, decay_diff, keep_products):
                    for t in pr:
                        step(t)
                for k in range(1, LEVELS):
                    for t in pr:
                        keep_p(t, k)
                    if n:
                        chain_step(k, *pairs[n - 1])
                    for t in pr:
                        keep_xy(t, k)
            for k in range(1, LEVELS):
                chain_step(k, *pairs[-1])

            for f in range(N_OUT):
                n = N_IN + f
                for g, (c0, w) in enumerate(GROUPS):
                    m = 3 * f + g
                    hc = hT[:, f, c0:c0 + w]
                    dve.wait_ge(x_slice_t, m + 1)
                    dve.tensor_copy(hc, ps[6 + m % 2][:, 0:w]).then_inc(x_slice_kept, 1)
                    dve.wait_ge(acc_done, 3 * n + g + 1)
                    dve.wait_ge(x_slice_kept, m + 1)
                    dve.tensor_tensor(hc, hc, ps[(n % 2) * 3 + g][:, 0:w], ALU.add).then_inc(acc_read_dve, 1)
                    dve.wait_ge(acc_read_dve, dve_reads_to(n) + g + 1)
                    hs_ = hsq[:, c0:c0 + w]
                    if f == 0:
                        dve.tensor_tensor(hs_, hc, hc, ALU.mult).then_inc(h_sq, 1)
                    else:
                        square = ps[6 + m % 2][:, 0:w]
                        link(dve.tensor_tensor(square, hc, hc, ALU.mult))
                        dve.tensor_tensor(hs_, hs_, square, ALU.add).then_inc(h_sq, 1)
                    dve.wait_ge(hg_high_s, m + 1)
                    dve.scalar_tensor_tensor(out=hg_l[:, f, c0:c0 + w], in0=hc, scalar=tn[:, 8 + f:9 + f],
                                             in1=hg_h[:, f, c0:c0 + w].bitcast(F32), op0=ALU.mult,
                                             op1=ALU.subtract).then_inc(hg_low_s, 1)
            for g, (c0, w) in enumerate(GROUPS):
                dve.wait_ge(h_sum, g + 1)
                dve.tensor_scalar(hsq[:, c0:c0 + w], ps[6 + g % 2][:, 0:w], 1.0 / D, EPS, ALU.mult,
                                  ALU.add).then_inc(rstd_mid, 1)
            dve.wait_ge(rstd_b, 1)
            link(dve.reciprocal(hsq[:, :], hsq[:, :]))

            def up_rows(g, i):
                n = N_MIX + i
                for m, (c0, w) in enumerate(GROUPS):
                    j = 3 * i + m
                    dve.wait_ge(acc_done, g * (6 * KT) + 3 * n + m + 1)
                    ub = ut[j % 2][:, 0:w]
                    dve.tensor_tensor(ub, ps[(n % 2) * 3 + m][:, 0:w], hsq[:, c0:c0 + w], ALU.mult).then_inc(acc_read_dve, 1)
                    dve.wait_ge(acc_read_dve, g * (6 * KT) + dve_reads_to(n) + m + 1)
                    dve.scalar_tensor_tensor(out=ub, in0=ub, scalar=0.0, in1=ub, op0=ALU.max, op1=ALU.mult).then_inc(u_full, 1)
                    dve.wait_ge(u_high_s, g * (3 * KT) + j + 1)
                    dve.tensor_tensor(u_l[:, i, c0:c0 + w], ub, u_h[:, i, c0:c0 + w].bitcast(F32),
                                      ALU.subtract).then_inc(u_low_s, 1)

            def down_rows(g, i):
                n = N_MIX + KT + i
                for m, (c0, w) in enumerate(GROUPS):
                    hc = hT[:, i, c0:c0 + w]
                    dve.wait_ge(acc_done, g * (6 * KT) + 3 * n + m + 1)
                    dve.tensor_tensor(hc, hc, ps[(n % 2) * 3 + m][:, 0:w], ALU.add)\
                       .then_inc(acc_read_dve, 1)

            with dve.Fori(0, FG) as g:
                for i in range(KT):
                    up_rows(g, i)
                for i in range(KT):
                    down_rows(g, i)
            dve.wait_ge(fin_const, 16)
            for t in range(NT):
                c = rows(t)
                dve.wait_ge(fin_sq, t + 1)
                link(dve.tensor_tensor(ssx[0:c, t:t + 1], sc["sso"][0:c, t, 0:1], sc["sso"][0:c, t, 1:2], ALU.add))
                dve.tensor_scalar(ssx[0:c, t:t + 1], ssx[0:c, t:t + 1], 1.0 / D, EPS, ALU.mult, ALU.add).then_inc(fin_ms, 1)
                dve.wait_ge(fin_pow, t + 1)
                for half in range(2):
                    ins = dve.scalar_tensor_tensor(out=yt[t % 3][0:c, 512 * half:512 * half + 512],
                                                   in0=ps[4 * (t % 2) + half][0:c, :], scalar=rx[0:c, t:t + 1],
                                                   in1=nfin[0:c, 512 * half:512 * half + 512], op0=ALU.mult, op1=ALU.mult)
                ins.then_inc(fin_y, 1)


_INS = ["x_prompt", "x_sample", "state_conv_a", "state_conv_qkv", "state_ssm", "meta_tokens", "norm_mix", "w_in",
        "conv_a_w", "conv_qkv_w", "a_log", "dt_bias", "gdn_norm", "w_out", "norm_ffn", "w_up", "w_down", "norm_final"]
_OUTS = [(1, SEQ, D), (NSEQ, LSEQ, D), (1, 1, 2, CONV), (1, 1, 3, QKVW), (1, 1, NH, P, P),
         (1, NSEQ, 2, CONV), (1, NSEQ, 3, QKVW), (1, NSEQ, NH, P, P)]


def kernel(**inputs):
    import concourse.bacc as bacc
    from concourse.bass_utils import run_bass_kernel_spmd

    nc = bacc.Bacc("TRN2", target_bir_lowering=False, num_devices=1)
    arrays, args = {}, []
    tables = dict(zip(("c_main", "c_gdn"), constants()))
    for name in _INS + list(tables):
        a = np.ascontiguousarray(tables[name] if name in tables else inputs[name])
        arrays[f"in_{name}"] = a
        args.append(nc.dram_tensor(f"in_{name}", a.shape, mybir.dt.from_np(a.dtype), kind="ExternalInput").ap())
    for i, shape in enumerate(_OUTS):
        args.append(nc.dram_tensor(f"out_{i}", shape, F32, kind="ExternalOutput").ap())
    build(nc, *args)
    got = run_bass_kernel_spmd(nc, [arrays], core_ids=[0])
    return tuple(got.results[0][f"out_{i}"] for i in range(len(_OUTS)))
```

```python
from contextlib import ExitStack

import numpy as np

import concourse.bass as bass
from concourse import mybir

ALU = mybir.AluOpType
ACT = mybir.ActivationFunctionType
AX = mybir.AxisListType
F32 = mybir.dt.float32
F32R = mybir.dt.float32r

P = 128
D = 1024
KT = D // P
SEQ, META, NSEQ, LSEQ = 1024, 16, 8, 4
NH = 4
CONV = D // 2
QKVW = NH * 3 * P
FFN = 4 * D
EPS = 1e-6
NS = NSEQ * LSEQ
C0 = NS + META
NT = 1 + SEQ // P
TOK = C0 + SEQ
PRM = TOK - NS
GROUPS = [(0, C0 + 2 * P), (C0 + 2 * P, 3 * P), (C0 + 5 * P, 3 * P)]
GTILES = [(0, 1, 2), (3, 4, 5), (6, 7, 8)]
O_B, O_C, O_H, O_QKV = 0, CONV, 2 * CONV, 3 * CONV
O_G = O_QKV + QKVW
O_A = O_G + NH * P
SMALL_LEVELS, LEVELS = 4, 7

IN_TILES = ([("k", h, O_QKV + NH * P + P * h) for h in range(NH)] + [("q", h, O_QKV + P * h) for h in range(NH)]
            + [("v", h, O_QKV + 2 * NH * P + P * h) for h in range(NH)] + [("gate", h, O_G + P * h) for h in range(NH)]
            + [x for i in range(CONV // P) for x in (("C", i, O_C + P * i), ("H", i, O_H + P * i), ("B", i, O_B + P * i))])
N_IN = len(IN_TILES)
N_OUT = D // P
N_MIX = N_IN + N_OUT
FG = FFN // D


def tile_cols(t):
    return (0, C0) if t == 0 else (C0 + (t - 1) * P, P)


def constants():
    j, i = np.arange(P)[:, None], np.arange(P)[None, :]
    seq = np.where(np.arange(C0) < NS, np.arange(C0) // LSEQ, NSEQ)
    same = seq[:, None] == seq[None, :]
    up = (j <= i)
    main = np.zeros((P, 2 * P + 2 * C0 + 2 * NH), np.float32)
    main[:, 0:P] = j == i
    main[:, P:2 * P] = up
    main[:C0, 2 * P:2 * P + C0] = same & up[:C0, :C0]
    main[:C0, 2 * P + C0:2 * P + 2 * C0] = same
    main[:16, 2 * P + 2 * C0:] = np.tile(np.eye(8), (2, 1))
    g = [((i == j + 1) & (j % 2 == 0)).astype(np.float32)]
    for c, levels in ((P, LEVELS), (C0, SMALL_LEVELS)):
        for k in range(1, levels):
            b = 2 ** k
            first = np.arange(c // 2) // b
            m = np.zeros((P, c // 2), np.float32)
            r = np.arange(c)
            m[:c] = (r[:, None] // (2 * b) == first[None, :]) & (r[:, None] % (2 * b) >= b)
            g.append(m)
    own = np.zeros((P, NSEQ + 1), np.float32)
    own[np.arange(C0), seq] = 1
    g.append(own)
    return main, np.concatenate(g, axis=1).astype(np.float32)


def build(nc, x_prompt, x_sample, state_conv_a, state_conv_qkv, state_ssm, meta_tokens, norm_mix, w_in,
          conv_a_w, conv_qkv_w, a_log, dt_bias, gdn_norm, w_out, norm_ffn, w_up, w_down, norm_final,
          c_main, c_gdn, y_prompt, y_sample, new_a_prompt, new_qkv_prompt, new_ssm_prompt,
          new_a_sample, new_qkv_sample, new_ssm_sample):
    ctx = ExitStack()
    with ctx:
        SLOT = TOK * 4
        R1 = 16512
        RK = R1 + 16 * SLOT
        RYA = RK + 8 * SLOT
        RQ = RK + 16 * SLOT
        RG = RK + 20 * SLOT
        RING = RK + 24 * SLOT
        RZ = RING + 6 * 4096
        ZB = 4448
        RS = RZ + 2 * ZB
        at = {"small": RS}

        def place(name, shape, dt, offset):
            return nc.alloc_sbuf_tensor_at(name, shape, dt, offset=offset)

        def small(name, shape):
            size = 4
            for s in shape[1:]:
                size *= s
            t = place(name, shape, F32, at["small"])
            at["small"] += (size + 31) // 32 * 32
            assert at["small"] <= 229368, name
            return t

        def sem(name):
            return ctx.enter_context(nc.semaphore(name))

        ps = [ctx.enter_context(nc.psum_tensor(f"bank{i}", [P, 512], F32)) for i in range(8)]

        xh = place("xn_high", [P, KT, TOK], F32R, R1)
        xl = place("xn_low", [P, KT, TOK], F32R, R1 + KT * SLOT)
        kf = place("k_feat", [P, NH, TOK], F32, RK)
        vf = place("v_feat", [P, NH, TOK], F32, RK + 4 * SLOT)
        qf = place("q_feat", [P, NH, TOK], F32, RQ)
        gate = place("gate_feat", [P, NH, TOK], F32, RG)
        ya_h = place("ya_high", [P, NH, TOK], F32R, RYA)
        ya_l = place("ya_low", [P, NH, TOK], F32R, RYA + 4 * SLOT)
        yb_h = place("yb_high", [P, NH, TOK], F32R, RK + 4 * SLOT)
        yb_l = place("yb_low", [P, NH, TOK], F32R, RK)
        hT = place("hT", [P, KT, TOK], F32, RQ)
        hg_h = place("hg_high", [P, KT, TOK], F32R, R1)
        hg_l = place("hg_low", [P, KT, TOK], F32R, R1 + KT * SLOT)
        u_h = place("u_high", [P, KT, TOK], F32R, RK)
        u_l = place("u_low", [P, KT, TOK], F32R, RK + KT * SLOT)
        w_raw = [place(f"w_raw{i}", [P, KT, P], F32, RING + 4096 * i) for i in range(2)]
        w_h = [place(f"w_high{i}", [P, KT, P], F32R, RING + 4096 * (2 + i)) for i in range(2)]
        w_l = [place(f"w_low{i}", [P, KT, P], F32R, RING + 4096 * (4 + i)) for i in range(2)]
        z = [place(f"conv_row{i}", [P, ZB // 4], F32, RZ + ZB * i) for i in range(2)]

        x_big = place("x_tok", [P, NT - 1, D], F32, RYA)
        x_small = place("x_tok0", [P, D], F32, RZ)
        square_out = place("square_out", [P, D], F32, RK)
        rows_q = place("rows_q", [28, QKVW], F32, RG)
        rows_a = place("rows_a", [19, CONV], F32, RG + 6144)
        rows_n = place("rows_n", [16, P], F32, RG + 8192)
        ab_raw = place("ab_raw", [P, KT, 8], F32, RG + 3 * SLOT)
        ab_w = place("ab_w", [P, KT, 16], F32R, RG + 3 * SLOT + 256)
        abT = place("abT", [16, TOK], F32, RK + 4 * SLOT)
        sq = [place(f"squares{i}", [P, TOK], F32, RYA + i * SLOT) for i in range(2)]
        sq_h = [place(f"squares_high{i}", [P, TOK], F32R, RYA + (2 + i) * SLOT) for i in range(2)]
        sq_l = [place(f"squares_low{i}", [P, TOK], F32R, RYA + (4 + i) * SLOT) for i in range(2)]
        NROW = 3 * 2 * NH
        pick = place("pick", [P, 2 * NROW], F32R, RYA + 6 * SLOT)
        ssr = place("ss_rows", [NROW, 3 * P], F32, RYA + 7 * SLOT)

        cm = small("c_main", [P, 2 * P + 2 * C0 + 2 * NH])
        eye, upper = cm[:, 0:P], cm[:, P:2 * P]
        upper_s, same_s = cm[0:C0, 2 * P:2 * P + C0], cm[0:C0, 2 * P + C0:2 * P + 2 * C0]
        fold_ab = cm[0:16, 2 * P + 2 * C0:]
        one = small("one", [P, 1])
        mhalf = small("minus_half", [P, 1])
        tq = small("tq", [P, QKVW // P, 28])
        ta = small("ta", [P, CONV // P, 19])
        tn = small("tn", [P, 16])
        gn = small("gdn_norm_col", [P, 1])
        al = small("a_log_b", [P, NH])
        dtb = small("dt_bias_b", [P, NH])
        last_in = [small(f"last_in{i}", [P, 27]) for i in range(2)]
        last_out = [small(f"last_out{i}", [27, P]) for i in range(2)]
        ssx = small("ssx", [P, NT])
        rx = small("rx", [P, NT])
        ab = small("ab", [P, NT, 2 * NH])
        sc = {n: small(n, [P, NT, NH]) for n in
              ("g", "beta", "gneg", "eg", "egl", "eglb", "nk", "rk", "c", "p", "kd_s", "rq_s", "sso", "fo", "tmp")}
        g_seq = small("g_seq", [P, NSEQ, NH])
        eg_seq = small("eg_seq", [P, NSEQ, NH])

        HB = NH * P * 4
        SET = ("Y", "wn", "vn", "kd", "qk")
        gd = [{n: place(f"{n}_{s}", [P, NH * P], F32, R1 + (5 * s + m) * HB) for m, n in enumerate(SET)} for s in range(4)]
        TB = R1 + 20 * HB
        tmpb = [{n: place(f"{n}_{s}", [P, NH * P], F32, TB + (3 * s + m) * HB) for m, n in enumerate(("kg", "At", "X"))}
                for s in range(2)]
        pb = [[place(f"pairs_{s}{i}", [P, NH * P], F32, TB + (6 + 2 * s + i) * HB) for i in range(2)] for s in range(2)]
        HC, T0 = NH * C0 * 4, R1 + 10 * HB
        CG_END = (TB + 11 * HB + 4 * c_gdn.shape[1] + 31) // 32 * 32
        assert CG_END + HB <= RK
        gd.append({**{n: place(f"{n}_t0", [C0, NH * C0], F32, T0 + 2 * HB + m * HC) for m, n in enumerate(("Y", "wn", "qk"))},
                   "vn": place("vn_t0", [C0, NH * P], F32, T0), "kd": place("kd_t0", [C0, NH * P], F32, CG_END)})
        tmpb.append({"kg": place("kg_t0", [C0, NH * P], F32, T0 + HB),
                     **{n: place(f"{n}_t0", [C0, NH * C0], F32, T0 + 2 * HB + (3 + m) * HC) for m, n in enumerate(("At", "X"))}})
        pb.append([place(f"pairs_t0{i}", [C0, NH * C0], F32, T0 + 2 * HB + (5 + i) * HC) for i in range(2)])
        S = place("S", [P, NH * P], F32, TB + 10 * HB)
        cg = place("c_gdn", [P, c_gdn.shape[1]], F32, TB + 11 * HB)
        assert TB + 11 * HB + 4 * c_gdn.shape[1] <= RK
        m0 = cg[:, 0:P]
        off = P
        lev_big = [None]
        for k in range(1, LEVELS):
            lev_big.append(cg[:, off:off + P // 2])
            off += P // 2
        lev_small = [None]
        for k in range(1, SMALL_LEVELS):
            lev_small.append(cg[:, off:off + C0 // 2])
            off += C0 // 2
        own = cg[:, off:off + NSEQ + 1]
        wq = place("wq_sample", [P, NH, NSEQ, 2 * LSEQ], F32, T0 + 5 * HB)
        wsT = place("ws_feat", [P, NH, C0], F32, T0 + 6 * HB)
        qsT = place("qs_feat", [P, NH, C0], F32, T0 + 6 * HB + HC)
        v_meta = place("v_meta", [C0, NH * P], F32, T0 + 7 * HB)
        SSs = place("S_sample", [P, NH, NSEQ, P], F32, RING)
        vm = [place(f"v_masked{i}", [C0, NSEQ, P], F32, RING + 4096 * (4 + i)) for i in range(2)]
        ob = place("o_tok", [P, NH * P], F32, RZ)
        t1 = place("qs_scaled", [P, NH * P], F32, RZ + HB)
        vnew = place("v_new", [P, NH * P], F32, RZ + 2 * HB)
        ybt = place("yb_full", [P, NH, P], F32, RZ + 3 * HB)

        xs = place("x_slice", [P, NT, P], F32, RZ)
        hsq = place("h_squares", [P, TOK], F32, RZ + NT * P * 4)
        ut = [place(f"u_work{i}", [P, 3 * P], F32, RZ + 3 * P * 4 * i) for i in range(2)]
        nfin = place("norm_final_b", [P, D], F32, R1)
        yt = [place(f"y_tok{i}", [P, D], F32, R1 + 4096 * (1 + i)) for i in range(3)]

        s_row = sem("s_row"); s_xin = [sem(f"s_xin{i}") for i in range(3)]; s_const = sem("s_const")
        x_sq = sem("x_sq"); x_pow = sem("x_pow"); x_ms = sem("x_ms"); x_scaled = sem("x_scaled")
        x_turned = sem("x_turned"); x_high = sem("x_high"); x_low = sem("x_low")
        set_ones = sem("set_ones"); rows_turned = sem("rows_turned"); rows_kept = sem("rows_kept")
        ab_hi = sem("ab_hi"); ab_lo = sem("ab_lo"); ab_made = sem("ab_made"); ab_kept = sem("ab_kept")
        ab_turned = sem("ab_turned"); ab_tok = sem("ab_tok"); ab_act = sem("ab_act"); g_ready = sem("g_ready")
        g_summed = sem("g_summed"); g_kept = sem("g_kept"); g_exp = sem("g_exp")
        w_load = [sem("w_load0"), sem("w_load1")]
        w_high = sem("w_high"); w_low = sem("w_low"); acc_done = sem("acc_done")
        acc_read_act = sem("acc_read_act"); acc_read_dve = sem("acc_read_dve")
        z_hist = sem("z_hist"); conv_done = sem("conv_done"); silu_done = sem("silu_done")
        last_cols = sem("last_cols"); last_turned = sem("last_turned"); last_kept = sem("last_kept")
        last_sent = [sem("last_sent0"), sem("last_sent1")]
        ya_high_s = sem("ya_high_s")
        ya_low_s = sem("ya_low_s")
        sq_full = sem("sq_full"); sq_high = sem("sq_high"); sq_low = sem("sq_low"); pick_set = sem("pick_set"); ss_rows = sem("ss_rows"); ss_turned = sem("ss_turned"); ss_done = sem("ss_done"); norms_done = sem("norms_done"); norms_mid = sem("norms_mid")
        s_gdn = sem("s_gdn"); s_states = sem("s_states")
        kv_turned = sem("kv_turned"); kv_kept = sem("kv_kept"); g_rows = sem("g_rows"); g_diff = sem("g_diff")
        d_exp = sem("d_exp"); d_mask = sem("d_mask"); kk_made = sem("kk_made"); kk_kept = sem("kk_kept")
        y_first = sem("y_first"); x_first_t = sem("x_first_t"); x_first = sem("x_first")
        pair_zero = [sem(f"pair_zero{i}") for i in range(3)]
        p_made = [sem(f"p_made{i}") for i in range(3)]; p_kept = [sem(f"p_kept{i}") for i in range(3)]
        xy_made = [sem(f"xy_made{i}") for i in range(3)]; xy_kept = [sem(f"xy_kept{i}") for i in range(3)]
        w_made = sem("w_made"); w_kept = sem("w_kept")
        v_made = sem("v_made"); v_kept = sem("v_kept"); qs_kept = sem("qs_kept")
        os_made = sem("os_made"); s_kept = sem("s_kept"); o_kept = sem("o_kept"); o_sq = sem("o_sq"); o_ms = sem("o_ms")
        o_pow = sem("o_pow"); o_normed = sem("o_normed"); o_turned = sem("o_turned"); yb_full_s = sem("yb_full_s")
        yb_high_s = sem("yb_high_s"); yb_low_s = sem("yb_low_s")
        q_beside = sem("q_beside"); ws_kept = sem("ws_kept"); ss_decayed = sem("ss_decayed"); vm_made = sem("vm_made"); ss_made = sem("ss_made"); ss_kept = sem("ss_kept")
        x_slice = sem("x_slice"); x_slice_t = sem("x_slice_t"); x_slice_kept = sem("x_slice_kept")
        hg_high_s = sem("hg_high_s"); hg_low_s = sem("hg_low_s"); h_sq = sem("h_sq")
        h_sum = sem("h_sum"); rstd_b = sem("rstd_b"); rstd_mid = sem("rstd_mid")
        u_full = sem("u_full"); u_high_s = sem("u_high_s"); u_low_s = sem("u_low_s")
        fin_const = sem("fin_const"); fin_turned = sem("fin_turned"); fin_sq = sem("fin_sq"); fin_ms = sem("fin_ms")
        fin_pow = sem("fin_pow"); fin_y = sem("fin_y"); fin_sent = [sem(f"fin_sent{i}") for i in range(3)]
        out_sent = sem("out_sent"); dve_step = sem("dve_step"); pool_step = sem("pool_step")

        act_reads = [k in ("k", "q", "v", "gate", "C") for k, _, _ in IN_TILES]

        def acc_free(pe, n, g):
            if n < N_IN and act_reads[n]:
                pe.wait_ge(acc_read_act, 3 * sum(act_reads[:n]) + g + 1)
            else:
                pe.wait_ge(acc_read_dve, dve_reads_to(n) + g + 1)

        def dve_reads_to(n):
            return 3 * (sum(not a for a in act_reads[:n]) + max(0, n - N_IN))

        def has_last(n):
            return IN_TILES[n][0] in ("k", "q", "v", "H")

        N_LAST = sum(has_last(n) for n in range(N_IN))

        def last_index(n):
            return sum(has_last(m) for m in range(n))

        def x_tile(t):
            return x_small[0:C0, :] if t == 0 else x_big[:, t - 1, :]

        def x_arrived(eng, t):
            if t == 0:
                eng.wait_ge(s_xin[0], 32)
            elif t <= 2:
                eng.wait_ge(s_xin[1], 16)
            else:
                eng.wait_ge(s_xin[2], 16)

        def rows(t):
            return C0 if t == 0 else P

        def heads(tile, c):
            return tile[0:c, 0:NH * c]

        def first(ap, b):
            return ap.rearrange("p (n two b) -> p n two b", two=2, b=b)[:, :, 0, :]

        def second(ap, b):
            return ap.rearrange("p (n two b) -> p n two b", two=2, b=b)[:, :, 1, :]

        def per_head(ap, c, w):
            return ap.unsqueeze(2).to_broadcast([c, NH, w])

        def over_heads(ap, c, w):
            return ap.unsqueeze(1).to_broadcast([c, NH, w])

        def parity(t):
            return 2 if t == 0 else (t - 1) % 2

        def cset(t):
            return 4 if t == 0 else (t - 1) % 4

        def level_at(t, k):
            if t == 0:
                return k
            return (LEVELS - 1) * ((t - 1) // 2) + k

        pairs = [(1 + 2 * i, 2 + 2 * i) for i in range((NT - 1) // 2)]
        w_up_v = w_up.rearrange("l (k p) n -> l p k n", p=P)[0]
        w_down_v = w_down.rearrange("l (k p) n -> l p k n", p=P)[0]
        w_in_v = w_in.rearrange("l (k p) n -> l p k n", p=P)[0]
        w_out_v = w_out.rearrange("l (k p) n -> l p k n", p=P)[0]
        xp_v = x_prompt.rearrange("b (t p) n -> (b p) t n", p=P)
        xs_v = x_sample.rearrange("b s n -> (b s) n")
        ssm_v = state_ssm.rearrange("l b h d e -> l d h b e")[0]
        ssm_out_v = new_ssm_sample.rearrange("l b h d e -> l d h b e")[0]

        block = ctx.enter_context(nc.Block())

        @block.sync
        def _(sp):
            sp.dma_start(x_small[0:NS, :], xs_v).then_inc(s_xin[0], 16)
            sp.dma_start(x_small[NS:C0, :], meta_tokens).then_inc(s_xin[0], 16)
            sp.dma_start(x_big[:, 0:2, :], xp_v[:, 0:2, :]).then_inc(s_xin[1], 16)
            sp.dma_start(x_big[:, 2:8, :], xp_v[:, 2:8, :]).then_inc(s_xin[2], 16)

            def load(n):
                if n >= 2:
                    sp.wait_ge(w_low, n - 1)
                if n < N_IN:
                    c = IN_TILES[n][2]
                    src = w_in_v[:, :, c:c + P]
                elif n < N_MIX:
                    src = w_out_v[:, :, P * (n - N_IN):P * (n - N_IN + 1)]
                sp.dma_start(w_raw[n % 2][:, :, :], src).then_inc(w_load[n % 2], 16)

            def send_last(n):
                kind, i, _ = IN_TILES[n]
                m = last_index(n)
                sp.wait_ge(last_kept, m + 1)
                if kind == "H":
                    sp.dma_start(new_a_sample.rearrange("l b r c -> (l b r) c")[:, P * i:P * i + P],
                                 last_out[m % 2][0:16, :]).then_inc(last_sent[m % 2], 16)
                    sp.dma_start(new_a_prompt.rearrange("l b r c -> (l b r) c")[:, P * i:P * i + P],
                                 last_out[m % 2][16:18, :]).then_inc(last_sent[m % 2], 16)
                else:
                    c = {"q": 0, "k": NH * P, "v": 2 * NH * P}[kind] + P * i
                    sp.dma_start(new_qkv_sample.rearrange("l b r c -> (l b r) c")[:, c:c + P],
                                 last_out[m % 2][0:24, :]).then_inc(last_sent[m % 2], 16)
                    sp.dma_start(new_qkv_prompt.rearrange("l b r c -> (l b r) c")[:, c:c + P],
                                 last_out[m % 2][24:27, :]).then_inc(last_sent[m % 2], 16)

            def slice_x(f):
                if f == 0:
                    sp.wait_ge(yb_low_s, NT)
                else:
                    sp.wait_ge(x_slice_t, 3 * f)
                cols = slice(P * f, P * f + P)
                sp.dma_start(xs[0:NS, 0, :], xs_v[:, cols]).then_inc(x_slice, 16)
                sp.dma_start(xs[NS:C0, 0, :], meta_tokens[:, cols]).then_inc(x_slice, 16)
                sp.dma_start(xs[:, 1:NT, :], xp_v[:, :, cols]).then_inc(x_slice, 16)

            for n in range(N_IN):
                load(n)
                if n >= 4 and has_last(n - 4):
                    send_last(n - 4)
            sp.wait_ge(acc_done, 3 * N_IN)
            sp.dma_start(cg[:, :], c_gdn).then_inc(s_gdn, 16)
            for h in range(NH):
                sp.dma_start(SSs[:, h, :, :], ssm_v[:, h, :, :]).then_inc(s_states, 16)
            for n in range(N_IN - 4, N_IN):
                if has_last(n):
                    send_last(n)
            for h in range(NH):
                sp.wait_ge(ss_kept, 2 * (h + 1))
                sp.dma_start(ssm_out_v[:, h, :, :], SSs[:, h, :, :]).then_inc(out_sent, 16)
            sp.wait_ge(out_sent, 16 * NH)
            for n in range(N_IN, N_MIX):
                if n == N_IN + 3:
                    sp.wait_ge(s_kept, NT)
                    sp.dma_start(new_ssm_prompt.rearrange("l b h d e -> d (l b h) e"),
                                 S[:, :].rearrange("p (h e) -> p h e", h=NH)).then_inc(out_sent, 16)
                if n >= N_IN + 3:
                    slice_x(n - N_IN - 3)
                load(n)
            for f in range(N_MIX - N_IN - 3, N_OUT):
                slice_x(f)

            with sp.Fori(0, FG) as g:
                for i in range(2 * KT):
                    n = N_MIX + i
                    sp.wait_ge(w_low, g * (2 * KT) + (n - 1))
                    if i < KT:
                        src = w_up_v[:, :, bass.ds(g * D + P * i, P)]
                    else:
                        src = w_down_v[:, bass.ds(g * KT, KT), P * (i - KT):P * (i - KT) + P]
                    sp.dma_start(w_raw[n % 2][:, :, :], src).then_inc(w_load[n % 2], 16)
            sp.wait_ge(acc_done, 3 * (N_MIX + 2 * KT * FG - KT))
            sp.dma_start(nfin[:, :], norm_final.rearrange("(a n) -> a n", a=1).to_broadcast([P, D])).then_inc(fin_const, 16)
            for t in range(NT):
                sp.wait_ge(fin_y, t + 1)
                if t == 0:
                    sp.dma_start(y_sample.rearrange("b s n -> (b s) n"), yt[0][0:NS, :]).then_inc(fin_sent[0], 16)
                else:
                    sp.dma_start(y_prompt[0, P * (t - 1):P * t, :], yt[t % 3][:, :]).then_inc(fin_sent[t % 3], 16)
            for i in range(3):
                sp.wait_ge(fin_sent[i], 16 * len(range(i, NT, 3)))
            sp.wait_ge(out_sent, 16 * (NH + 1))
            for i in range(2):
                sp.wait_ge(last_sent[i], 32 * len(range(i, N_LAST, 2)))

        @block.gpsimd
        def _(pool):
            pool.memset(one[:, :], 1.0).then_inc(set_ones, 1)
            pool.memset(mhalf[:, :], -0.5).then_inc(set_ones, 1)
            pool.memset(ab[:, :, :], 0.0).then_inc(set_ones, 1)
            pool.wait_ge(set_ones, 3)
            for t in range(NT):
                pool.wait_ge(x_ms, t + 1)
                pool.tensor_tensor(rx[0:rows(t), t:t + 1], ssx[0:rows(t), t:t + 1], mhalf[0:rows(t), :],
                                   ALU.pow).then_inc(x_pow, 1)
            pool.wait_ge(ab_hi, 1)
            pool.tensor_tensor(ab_w[:, :, 8:16], ab_raw[:, :, :], ab_w[:, :, 0:8].bitcast(F32),
                               ALU.subtract).then_inc(ab_lo, 1)

            def split_low(n, g=0):
                pool.wait_ge(w_high, g * (2 * KT) + (n + 1))
                if n >= 2:
                    pool.wait_ge(acc_done, g * (6 * KT) + 3 * (n - 1))
                pool.tensor_tensor(w_l[n % 2][:, :, :], w_raw[n % 2][:, :, :], w_h[n % 2][:, :, :].bitcast(F32),
                                   ALU.subtract).then_inc(w_low, 1)

            split_low(0)
            for n in range(N_IN):
                kind, i, _ = IN_TILES[n]
                if kind in ("k", "q", "v"):
                    f = {"q": 0, "k": NH, "v": 2 * NH}[kind] + i
                    if n == 0:
                        pool.wait_ge(x_turned, 24)
                        pool.wait_ge(rows_kept, 3)
                    elif n == 1:
                        pool.wait_ge(ab_turned, 1)
                    else:
                        pool.wait_ge(conv_done, n - 1)
                    zb = z[n % 2]
                    pool.tensor_copy(zb[:, 0:56].rearrange("p (b r) -> p b r", r=7)[:, :, 0:3],
                                     tq[:, f, 0:24].rearrange("p (b r) -> p b r", r=3))
                    pool.memset(zb[:, 56:59], 0.0).then_inc(z_hist, 1)
                if n == 3 * NH:
                    pool.wait_ge(x_low, 3 * KT)
                    pool.memset(pick[:, :].bitcast(F32), 0.0).then_inc(pick_set, 1)
                    pool.wait_ge(pick_set, 1)
                    pool.memset(pick[:, NROW:NROW + 1].bitcast(F32), 1.0).then_inc(pick_set, 1)
                if kind == "H":
                    if i:
                        pool.wait_ge(ya_low_s, i)
                    else:
                        pool.wait_ge(conv_done, 3 * NH)
                    pool.tensor_copy(z[1][:, 0:48].rearrange("p (b r) -> p b r", r=6)[:, :, 0:2],
                                     ta[:, i, 0:16].rearrange("p (b r) -> p b r", r=2))
                    pool.memset(z[1][:, 48:50], 0.0).then_inc(z_hist, 1)
                if n + 1 < N_IN:
                    split_low(n + 1)
                if has_last(n):
                    m = last_index(n)
                    if m >= 2:
                        pool.wait_ge(last_turned, m - 1)
                    if kind == "H":
                        pool.wait_ge(acc_read_dve, dve_reads_to(n) + 3)
                        pool.tensor_copy(last_in[m % 2][:, 0:16].rearrange("p (b r) -> p b r", r=2),
                                         z[1][:, 0:48].rearrange("p (b r) -> p b r", r=6)[:, :, 4:6])
                        pool.tensor_copy(last_in[m % 2][:, 16:18], z[1][:, 50 + PRM - 2:50 + PRM]).then_inc(last_cols, 1)
                    else:
                        pool.wait_ge(acc_read_act, 3 * n + 3)
                        pool.tensor_copy(last_in[m % 2][:, 0:24].rearrange("p (b r) -> p b r", r=3),
                                         z[n % 2][:, 0:56].rearrange("p (b r) -> p b r", r=7)[:, :, 4:7])
                        pool.tensor_copy(last_in[m % 2][:, 24:27], z[n % 2][:, 59 + PRM - 3:59 + PRM]).then_inc(last_cols, 1)

            def decay_mask(t):
                c, st = rows(t), gd[cset(t)]
                pool.wait_ge(d_exp, t + 1)
                m = upper_s if t == 0 else upper
                d = heads(st["wn"], c).rearrange("p (h i) -> p h i", h=NH)
                pool.tensor_tensor(d, d, over_heads(m[0:c, 0:c], c, c), ALU.mult).then_inc(d_mask, 1)

            def first_level(t):
                c, st, tb = rows(t), gd[cset(t)], tmpb[parity(t)]
                pool.wait_ge(kk_kept, t + 1)
                if t >= 5:
                    pool.wait_ge(v_made, t - 4)
                y = heads(st["Y"], c).rearrange("p (h i) -> p h i", h=NH)
                pool.tensor_tensor(y, heads(tb["At"], c).rearrange("p (h i) -> p h i", h=NH),
                                   over_heads(m0[0:c, 0:c], c, c), ALU.mult).then_inc(pool_step, 1)
                pool.wait_ge(pool_step, pst(t))
                pool.tensor_tensor(y, over_heads(eye[0:c, 0:c], c, c), y, ALU.subtract).then_inc(y_first, 1)

            def pst(t):
                return t + 1

            def zero_pairs(t, k):
                c, par = rows(t), parity(t)
                at_level = level_at(t, k)
                if at_level >= 3:
                    pool.wait_ge(xy_made[par], at_level - 2)
                pool.memset(heads(pb[par][at_level % 2], c), 0.0).then_inc(pair_zero[par], 1)

            def power(t):
                c = rows(t)
                pool.wait_ge(o_ms, t + 1)
                pool.tensor_tensor(sc["fo"][0:c, t, :], sc["tmp"][0:c, t, :], mhalf[0:c, :].to_broadcast([c, NH]),
                                   ALU.pow).then_inc(o_pow, 1)

            pool.wait_ge(acc_done, 3 * N_IN)
            pool.wait_ge(s_gdn, 16)
            def decay_states(h):
                pool.wait_ge(ss_made, 1)
                pool.tensor_tensor(SSs[:, h, :, :], SSs[:, h, :, :], eg_seq[:, :, h:h + 1].to_broadcast([P, NSEQ, P]),
                                   ALU.mult).then_inc(ss_decayed, 1)

            for n, pr in enumerate(pairs):
                first_tiles = (0, *pr) if n == 0 else pr
                for t in first_tiles:
                    decay_mask(t)
                for t in first_tiles:
                    zero_pairs(t, 1)
                    zero_pairs(t, 2)
                    first_level(t)
                if n == 0:
                    pool.tensor_copy(wq[:, :, :, LSEQ:2 * LSEQ], qf[:, :, 0:NS].rearrange("p h (b r) -> p h b r", r=LSEQ))
                    pool.memset(wsT[:, :, NS:C0], 0.0)
                    pool.memset(qsT[:, :, NS:C0], 0.0).then_inc(q_beside, 1)
                for k in range(1, LEVELS):
                    if n and k == 3:
                        power(pairs[n - 1][0])
                    if n and k == 5:
                        power(pairs[n - 1][1])
                    for t in first_tiles:
                        if k + 2 < (SMALL_LEVELS if t == 0 else LEVELS):
                            zero_pairs(t, k + 2)
                if n == 2:
                    split_low(N_IN)
                if n == 0:
                    decay_states(0)
                    decay_states(1)
                    power(0)
                    decay_states(2)
                    decay_states(3)
            for t in pairs[-1]:
                power(t)

            for n in range(N_IN + 1, N_MIX + 1):
                split_low(n)
            with pool.Fori(0, FG - 1) as g:
                for i in range(2 * KT):
                    split_low(N_MIX + 1 + i, g)
            for i in range(2 * KT - 1):
                split_low(N_MIX + 1 + i, FG - 1)
            for t in range(NT):
                c = rows(t)
                pool.wait_ge(fin_ms, t + 1)
                pool.tensor_tensor(rx[0:c, t:t + 1], ssx[0:c, t:t + 1], mhalf[0:c, :], ALU.pow).then_inc(fin_pow, 1)

        @block.scalar
        def _(act):
            act.dma_start(cm[:, :], c_main).then_inc(s_const, 16)
            act.dma_start(rows_n[0:8, :], norm_mix.rearrange("l (k p) -> (l k) p", p=P)).then_inc(s_row, 16)
            act.dma_start(rows_n[8:16, :], norm_ffn.rearrange("l (k p) -> (l k) p", p=P)).then_inc(s_row, 16)
            act.dma_start(ab_raw[:, :, :], w_in_v[:, :, O_A:O_A + 8]).then_inc(s_row, 16)
            act.dma_start(rows_q[0:24, :], state_conv_qkv.rearrange("l b r c -> (l b r) c")).then_inc(s_row, 16)
            act.dma_start(rows_q[24:28, :], conv_qkv_w[0]).then_inc(s_row, 16)
            act.dma_start(rows_a[0:16, :], state_conv_a.rearrange("l b r c -> (l b r) c")).then_inc(s_row, 16)
            act.dma_start(rows_a[16:19, :], conv_a_w[0]).then_inc(s_row, 16)
            act.dma_start(gn[:, :], gdn_norm.rearrange("l (p a) -> (l p) a", a=1)).then_inc(s_row, 16)
            act.dma_start(al[:, :], a_log.to_broadcast([P, NH])).then_inc(s_row, 16)
            act.dma_start(dtb[:, :], dt_bias.to_broadcast([P, NH])).then_inc(s_row, 16)
            for t in range(NT):
                x_arrived(act, t)
                if t:
                    act.wait_ge(x_sq, t)
                act.activation(square_out[0:rows(t), :], x_tile(t), ACT.Square,
                               accum_out=ssx[0:rows(t), t:t + 1]).then_inc(x_sq, 1)
            act.wait_ge(s_row, 160)
            act.activation(ab_w[:, :, 0:8], ab_raw[:, :, :], ACT.Copy).then_inc(ab_hi, 1)

            def split_high(n, g=0):
                act.wait_ge(w_load[n % 2], g * (16 * KT) + 16 * (n // 2 + 1))
                if n >= 2:
                    act.wait_ge(acc_done, g * (6 * KT) + 3 * (n - 1))
                act.activation(w_h[n % 2][:, :, :], w_raw[n % 2][:, :, :], ACT.Copy).then_inc(w_high, 1)

            split_high(0)
            act.wait_ge(rows_kept, 1)
            for g, (c0, w) in enumerate(GROUPS):
                for k in range(KT):
                    act.wait_ge(x_turned, KT * g + k + 1)
                    act.activation(xh[:, k, c0:c0 + w], ps[k][:, 0:w], ACT.Copy, scale=tn[:, k:k + 1]).then_inc(x_high, 1)
            for g, (c0, w) in enumerate(GROUPS):
                act.wait_ge(ab_made, g + 1)
                act.activation(abT[:, c0:c0 + w], ps[3 + g][0:16, 0:w], ACT.Copy).then_inc(ab_kept, 1)
            act.wait_ge(ab_tok, 2)
            act.activation(sc["tmp"][:, :, :], sc["eg"][:, :, :], ACT.Exp, scale=-1.0).then_inc(ab_act, 1)
            act.activation(sc["beta"][:, :, :], ab[:, :, NH:2 * NH], ACT.Exp, scale=-1.0).then_inc(ab_act, 1)
            act.activation(al[:, :], al[:, :], ACT.Exp).then_inc(ab_act, 1)
            act.wait_ge(ab_act, 3)
            act.activation(sc["tmp"][:, :, :], sc["tmp"][:, :, :], ACT.Ln, bias=one[:, 0:1]).then_inc(ab_act, 1)

            def silu(n):
                kind, i, _ = IN_TILES[n]
                dst = {"k": kf, "q": qf, "v": vf}[kind][:, i, :]
                act.wait_ge(conv_done, n + 1)
                act.activation(dst, dst, ACT.Silu).then_inc(silu_done, 1)

            def square_high(j):
                act.wait_ge(sq_full, j + 1)
                if j >= 2:
                    act.wait_ge(ss_done, j - 1)
                act.activation(sq_h[j % 2][:, :], sq[j % 2][:, :], ACT.Copy).then_inc(sq_high, 1)

            for n in range(N_IN):
                kind, i, _ = IN_TILES[n]
                if n + 1 < N_IN:
                    split_high(n + 1)
                if kind in ("k", "q", "v"):
                    zb = z[n % 2]
                    if n == 0:
                        act.wait_ge(x_turned, 24)
                    elif n == 1:
                        act.wait_ge(ab_turned, 1)
                    else:
                        act.wait_ge(conv_done, n - 1)
                        act.wait_ge(last_cols, n - 1)
                    for g, (c0, w) in enumerate(GROUPS):
                        act.wait_ge(acc_done, 3 * n + g + 1)
                        bank = ps[(n % 2) * 3 + g]
                        if g == 0:
                            act.activation(zb[:, 0:56].rearrange("p (b r) -> p b r", r=7)[:, :, 3:7],
                                           bank[:, 0:NS].rearrange("p (b r) -> p b r", r=LSEQ), ACT.Copy)
                            act.activation(zb[:, 59:59 + w - NS], bank[:, NS:w], ACT.Copy).then_inc(acc_read_act, 1)
                        else:
                            act.activation(zb[:, 59 + c0 - NS:59 + c0 - NS + w], bank[:, 0:w],
                                           ACT.Copy).then_inc(acc_read_act, 1)
                    if n:
                        silu(n - 1)
                if kind == "gate":
                    for g, (c0, w) in enumerate(GROUPS):
                        act.wait_ge(acc_done, 3 * n + g + 1)
                        if i == 0 and g == 0:
                            act.wait_ge(rows_kept, 3)
                            act.wait_ge(ab_made, 3)
                        act.activation(gate[:, i, c0:c0 + w], ps[(n % 2) * 3 + g][:, 0:w], ACT.Silu).then_inc(acc_read_act, 1)
                    if i == 0:
                        silu(n - 1)
                    square_high(2 * i)
                    square_high(2 * i + 1)
                if kind == "C":
                    if i == 0:
                        act.wait_ge(conv_done, 3 * NH)
                        act.wait_ge(last_cols, 3 * NH)
                    else:
                        act.wait_ge(acc_read_dve, dve_reads_to(n))
                    for g, (c0, w) in enumerate(GROUPS):
                        act.wait_ge(acc_done, 3 * n + g + 1)
                        act.activation(z[0][:, c0:c0 + w], ps[(n % 2) * 3 + g][:, 0:w], ACT.Copy).then_inc(acc_read_act, 1)
                if kind == "B":
                    for g, (c0, w) in enumerate(GROUPS):
                        act.wait_ge(acc_read_dve, dve_reads_to(n) + g + 1)
                        act.activation(ya_h[:, i, c0:c0 + w], z[1][:, c0:c0 + w], ACT.Copy).then_inc(ya_high_s, 1)
                if n == 1:
                    act.wait_ge(g_kept, 4)
                    act.activation(sc["eg"][:, :, :], sc["gneg"][:, :, :], ACT.Exp, scale=-1.0).then_inc(g_exp, 1)
                    act.activation(sc["egl"][:, :, :], sc["egl"][:, :, :], ACT.Exp).then_inc(g_exp, 1)
                    act.activation(sc["eglb"][:, :, :], sc["eglb"][:, :, :], ACT.Exp).then_inc(g_exp, 1)
                    act.activation(eg_seq[:, :, :], eg_seq[:, :, :], ACT.Exp).then_inc(g_exp, 1)
                if n == 4 * NH + 1:
                    act.wait_ge(norms_mid, 1)
                    act.activation(sc["nk"][:, :, :], sc["nk"][:, :, :], ACT.Sqrt).then_inc(norms_mid, 1)
                    act.activation(sc["rq_s"][:, :, :], sc["rq_s"][:, :, :], ACT.Sqrt).then_inc(norms_mid, 1)

            def decay_exp(t):
                c, st = rows(t), gd[cset(t)]
                act.wait_ge(g_diff, t + 1)
                act.activation(heads(st["wn"], c), heads(st["wn"], c), ACT.Exp).then_inc(d_exp, 1)

            def keep_x(t):
                c, tb = rows(t), tmpb[parity(t)]
                act.wait_ge(x_first_t, t + 1)
                act.activation(heads(tb["X"], c), ps[2 * parity(t)][0:c, 0:NH * c], ACT.Copy).then_inc(x_first, 1)

            def keep_w(t):
                c, st = rows(t), gd[cset(t)]
                act.wait_ge(w_made, t + 1)
                made = ps[2 * parity(t)][:, 0:NH * c]
                if t == 0:
                    made = made.rearrange("p (h i) -> p h i", h=NH)[:, :, 0:NS].rearrange("p h (b r) -> p h b r", r=LSEQ)
                act.activation(wq[:, :, :, 0:LSEQ] if t == 0 else st["wn"][:, :], made, ACT.Copy, scale=-1.0).then_inc(w_kept, 1)

            def o_square(t):
                c = rows(t)
                act.wait_ge(o_kept, t + 1)
                for h in range(NH):
                    ins = act.activation(t1[0:c, P * h:P * h + P], ob[0:c, P * h:P * h + P], ACT.Square,
                                         scale=sc["rq_s"][0:c, t, h:h + 1], accum_out=sc["sso"][0:c, t, h:h + 1])
                ins.then_inc(o_sq, 1)

            def yb_high(t):
                c0, c = tile_cols(t)
                act.wait_ge(yb_full_s, t + 1)
                act.activation(yb_h[:, :, c0:c0 + c], ybt[:, :, 0:c], ACT.Copy).then_inc(yb_high_s, 1)

            for n, pr in enumerate(pairs):
                first_tiles = (0, *pr) if n == 0 else pr
                for t in first_tiles:
                    decay_exp(t)
                for t in first_tiles:
                    keep_x(t)
                if n == 0:
                    keep_w(0)
                    o_square(0)
                    yb_high(0)
                else:
                    for t in pairs[n - 1]:
                        o_square(t)
                        yb_high(t)
                for t in pr:
                    keep_w(t)
                if n == 1:
                    split_high(N_IN)
            for t in pairs[-1]:
                o_square(t)
                yb_high(t)

            act.wait_ge(out_sent, 16 * (NH + 1))
            for f in range(N_OUT):
                n = N_IN + f
                split_high(n + 1)
                for g, (c0, w) in enumerate(GROUPS):
                    act.wait_ge(acc_read_dve, dve_reads_to(n) + g + 1)
                    act.activation(hg_h[:, f, c0:c0 + w], hT[:, f, c0:c0 + w], ACT.Copy,
                                   scale=tn[:, 8 + f:9 + f]).then_inc(hg_high_s, 1)

            act.wait_ge(rstd_mid, 3)
            act.activation(hsq[:, :], hsq[:, :], ACT.Sqrt).then_inc(rstd_b, 1)

            def up_high(g, i):
                for m, (c0, w) in enumerate(GROUPS):
                    act.wait_ge(u_full, g * (3 * KT) + 3 * i + m + 1)
                    if i == 0 and m == 0:
                        act.wait_ge(acc_done, g * (6 * KT) + 3 * N_MIX)
                    act.activation(u_h[:, i, c0:c0 + w], ut[(3 * i + m) % 2][:, 0:w], ACT.Copy).then_inc(u_high_s, 1)

            with act.Fori(0, FG - 1) as g:
                for i in range(KT):
                    split_high(N_MIX + 1 + i, g)
                    up_high(g, i)
                for i in range(KT):
                    split_high(N_MIX + KT + 1 + i, g)
            for i in range(KT):
                split_high(N_MIX + 1 + i, FG - 1)
                up_high(FG - 1, i)
            for i in range(KT - 1):
                split_high(N_MIX + KT + 1 + i, FG - 1)
            for t in range(NT):
                c = rows(t)
                act.wait_ge(fin_turned, t + 1)
                if t == 0:
                    act.wait_ge(acc_done, 3 * (N_MIX + 2 * KT * FG))
                if t >= 3:
                    act.wait_ge(fin_sent[t % 3], 16 * (t // 3))
                for half in range(2):
                    ins = act.activation(yt[t % 3][0:c, 512 * half:512 * half + 512], ps[4 * (t % 2) + half][0:c, :],
                                         ACT.Square, accum_out=sc["sso"][0:c, t, half:half + 1])
                ins.then_inc(fin_sq, 1)

        @block.tensor
        def _(pe):
            pe.wait_ge(s_const, 16)
            pe.wait_ge(s_row, 160)
            pe.transpose(ps[0][:, 0:16], rows_n[:, :], eye[0:16, 0:16]).then_inc(rows_turned, 1)
            for f in range(QKVW // P):
                ins = pe.transpose(ps[1][:, 28 * f:28 * f + 28], rows_q[:, P * f:P * f + P], eye[0:28, 0:28])
            for f in range(CONV // P):
                ins = pe.transpose(ps[2][:, 19 * f:19 * f + 19], rows_a[:, P * f:P * f + P], eye[0:19, 0:19])
            ins.then_inc(rows_turned, 1)
            for g, (c0, w) in enumerate(GROUPS):
                for k in range(KT):
                    if g == 0 and k == 0:
                        pe.wait_ge(rows_kept, 3)
                    if g:
                        pe.wait_ge(x_low, KT * (g - 1) + k + 1)
                    for t in GTILES[g]:
                        o, c = tile_cols(t)
                        if k == 0:
                            pe.wait_ge(x_scaled, t + 1)
                        ins = pe.transpose(ps[k][:, o - c0:o - c0 + c], x_tile(t)[:, P * k:P * k + P], eye[0:c, 0:c])
                    ins.then_inc(x_turned, 1)
            pe.wait_ge(ab_lo, 1)
            for g, (c0, w) in enumerate(GROUPS):
                pe.wait_ge(x_low, KT * (g + 1))
                if g == 0:
                    pe.wait_ge(x_low, 2 * KT + 6)
                for k in range(KT):
                    pe.matmul(ps[3 + g][0:16, 0:w], ab_w[:, k, 0:16], xh[:, k, c0:c0 + w], start=(k == 0), stop=False)
                for k in range(KT):
                    ins = pe.matmul(ps[3 + g][0:16, 0:w], ab_w[:, k, 0:16], xl[:, k, c0:c0 + w], start=False,
                                    stop=(k == KT - 1))
                ins.then_inc(ab_made, 1)

            def dense(n, rhs, g0=0, order=range(KT), prepare=None):
                for g, (c0, w) in enumerate(GROUPS):
                    if g == 0:
                        pe.wait_ge(w_low, g0 * (2 * KT) + (n + 1))
                    if prepare:
                        prepare(g)
                    bank = ps[(n % 2) * 3 + g]
                    for m, k in enumerate(order):
                        hi, lo = rhs(k)
                        pe.matmul(bank[:, 0:w], w_h[n % 2][:, k, :], hi[:, c0:c0 + w], start=(m == 0), stop=False)
                        pe.matmul(bank[:, 0:w], w_h[n % 2][:, k, :], lo[:, c0:c0 + w], start=False, stop=False)
                        ins = pe.matmul(bank[:, 0:w], w_l[n % 2][:, k, :], hi[:, c0:c0 + w], start=False,
                                        stop=(m == KT - 1))
                    ins.then_inc(acc_done, 1)

            def turn_last(n):
                m = last_index(n)
                r = 18 if IN_TILES[n][0] == "H" else 27
                pe.wait_ge(last_cols, m + 1)
                if m:
                    pe.wait_ge(last_kept, m)
                pe.transpose(ps[6][0:r, 0:P], last_in[m % 2][:, 0:r], eye).then_inc(last_turned, 1)

            def sum_squares(j):
                pe.wait_ge(pick_set, 2)
                pe.wait_ge(sq_low, j + 1)
                for m, g in enumerate((1, 0, 2)):
                    c0, w = GROUPS[g]
                    row = 2 * NH * g + j
                    for part in (sq_h, sq_l):
                        ins = pe.matmul(ps[7][0:NROW, 0:w], pick[:, NROW - row:2 * NROW - row], part[j % 2][:, c0:c0 + w],
                                        start=(j == 0 and m == 0 and part is sq_h),
                                        stop=(j == 2 * NH - 1 and m == 2 and part is sq_l))
                ins.then_inc(ss_done, 1)

            def turn_squares():
                pe.wait_ge(ss_rows, 1)
                for t in range(NT):
                    o, c = tile_cols(t)
                    g = [t in x for x in GTILES].index(True)
                    o -= GROUPS[g][0]
                    ins = pe.transpose(ps[7][0:c, NROW * t:NROW * t + NROW], ssr[:, o:o + c], eye[0:NROW, 0:NROW])
                ins.then_inc(ss_turned, 1)

            for n in range(N_IN):
                def prepare(g, n=n):
                    if n >= 2:
                        acc_free(pe, n - 2, g)
                    elif n == 0:
                        pe.wait_ge(x_low, 3 * KT)
                    else:
                        pe.wait_ge(ab_kept, g + 1)
                dense(n, lambda k: (xh[:, k, :], xl[:, k, :]), prepare=prepare)
                if n == 0:
                    pe.wait_ge(ab_kept, 3)
                    for t in range(NT):
                        o, c = tile_cols(t)
                        ins = pe.matmul(ps[6][0:c, 8 * t:8 * t + 8], abT[:, o:o + c], fold_ab, start=True, stop=True)
                    ins.then_inc(ab_turned, 1)
                    pe.wait_ge(g_ready, 2)
                    big = sc["g"][:, 1:NT, :]
                    small_g = sc["g"][0:C0, 0, :]
                    pe.matmul(ps[7][:, 0:32], upper, big, start=True, stop=True)
                    pe.matmul(ps[7][0:C0, 32:36], upper_s, small_g, start=True, stop=True)
                    pe.matmul(ps[7][:, 64:96], one[:, 0:1].to_broadcast([P, P]), big, start=True, stop=True)
                    pe.matmul(ps[7][0:C0, 96:100], same_s, small_g, start=True, stop=True)
                    pe.matmul(ps[7][:, 128:160], one[0:C0, 0:1].to_broadcast([C0, P]), g_seq[0:C0, :, :],
                              start=True, stop=True).then_inc(g_summed, 1)
                if n and has_last(n - 1):
                    if n == 1:
                        pe.wait_ge(ab_tok, 1)
                    turn_last(n - 1)
                if IN_TILES[n][0] == "gate" and IN_TILES[n][1]:
                    sum_squares(2 * IN_TILES[n][1] - 2)
                    sum_squares(2 * IN_TILES[n][1] - 1)
                if n == 4 * NH:
                    sum_squares(2 * NH - 2)
                    sum_squares(2 * NH - 1)
                if n == 4 * NH + 1:
                    turn_squares()

            def turn_kv(t):
                o, c = tile_cols(t)
                b = ps[2 * parity(t)], ps[2 * parity(t) + 1]
                if t >= 3:
                    pe.wait_ge(w_kept, t - 1)
                for i, src in enumerate((kf, vf)):
                    for h in range(NH):
                        ins = pe.transpose(b[i][0:c, P * h:P * h + P], src[:, h, o:o + c], eye)
                ins.then_inc(kv_turned, 1)

            def decay_rows(t):
                c = rows(t)
                pe.wait_ge(kv_kept, t + 1)
                u = upper_s if t == 0 else upper
                for h in range(NH):
                    ins = pe.matmul(ps[2 * parity(t)][0:c, c * h:c * h + c],
                                    sc["g"][0:c, t, h:h + 1].to_broadcast([c, c]), u, start=True, stop=True)
                ins.then_inc(g_rows, 1)

            def products(t):
                o, c = tile_cols(t)
                pe.wait_ge(g_diff, t + 1)
                for i, rhs in enumerate((kf, qf)):
                    for h in range(NH):
                        ins = pe.matmul(ps[2 * parity(t) + i][0:c, c * h:c * h + c], kf[:, h, o:o + c],
                                        rhs[:, h, o:o + c], start=True, stop=True)
                ins.then_inc(kk_made, 1)

            def turn_y(t):
                c, st = rows(t), gd[cset(t)]
                pe.wait_ge(y_first, t + 1)
                for h in range(NH):
                    ins = pe.transpose(ps[2 * parity(t)][0:c, c * h:c * h + c], st["Y"][0:c, c * h:c * h + c],
                                       eye[0:c, 0:c])
                ins.then_inc(x_first_t, 1)

            def level_p(t, k):
                c, tb, par = rows(t), tmpb[parity(t)], parity(t)
                if k == 1:
                    pe.wait_ge(x_first, t + 1)
                else:
                    pe.wait_ge(xy_kept[par], level_at(t, k) - 1)
                for h in range(NH):
                    hs = slice(c * h, c * h + c)
                    ins = pe.matmul(ps[2 * par][0:c, hs], tb["At"][0:c, hs], tb["X"][0:c, hs], start=True, stop=True)
                ins.then_inc(p_made[par], 1)

            def level_xy(t, k):
                c, tb, st, par = rows(t), tmpb[parity(t)], gd[cset(t)], parity(t)
                at_level, last = level_at(t, k), k == (SMALL_LEVELS if t == 0 else LEVELS) - 1
                pk = pb[par][at_level % 2]
                pe.wait_ge(p_kept[par], at_level)
                for h in range(NH):
                    hs = slice(c * h, c * h + c)
                    if not last:
                        pe.matmul(ps[2 * par + 1][0:c, hs], st["Y"][0:c, hs], pk[0:c, hs], start=True, stop=False)
                    ins = pe.matmul(ps[2 * par + 1][0:c, hs], pk[0:c, hs], st["Y"][0:c, hs], start=last, stop=True)
                ins.then_inc(xy_made[par], 1)

            def make_w(t):
                c, st, tb = rows(t), gd[cset(t)], tmpb[parity(t)]
                pe.wait_ge(xy_kept[parity(t)], level_at(t, (SMALL_LEVELS if t == 0 else LEVELS) - 1))
                for h in range(NH):
                    ins = pe.matmul(ps[2 * parity(t)][:, c * h:c * h + c], tb["kg"][0:c, P * h:P * h + P],
                                    st["Y"][0:c, c * h:c * h + c], start=True, stop=True)
                ins.then_inc(w_made, 1)

            def use_state(t):
                o, c = tile_cols(t)
                st = gd[cset(t)]
                pe.wait_ge(w_kept, t + 1)
                pe.wait_ge(s_kept, t)
                pe.wait_ge(v_kept, t)
                pe.wait_ge(qs_kept, t)
                pe.wait_ge(yb_full_s, t - 1 + t % 2)
                if t == 1:
                    pe.wait_ge(ss_kept, 2 * NH)
                for h in range(NH):
                    hs = slice(P * h, P * h + P)
                    pe.matmul(ps[4][:, hs], st["Y"][:, hs], st["vn"][:, hs], start=True, stop=False)
                    pe.matmul(ps[4][:, hs], st["wn"][:, hs], S[:, hs], start=False, stop=True)
                for h in range(NH):
                    hs = slice(P * h, P * h + P)
                    ins = pe.matmul(ps[5][:, hs], qf[:, h, o:o + c], S[:, hs], start=True, stop=True)
                ins.then_inc(v_made, 1)

            def next_state(t):
                c, st = rows(t), gd[cset(t)]
                pe.wait_ge(v_kept, t + 1)
                pe.wait_ge(o_kept, t)
                for h in range(NH):
                    hs = slice(P * h, P * h + P)
                    pe.matmul(ps[7][:, hs], st["kd"][0:c, hs], vnew[0:c, hs],
                              start=True, stop=True)
                for h in range(NH):
                    ins = pe.matmul(ps[6][0:c, P * h:P * h + P], st["qk"][0:c, c * h:c * h + c],
                                    vnew[0:c, P * h:P * h + P], start=True, stop=True)
                ins.then_inc(os_made, 1)

            def turn_o(t):
                c = rows(t)
                pe.wait_ge(o_normed, t + 1)
                if t:
                    pe.wait_ge(qs_kept, t + 1 + (t % 2))
                    pe.wait_ge(yb_full_s, t)
                else:
                    pe.wait_ge(ss_kept, 2)
                for h in range(NH):
                    ins = pe.transpose(ps[5 if t else 4][:, c * h:c * h + c], ob[0:c, P * h:P * h + P], eye[0:c, 0:c])
                ins.then_inc(o_turned, 1)

            def chain_step(k, a, b):
                if k == 1:
                    use_state(a)
                if k == 2:
                    next_state(a)
                if k == 3:
                    use_state(b)
                if k == 4:
                    turn_o(a)
                    next_state(b)
                if k == 6:
                    turn_o(b)

            def sample_states(h):
                pe.wait_ge(vm_made, h + 1)
                if h == 2:
                    pe.wait_ge(yb_full_s, 1)
                if h == 3:
                    pe.wait_ge(ss_kept, 4)
                for half in range(2):
                    ins = pe.matmul(ps[4 + 2 * (h % 2) + half][:, :], gd[4]["kd"][0:C0, P * h:P * h + P],
                                    vm[h % 2][:, 4 * half:4 * half + 4, :], start=True, stop=True)
                ins.then_inc(ss_made, 1)

            def tile0_step(m):
                st = gd[4]
                if m == 0:
                    make_w(0)
                if m in (1, 2):
                    if m == 1:
                        pe.wait_ge(s_states, 16 * NH)
                        pe.wait_ge(w_kept, 1)
                        pe.wait_ge(q_beside, 1)
                    for h in (2 * m - 2, 2 * m - 1):
                        for b in range(NSEQ):
                            o = 2 * LSEQ * (NSEQ * h + b)
                            ins = pe.matmul(ps[6][:, o:o + 2 * LSEQ], SSs[:, h, b, :], wq[:, h, b, :], start=True,
                                            stop=True)
                    if m == 2:
                        ins.then_inc(ss_made, 1)
                if m == 3:
                    pe.wait_ge(ws_kept, 2)
                    for h in range(NH):
                        hs, cs = slice(P * h, P * h + P), slice(C0 * h, C0 * h + C0)
                        pe.matmul(ps[4][0:C0, hs], st["Y"][0:C0, cs], st["vn"][0:C0, hs], start=True, stop=False)
                        pe.matmul(ps[4][0:C0, hs], wsT[:, h, :], eye, start=False, stop=True)
                    for h in range(NH):
                        ins = pe.matmul(ps[5][0:C0, P * h:P * h + P], qsT[:, h, :], eye, start=True, stop=True)
                    ins.then_inc(ss_made, 1)
                if m == 4:
                    sample_states(0)
                    for h in range(NH):
                        hs, cs = slice(P * h, P * h + P), slice(C0 * h, C0 * h + C0)
                        pe.matmul(ps[7][:, hs], st["kd"][0:C0, hs], v_meta[0:C0, hs], start=True, stop=True)
                        ins = pe.matmul(ps[6][0:C0, hs], st["qk"][0:C0, cs], vnew[0:C0, hs], start=True, stop=True)
                    ins.then_inc(os_made, 1)
                if m == 5:
                    pe.wait_ge(s_kept, 1)
                    pe.wait_ge(o_kept, 1)
                    sample_states(1)
                    turn_o(0)

            pe.wait_ge(norms_done, 1)
            acc_free(pe, N_IN - 1, 2)
            for n, pr in enumerate(pairs):
                first_tiles = (0, *pr) if n == 0 else pr
                for step in (turn_kv, decay_rows, products, turn_y):
                    for t in first_tiles:
                        step(t)
                    if n == 1 and step in (turn_kv, decay_rows):
                        sample_states(2 if step == turn_kv else 3)
                for k in range(1, LEVELS):
                    now = first_tiles if k < SMALL_LEVELS else pr
                    for t in now:
                        level_p(t, k)
                    if n:
                        chain_step(k, *pairs[n - 1])
                    elif k >= SMALL_LEVELS:
                        tile0_step(2 * (k - SMALL_LEVELS))
                    for t in now:
                        level_xy(t, k)
                    if n == 0 and k >= SMALL_LEVELS:
                        tile0_step(2 * (k - SMALL_LEVELS) + 1)
                for t in pr:
                    make_w(t)
            for k in range(1, LEVELS):
                chain_step(k, *pairs[-1])

            for f in range(N_OUT):
                n = N_IN + f

                def prepare(g, f=f, n=n):
                    m = 3 * f + g
                    pe.wait_ge(x_slice, 48 * (f + 1))
                    if m >= 2:
                        pe.wait_ge(h_sq, m - 1)
                    if m == 1:
                        pe.wait_ge(s_kept, NT)
                    for t in GTILES[g]:
                        o, c = tile_cols(t)
                        ins = pe.transpose(ps[6 + m % 2][:, o - GROUPS[g][0]:o - GROUPS[g][0] + c], xs[0:c, t, :],
                                           eye[0:c, 0:c])
                    ins.then_inc(x_slice_t, 1)
                    if f >= 2:
                        acc_free(pe, n - 2, g)

                if f == 0:
                    pe.wait_ge(yb_low_s, NT)
                    pe.wait_ge(ya_low_s, NH)
                dense(n, lambda k: (ya_h[:, k, :], ya_l[:, k, :]) if k < NH else (yb_h[:, k - NH, :], yb_l[:, k - NH, :]),
                      prepare=prepare)
            pe.wait_ge(h_sq, 3 * N_OUT)
            for g, (c0, w) in enumerate(GROUPS):
                if g == 0:
                    pe.wait_ge(x_slice_kept, 3 * N_OUT)
                if g == 2:
                    pe.wait_ge(rstd_mid, 1)
                pe.matmul(ps[6 + g % 2][:, 0:w], one[:, 0:1].to_broadcast([P, P]), hsq[:, c0:c0 + w], start=True,
                          stop=True).then_inc(h_sum, 1)

            def up(g, i):
                n = N_MIX + i

                def prepare(m):
                    pe.wait_ge(acc_read_dve, g * (6 * KT) + dve_reads_to(n - 2) + m + 1)
                    if i == 0:
                        pe.wait_ge(hg_low_s, 3 * N_OUT)
                dense(n, lambda k: (hg_h[:, k, :], hg_l[:, k, :]), g0=g, prepare=prepare)

            def down(g, i):
                n = N_MIX + KT + i

                def prepare(m):
                    pe.wait_ge(acc_read_dve, g * (6 * KT) + dve_reads_to(n - 2) + m + 1)
                    if i == 0:
                        pe.wait_ge(u_low_s, g * (3 * KT) + 3 * (KT - 1) + m + 1)
                dense(n, lambda k: (u_h[:, k, :], u_l[:, k, :]), g0=g, prepare=prepare)

            with pe.Fori(0, FG) as g:
                for i in range(KT):
                    up(g, i)
                for i in range(KT):
                    down(g, i)
            for t in range(NT):
                o, c = tile_cols(t)
                if t == 0:
                    pe.wait_ge(acc_read_dve, dve_reads_to(N_MIX + 2 * KT * FG))
                if t >= 2:
                    pe.wait_ge(fin_y, t - 1)
                for k in range(KT):
                    ins = pe.transpose(ps[4 * (t % 2) + k // 4][0:c, P * (k % 4):P * (k % 4) + P], hT[:, k, o:o + c], eye)
                ins.then_inc(fin_turned, 1)

        @block.vector
        def _(dve):
            steps = [0]

            def link(ins):
                steps[0] += 1
                ins.then_inc(dve_step, 1)
                dve.wait_ge(dve_step, steps[0])

            for t in range(NT):
                dve.wait_ge(x_sq, t + 1)
                dve.tensor_scalar(ssx[0:rows(t), t:t + 1], ssx[0:rows(t), t:t + 1], 1.0 / D, EPS, ALU.mult,
                                  ALU.add).then_inc(x_ms, 1)
                if t == 0:
                    dve.wait_ge(rows_turned, 2)
                    dve.tensor_copy(tn[:, :], ps[0][:, 0:16]).then_inc(rows_kept, 1)
                    dve.tensor_copy(tq[:, :, :], ps[1][:, 0:336].rearrange("p (f r) -> p f r", r=28)).then_inc(rows_kept, 1)
                    dve.tensor_copy(ta[:, :, :], ps[2][:, 0:76].rearrange("p (f r) -> p f r", r=19)).then_inc(rows_kept, 1)
                if t:
                    dve.wait_ge(x_pow, t)
                    dve.tensor_scalar(x_tile(t - 1), x_tile(t - 1), rx[0:rows(t - 1), t - 1:t], None,
                                      ALU.mult).then_inc(x_scaled, 1)
            dve.wait_ge(x_pow, NT)
            dve.tensor_scalar(x_tile(NT - 1), x_tile(NT - 1), rx[:, NT - 1:NT], None, ALU.mult).then_inc(x_scaled, 1)
            for g, (c0, w) in enumerate(GROUPS):
                for k in range(KT):
                    dve.wait_ge(x_high, KT * g + k + 1)
                    dve.scalar_tensor_tensor(out=xl[:, k, c0:c0 + w], in0=ps[k][:, 0:w], scalar=tn[:, k:k + 1],
                                             in1=xh[:, k, c0:c0 + w].bitcast(F32), op0=ALU.mult,
                                             op1=ALU.subtract).then_inc(x_low, 1)
            dve.wait_ge(ab_turned, 1)
            dve.wait_ge(set_ones, 3)
            dve.tensor_copy(ab[0:C0, 0, :], ps[6][0:C0, 0:8])
            dve.tensor_copy(ab[:, 1:NT, :], ps[6][:, 8:8 * NT].rearrange("p (t j) -> p t j", j=8)).then_inc(ab_tok, 1)
            dve.wait_ge(ab_tok, 1)
            link(dve.tensor_tensor(sc["g"][:, :, :], ab[:, :, 0:NH], dtb[:, :].unsqueeze(1).to_broadcast([P, NT, NH]), ALU.add))
            link(dve.tensor_scalar(sc["eg"][:, :, :], sc["g"][:, :, :], -1.0, None, ALU.mult))
            dve.tensor_tensor(sc["eg"][:, :, :], sc["eg"][:, :, :], sc["g"][:, :, :], ALU.max).then_inc(ab_tok, 1)
            dve.wait_ge(ab_act, 4)
            link(dve.tensor_scalar(sc["g"][:, :, :], sc["g"][:, :, :], 0.0, None, ALU.max))
            link(dve.tensor_tensor(sc["g"][:, :, :], sc["g"][:, :, :], sc["tmp"][:, :, :], ALU.add))
            link(dve.tensor_tensor(sc["g"][:, :, :], sc["g"][:, :, :], al[:, :].unsqueeze(1).to_broadcast([P, NT, NH]), ALU.mult))
            link(dve.tensor_scalar(sc["g"][:, :, :], sc["g"][:, :, :], -1.0, None, ALU.mult))
            link(dve.tensor_scalar(sc["beta"][:, :, :], sc["beta"][:, :, :], 1.0, None, ALU.add))
            dve.reciprocal(sc["beta"][:, :, :], sc["beta"][:, :, :]).then_inc(g_ready, 1)
            dve.tensor_tensor(g_seq[0:C0, :, :], sc["g"][0:C0, 0, :].unsqueeze(1).to_broadcast([C0, NSEQ, NH]),
                              same_s[:, 0:NS:LSEQ].unsqueeze(2).to_broadcast([C0, NSEQ, NH]), ALU.mult).then_inc(g_ready, 1)

            def conv(zr, r, samp_w, pre, wt, taps, dst):
                zs = zr[:, 0:NSEQ * samp_w].rearrange("p (b r) -> p b r", r=samp_w)
                ds = dst[:, 0:NS].rearrange("p (b r) -> p b r", r=LSEQ)
                for j in range(taps):
                    w = wt[:, j:j + 1]
                    main = zr[:, pre + j:pre + j + PRM]
                    if j == 0:
                        dve.tensor_scalar(dst[:, NS:TOK], main, w, None, ALU.mult)
                        link(dve.tensor_scalar(ds, zs[:, :, j:j + LSEQ], w, None, ALU.mult))
                    else:
                        dve.scalar_tensor_tensor(out=dst[:, NS:TOK], in0=main, scalar=w, in1=dst[:, NS:TOK],
                                                 op0=ALU.mult, op1=ALU.add)
                        ins = dve.scalar_tensor_tensor(out=ds, in0=zs[:, :, j:j + LSEQ], scalar=w, in1=ds,
                                                       op0=ALU.mult, op1=ALU.add)
                        if j < taps - 1:
                            link(ins)
                return ins

            def keep_last(m, r):
                dve.wait_ge(last_turned, m + 1)
                if m >= 2:
                    dve.wait_ge(last_sent[m % 2], 32 * (m // 2))
                dve.tensor_copy(last_out[m % 2][0:r, :], ps[6][0:r, 0:P]).then_inc(last_kept, 1)

            nk, rk, c_, p_ = sc["nk"], sc["rk"], sc["c"], sc["p"]

            def square(j):
                src = (kf if j < NH else qf)[:, j % NH, :]
                dve.wait_ge(silu_done, j + 1)
                if j >= 2:
                    dve.wait_ge(sq_low, j - 1)
                dve.tensor_tensor(sq[j % 2][:, :], src, src, ALU.mult).then_inc(sq_full, 1)

            def square_low(j):
                dve.wait_ge(sq_high, j + 1)
                if j >= 2:
                    dve.wait_ge(ss_done, j - 1)
                dve.tensor_tensor(sq_l[j % 2][:, :], sq[j % 2][:, :], sq_h[j % 2][:, :].bitcast(F32),
                                  ALU.subtract).then_inc(sq_low, 1)

            def keep_norms():
                dve.wait_ge(ss_turned, 1)
                for dst, j in ((nk, 0), (sc["rq_s"], NH)):
                    link(dve.memset(dst[:, 0, :], 1.0))
                    for g, ts in enumerate(GTILES):
                        turned = ps[7][:, 0:NROW * NT].rearrange("p (t r) -> p t r", r=NROW)
                        r0 = 2 * NH * g + j
                        if g == 0:
                            dve.tensor_scalar(dst[0:C0, 0, :], turned[0:C0, 0, r0:r0 + NH], EPS, None, ALU.add)
                            ts = ts[1:]
                        ins = dve.tensor_scalar(dst[:, ts[0]:ts[-1] + 1, :], turned[:, ts[0]:ts[-1] + 1, r0:r0 + NH],
                                                EPS, None, ALU.add)
                ins.then_inc(norms_mid, 1)

            def scale_norms():
                dve.wait_ge(norms_mid, 3)
                dve.wait_ge(g_exp, 4)
                dve.reciprocal(rk[:, :, :], nk[:, :, :])
                link(dve.reciprocal(sc["rq_s"][:, :, :], sc["rq_s"][:, :, :]))
                dve.tensor_scalar(sc["rq_s"][:, :, :], sc["rq_s"][:, :, :], float(P) ** -0.5, None, ALU.mult)
                dve.tensor_tensor(sc["kd_s"][:, :, :], rk[:, :, :], sc["egl"][:, :, :], ALU.mult)
                link(dve.tensor_tensor(c_[:, :, :], rk[:, :, :], sc["beta"][:, :, :], ALU.mult))
                dve.tensor_tensor(p_[:, :, :], c_[:, :, :], rk[:, :, :], ALU.mult).then_inc(norms_done, 1)

            for n in range(N_IN):
                kind, i, _ = IN_TILES[n]
                if kind == "gate":
                    for j in (2 * i, 2 * i + 1):
                        square(j)
                    for j in (2 * i, 2 * i + 1):
                        square_low(j)
                if n == 4 * NH:
                    dve.wait_ge(ss_done, 2 * NH)
                    dve.tensor_copy(ssr[:, :], ps[7][0:NROW, 0:3 * P]).then_inc(ss_rows, 1)
                if kind in ("k", "q", "v"):
                    f = {"q": 0, "k": NH, "v": 2 * NH}[kind] + i
                    dst = {"k": kf, "q": qf, "v": vf}[kind][:, i, :]
                    dve.wait_ge(acc_read_act, 3 * n + 3)
                    dve.wait_ge(z_hist, n + 1)
                    if n == 0:
                        dve.wait_ge(x_sq, NT)
                    conv(z[n % 2], 3, 7, 56, tq[:, f, 24:28], 4, dst).then_inc(conv_done, 1)
                if kind == "H":
                    bank = [ps[(n % 2) * 3 + g] for g in range(3)]
                    dve.wait_ge(z_hist, 3 * NH + i + 1)
                    for g, (c0, w) in enumerate(GROUPS):
                        dve.wait_ge(acc_done, 3 * n + g + 1)
                        dve.wait_ge(acc_read_act, 3 * sum(act_reads[:n]))
                        if i and g == 0:
                            dve.wait_ge(last_cols, 3 * NH + i)
                        if g == 0:
                            dve.tensor_tensor(z[1][:, 0:48].rearrange("p (b r) -> p b r", r=6)[:, :, 2:6],
                                              bank[0][:, 0:NS].rearrange("p (b r) -> p b r", r=LSEQ),
                                              z[0][:, 0:NS].rearrange("p (b r) -> p b r", r=LSEQ), ALU.mult)
                            dve.tensor_tensor(z[1][:, 50:50 + w - NS], bank[0][:, NS:w], z[0][:, NS:w],
                                              ALU.mult).then_inc(acc_read_dve, 1)
                        else:
                            ins = dve.tensor_tensor(z[1][:, 50 + c0 - NS:50 + c0 - NS + w], bank[g][:, 0:w],
                                                    z[0][:, c0:c0 + w], ALU.mult)
                            ins.then_inc(acc_read_dve, 1)
                    dve.wait_ge(acc_read_dve, dve_reads_to(n) + 3)
                    conv(z[1], 2, 6, 48, ta[:, i, 16:19], 3, z[0]).then_inc(conv_done, 1)
                if kind == "B":
                    dve.wait_ge(conv_done, 3 * NH + i + 1)
                    dve.wait_ge(last_cols, 3 * NH + i + 1)
                    for g, (c0, w) in enumerate(GROUPS):
                        dve.wait_ge(acc_done, 3 * n + g + 1)
                        dve.tensor_tensor(z[1][:, c0:c0 + w], ps[(n % 2) * 3 + g][:, 0:w], z[0][:, c0:c0 + w],
                                          ALU.mult).then_inc(acc_read_dve, 1)
                    dve.wait_ge(ya_high_s, 3 * i + 3)
                    dve.tensor_tensor(ya_l[:, i, :], z[1][:, 0:TOK], ya_h[:, i, :].bitcast(F32),
                                      ALU.subtract).then_inc(ya_low_s, 1)
                if n == 0:
                    dve.wait_ge(g_summed, 1)
                    dve.memset(sc["gneg"][:, 0, :], 0.0)
                    link(dve.memset(sc["egl"][:, 0, :], 0.0))
                    dve.memset(sc["eglb"][:, 0, :], 0.0)
                    g3 = lambda ap: ap.rearrange("p (t h) -> p t h", h=NH)
                    dve.tensor_scalar(sc["gneg"][:, 1:NT, :], g3(ps[7][:, 0:32]), -1.0, None, ALU.mult)
                    link(dve.tensor_scalar(sc["gneg"][0:C0, 0, :], ps[7][0:C0, 32:36], -1.0, None, ALU.mult))
                    dve.tensor_tensor(sc["egl"][:, 1:NT, :], g3(ps[7][:, 64:96]), sc["gneg"][:, 1:NT, :],
                                      ALU.add).then_inc(g_kept, 1)
                    dve.tensor_tensor(sc["egl"][0:C0, 0, :], ps[7][0:C0, 96:100], sc["gneg"][0:C0, 0, :],
                                      ALU.add).then_inc(g_kept, 1)
                    dve.tensor_copy(sc["eglb"][:, 1:NT, :], g3(ps[7][:, 64:96])).then_inc(g_kept, 1)
                    dve.tensor_copy(eg_seq[:, :, :], ps[7][:, 128:160].rearrange("p (b h) -> p b h", h=NH)).then_inc(g_kept, 1)
                if n == 4 * NH + 1:
                    keep_norms()
                if n == 4 * NH + 2:
                    scale_norms()
                if n and has_last(n - 1):
                    keep_last(last_index(n - 1), 18 if IN_TILES[n - 1][0] == "H" else 27)

            dve.wait_ge(norms_done, 1)

            h3 = lambda ap: ap.rearrange("p (h i) -> p h i", h=NH)

            def keep_kv(t):
                c, st, tb = rows(t), gd[cset(t)], tmpb[parity(t)]
                b0, b1 = ps[2 * parity(t)][0:c, :], ps[2 * parity(t) + 1][0:c, :]
                dve.wait_ge(kv_turned, t + 1)
                if t >= 3:
                    dve.wait_ge(w_made, t - 1)
                if t >= 5:
                    dve.wait_ge(os_made, t - 3)
                dve.tensor_tensor(h3(tb["kg"][0:c, :]), h3(b0), per_head(sc["eg"][0:c, t, :], c, P), ALU.mult)
                dve.tensor_tensor(h3(st["kd"][0:c, :]), h3(b0), per_head(sc["kd_s"][0:c, t, :], c, P), ALU.mult)
                dve.tensor_tensor(h3(st["vn"][0:c, :]), h3(b1), per_head(nk[0:c, t, :], c, P), ALU.mult).then_inc(kv_kept, 1)

            def decay_diff(t):
                c, st = rows(t), gd[cset(t)]
                dve.wait_ge(g_rows, t + 1)
                for h in range(NH):
                    ins = dve.tensor_scalar(st["wn"][0:c, c * h:c * h + c], ps[2 * parity(t)][0:c, c * h:c * h + c],
                                            sc["gneg"][0:c, t, h:h + 1], 0.0, ALU.add, ALU.min)
                ins.then_inc(g_diff, 1)

            def keep_products(t):
                c, st, tb = rows(t), gd[cset(t)], tmpb[parity(t)]
                dve.wait_ge(kk_made, t + 1)
                dve.wait_ge(d_mask, t + 1)
                for i, (dst, s) in enumerate(((tb["At"], p_), (st["qk"], rk))):
                    for h in range(NH):
                        cs = slice(c * h, c * h + c)
                        ins = dve.scalar_tensor_tensor(out=dst[0:c, cs], in0=ps[2 * parity(t) + i][0:c, cs],
                                                       scalar=s[0:c, t, h:h + 1], in1=st["wn"][0:c, cs], op0=ALU.mult,
                                                       op1=ALU.mult)
                ins.then_inc(kk_kept, 1)

            def keep_p(t, k):
                c, par, b = rows(t), parity(t), 2 ** k
                at_level = level_at(t, k)
                dve.wait_ge(p_made[par], at_level)
                dve.wait_ge(pair_zero[par], at_level)
                m = (lev_small if t == 0 else lev_big)[k][0:c, :]
                src = ps[2 * par][0:c, 0:NH * c].rearrange("p (h n two b) -> p h n two b", h=NH, two=2, b=b)[:, :, :, 0, :]
                dst = heads(pb[par][at_level % 2], c).rearrange("p (h n two b) -> p h n two b", h=NH, two=2, b=b)[:, :, :, 0, :]
                mask = m.rearrange("p (n b) -> p n b", b=b).unsqueeze(1).to_broadcast([c, NH, c // 2 // b, b])
                dve.tensor_tensor(dst, src, mask, ALU.mult).then_inc(p_kept[par], 1)

            def keep_xy(t, k):
                c, st, tb, par, b = rows(t), gd[cset(t)], tmpb[parity(t)], parity(t), 2 ** k
                at_level, last = level_at(t, k), k == (SMALL_LEVELS if t == 0 else LEVELS) - 1
                dve.wait_ge(xy_made[par], at_level)
                made = ps[2 * par + 1][0:c, 0:NH * c]
                if not last:
                    xf = first(heads(tb["X"], c), b)
                    dve.tensor_tensor(xf, xf, first(made, b), ALU.subtract)
                ys = second(heads(st["Y"], c), b)
                dve.tensor_tensor(ys, ys, second(made, b), ALU.subtract).then_inc(xy_kept[par], 1)

            def keep_v(t):
                c = rows(t)
                dve.wait_ge(v_made, t)
                dve.wait_ge(os_made, t)
                dve.tensor_tensor(h3(vnew[0:c, :]), h3(ps[4][0:c, :]), per_head(c_[0:c, t, :], c, P),
                                  ALU.mult).then_inc(v_kept, 1)
                if t:
                    dve.wait_ge(o_sq, t)
                dve.tensor_tensor(h3(t1[0:c, :]), h3(ps[5][0:c, :]), per_head(sc["eg"][0:c, t, :], c, P),
                                  ALU.mult).then_inc(qs_kept, 1)

            def keep_state(t):
                dve.wait_ge(os_made, t + 1)
                for h in range(NH):
                    hs = slice(P * h, P * h + P)
                    ins = dve.scalar_tensor_tensor(out=S[:, hs], in0=S[:, hs], scalar=sc["eglb"][:, t, h:h + 1],
                                                   in1=ps[7][:, hs], op0=ALU.mult, op1=ALU.add)
                ins.then_inc(s_kept, 1)

            def keep_o(t):
                c = rows(t)
                dve.wait_ge(qs_kept, t + 1)
                if t:
                    dve.wait_ge(o_turned, t)
                dve.tensor_tensor(ob[0:c, :], ps[6][0:c, :], t1[0:c, :], ALU.add).then_inc(o_kept, 1)

            def norm_o(t):
                c = rows(t)
                dve.wait_ge(o_sq, t + 1)
                dve.tensor_scalar(sc["tmp"][0:c, t, :], sc["sso"][0:c, t, :], 1.0 / P, EPS, ALU.mult,
                                  ALU.add).then_inc(o_ms, 1)
                dve.wait_ge(o_pow, t + 1)
                link(dve.tensor_tensor(sc["fo"][0:c, t, :], sc["fo"][0:c, t, :], sc["rq_s"][0:c, t, :], ALU.mult))
                dve.tensor_tensor(h3(ob[0:c, :]), h3(ob[0:c, :]), per_head(sc["fo"][0:c, t, :], c, P),
                                  ALU.mult).then_inc(o_normed, 1)

            def gate_o(t):
                o, c = tile_cols(t)
                dve.wait_ge(o_turned, t + 1)
                dve.scalar_tensor_tensor(out=ybt[:, :, 0:c], in0=h3(ps[5 if t else 4][:, 0:NH * c]), scalar=gn[:, 0:1],
                                         in1=gate[:, :, o:o + c], op0=ALU.mult, op1=ALU.mult).then_inc(yb_full_s, 1)
                dve.wait_ge(yb_high_s, t + 1)
                dve.tensor_tensor(yb_l[:, :, o:o + c], ybt[:, :, 0:c], yb_h[:, :, o:o + c].bitcast(F32),
                                  ALU.subtract).then_inc(yb_low_s, 1)

            def chain_step(k, a, b):
                if k == 1:
                    keep_v(a)
                if k == 2:
                    keep_state(a)
                    keep_o(a)
                if k == 3:
                    keep_v(b)
                    norm_o(a)
                if k == 4:
                    gate_o(a)
                    keep_state(b)
                    keep_o(b)
                if k == 5:
                    norm_o(b)
                if k == 6:
                    gate_o(b)

            def mask_v(h):
                if h >= 2:
                    dve.wait_ge(ss_made, h + 1)
                dve.tensor_tensor(vm[h % 2][:, :, :], vnew[0:C0, P * h:P * h + P].unsqueeze(1).to_broadcast([C0, NSEQ, P]),
                                  own[0:C0, 0:NSEQ].unsqueeze(2).to_broadcast([C0, NSEQ, P]), ALU.mult).then_inc(vm_made, 1)

            def keep_sample_states(h):
                dve.wait_ge(ss_made, h + 3)
                dve.wait_ge(ss_decayed, h + 1)
                for half in range(2):
                    sh = SSs[:, h, 4 * half:4 * half + 4, :]
                    dve.tensor_tensor(sh, sh, ps[4 + 2 * (h % 2) + half][:, :].rearrange("p (b e) -> p b e", b=4),
                                      ALU.add).then_inc(ss_kept, 1)

            def tile0_step(m):
                if m == 2:
                    dve.wait_ge(ss_made, 1)
                    both = ps[6][:, 0:2 * NH * NS].rearrange("p (h b r) -> p h b r", h=NH, r=2 * LSEQ)
                    for i, dst in enumerate((wsT, qsT)):
                        dve.tensor_copy(dst[:, :, 0:NS].rearrange("p h (b r) -> p h b r", r=LSEQ),
                                        both[:, :, :, LSEQ * i:LSEQ * i + LSEQ]).then_inc(ws_kept, 1)
                if m == 3:
                    dve.wait_ge(ss_made, 2)
                    dve.tensor_tensor(h3(vnew[0:C0, :]), h3(ps[4][0:C0, :]), per_head(c_[0:C0, 0, :], C0, P),
                                      ALU.mult).then_inc(v_kept, 1)
                    dve.tensor_tensor(h3(t1[0:C0, :]), h3(ps[5][0:C0, :]), per_head(sc["eg"][0:C0, 0, :], C0, P),
                                      ALU.mult).then_inc(qs_kept, 1)
                    dve.wait_ge(v_kept, 1)
                    dve.tensor_scalar(v_meta[:, :], vnew[0:C0, :], own[0:C0, NSEQ:NSEQ + 1], None, ALU.mult)
                    mask_v(0)
                if m == 4:
                    mask_v(1)
                    dve.wait_ge(os_made, 1)
                    keep_o(0)
                    dve.tensor_copy(S[:, :], ps[7][:, :]).then_inc(s_kept, 1)
                    keep_sample_states(0)
                    norm_o(0)
                if m == 5:
                    mask_v(2)
                    keep_sample_states(1)
                    mask_v(3)
                    gate_o(0)

            dve.wait_ge(acc_done, 3 * N_IN)
            for n, pr in enumerate(pairs):
                first_tiles = (0, *pr) if n == 0 else pr
                for step in (keep_kv, decay_diff, keep_products):
                    for t in first_tiles:
                        step(t)
                    if n == 1 and step in (keep_kv, decay_diff):
                        keep_sample_states(2 if step == keep_kv else 3)
                for k in range(1, LEVELS):
                    now = first_tiles if k < SMALL_LEVELS else pr
                    for t in now:
                        keep_p(t, k)
                    if n:
                        chain_step(k, *pairs[n - 1])
                    elif k >= SMALL_LEVELS:
                        tile0_step(2 * (k - SMALL_LEVELS))
                    for t in now:
                        keep_xy(t, k)
                    if n == 0 and k >= SMALL_LEVELS:
                        tile0_step(2 * (k - SMALL_LEVELS) + 1)
            for k in range(1, LEVELS):
                chain_step(k, *pairs[-1])

            for f in range(N_OUT):
                n = N_IN + f
                for g, (c0, w) in enumerate(GROUPS):
                    m = 3 * f + g
                    hc = hT[:, f, c0:c0 + w]
                    dve.wait_ge(x_slice_t, m + 1)
                    dve.tensor_copy(hc, ps[6 + m % 2][:, 0:w]).then_inc(x_slice_kept, 1)
                    dve.wait_ge(acc_done, 3 * n + g + 1)
                    dve.wait_ge(x_slice_kept, m + 1)
                    dve.tensor_tensor(hc, hc, ps[(n % 2) * 3 + g][:, 0:w], ALU.add).then_inc(acc_read_dve, 1)
                    dve.wait_ge(acc_read_dve, dve_reads_to(n) + g + 1)
                    hs_ = hsq[:, c0:c0 + w]
                    if f == 0:
                        dve.tensor_tensor(hs_, hc, hc, ALU.mult).then_inc(h_sq, 1)
                    else:
                        square = ps[6 + m % 2][:, 0:w]
                        link(dve.tensor_tensor(square, hc, hc, ALU.mult))
                        dve.tensor_tensor(hs_, hs_, square, ALU.add).then_inc(h_sq, 1)
                    dve.wait_ge(hg_high_s, m + 1)
                    dve.scalar_tensor_tensor(out=hg_l[:, f, c0:c0 + w], in0=hc, scalar=tn[:, 8 + f:9 + f],
                                             in1=hg_h[:, f, c0:c0 + w].bitcast(F32), op0=ALU.mult,
                                             op1=ALU.subtract).then_inc(hg_low_s, 1)
            for g, (c0, w) in enumerate(GROUPS):
                dve.wait_ge(h_sum, g + 1)
                dve.tensor_scalar(hsq[:, c0:c0 + w], ps[6 + g % 2][:, 0:w], 1.0 / D, EPS, ALU.mult,
                                  ALU.add).then_inc(rstd_mid, 1)
            dve.wait_ge(rstd_b, 1)
            link(dve.reciprocal(hsq[:, :], hsq[:, :]))

            def up_rows(g, i):
                n = N_MIX + i
                for m, (c0, w) in enumerate(GROUPS):
                    j = 3 * i + m
                    dve.wait_ge(acc_done, g * (6 * KT) + 3 * n + m + 1)
                    ub = ut[j % 2][:, 0:w]
                    dve.tensor_tensor(ub, ps[(n % 2) * 3 + m][:, 0:w], hsq[:, c0:c0 + w], ALU.mult).then_inc(acc_read_dve, 1)
                    dve.wait_ge(acc_read_dve, g * (6 * KT) + dve_reads_to(n) + m + 1)
                    dve.scalar_tensor_tensor(out=ub, in0=ub, scalar=0.0, in1=ub, op0=ALU.max, op1=ALU.mult).then_inc(u_full, 1)
                    dve.wait_ge(u_high_s, g * (3 * KT) + j + 1)
                    dve.tensor_tensor(u_l[:, i, c0:c0 + w], ub, u_h[:, i, c0:c0 + w].bitcast(F32),
                                      ALU.subtract).then_inc(u_low_s, 1)

            def down_rows(g, i):
                n = N_MIX + KT + i
                for m, (c0, w) in enumerate(GROUPS):
                    hc = hT[:, i, c0:c0 + w]
                    dve.wait_ge(acc_done, g * (6 * KT) + 3 * n + m + 1)
                    dve.tensor_tensor(hc, hc, ps[(n % 2) * 3 + m][:, 0:w], ALU.add)\
                       .then_inc(acc_read_dve, 1)

            with dve.Fori(0, FG) as g:
                for i in range(KT):
                    up_rows(g, i)
                for i in range(KT):
                    down_rows(g, i)
            dve.wait_ge(fin_const, 16)
            for t in range(NT):
                c = rows(t)
                dve.wait_ge(fin_sq, t + 1)
                link(dve.tensor_tensor(ssx[0:c, t:t + 1], sc["sso"][0:c, t, 0:1], sc["sso"][0:c, t, 1:2], ALU.add))
                dve.tensor_scalar(ssx[0:c, t:t + 1], ssx[0:c, t:t + 1], 1.0 / D, EPS, ALU.mult, ALU.add).then_inc(fin_ms, 1)
                dve.wait_ge(fin_pow, t + 1)
                for half in range(2):
                    ins = dve.scalar_tensor_tensor(out=yt[t % 3][0:c, 512 * half:512 * half + 512],
                                                   in0=ps[4 * (t % 2) + half][0:c, :], scalar=rx[0:c, t:t + 1],
                                                   in1=nfin[0:c, 512 * half:512 * half + 512], op0=ALU.mult, op1=ALU.mult)
                ins.then_inc(fin_y, 1)


_INS = ["x_prompt", "x_sample", "state_conv_a", "state_conv_qkv", "state_ssm", "meta_tokens", "norm_mix", "w_in",
        "conv_a_w", "conv_qkv_w", "a_log", "dt_bias", "gdn_norm", "w_out", "norm_ffn", "w_up", "w_down", "norm_final"]
_OUTS = [(1, SEQ, D), (NSEQ, LSEQ, D), (1, 1, 2, CONV), (1, 1, 3, QKVW), (1, 1, NH, P, P),
         (1, NSEQ, 2, CONV), (1, NSEQ, 3, QKVW), (1, NSEQ, NH, P, P)]


def kernel(**inputs):
    import concourse.bacc as bacc
    from concourse.bass_utils import run_bass_kernel_spmd

    nc = bacc.Bacc("TRN2", target_bir_lowering=False, num_devices=1)
    arrays, args = {}, []
    tables = dict(zip(("c_main", "c_gdn"), constants()))
    for name in _INS + list(tables):
        a = np.ascontiguousarray(tables[name] if name in tables else inputs[name])
        arrays[f"in_{name}"] = a
        args.append(nc.dram_tensor(f"in_{name}", a.shape, mybir.dt.from_np(a.dtype), kind="ExternalInput").ap())
    for i, shape in enumerate(_OUTS):
        args.append(nc.dram_tensor(f"out_{i}", shape, F32, kind="ExternalOutput").ap())
    build(nc, *args)
    got = run_bass_kernel_spmd(nc, [arrays], core_ids=[0])
    return tuple(got.results[0][f"out_{i}"] for i in range(len(_OUTS)))
```

```python
from contextlib import ExitStack

import numpy as np

import concourse.bass as bass
from concourse import mybir

ALU = mybir.AluOpType
ACT = mybir.ActivationFunctionType
AX = mybir.AxisListType
F32 = mybir.dt.float32
F32R = mybir.dt.float32r

P = 128
D = 1024
KT = D // P
SEQ, META, NSEQ, LSEQ = 1024, 16, 8, 4
NH = 4
CONV = D // 2
QKVW = NH * 3 * P
FFN = 4 * D
EPS = 1e-6
NS = NSEQ * LSEQ
C0 = NS + META
NT = 1 + SEQ // P
TOK = C0 + SEQ
PRM = TOK - NS
GROUPS = [(0, C0 + 2 * P), (C0 + 2 * P, 3 * P), (C0 + 5 * P, 3 * P)]
GTILES = [(0, 1, 2), (3, 4, 5), (6, 7, 8)]
O_B, O_C, O_H, O_QKV = 0, CONV, 2 * CONV, 3 * CONV
O_G = O_QKV + QKVW
O_A = O_G + NH * P
FAR_BELOW = -1e30
SMALL_LEVELS, LEVELS = 4, 7

IN_TILES = ([("k", h, O_QKV + NH * P + P * h) for h in range(NH)] + [("q", h, O_QKV + P * h) for h in range(NH)]
            + [("v", h, O_QKV + 2 * NH * P + P * h) for h in range(NH)] + [("gate", h, O_G + P * h) for h in range(NH)]
            + [x for i in range(CONV // P) for x in (("C", i, O_C + P * i), ("H", i, O_H + P * i), ("B", i, O_B + P * i))])
N_IN = len(IN_TILES)
N_OUT = D // P
N_MIX = N_IN + N_OUT
FG = FFN // D


def tile_cols(t):
    return (0, C0) if t == 0 else (C0 + (t - 1) * P, P)


def constants():
    j, i = np.arange(P)[:, None], np.arange(P)[None, :]
    seq = np.where(np.arange(C0) < NS, np.arange(C0) // LSEQ, NSEQ)
    same = seq[:, None] == seq[None, :]
    up = (j <= i)
    main = np.zeros((P, 2 * P + 2 * C0 + 2 * NH), np.float32)
    main[:, 0:P] = j == i
    main[:, P:2 * P] = up
    main[:C0, 2 * P:2 * P + C0] = same & up[:C0, :C0]
    main[:C0, 2 * P + C0:2 * P + 2 * C0] = same
    main[:16, 2 * P + 2 * C0:] = np.tile(np.eye(8), (2, 1))
    g = [-((i == j + 1) & (j % 2 == 0)).astype(np.float32)]
    for c, levels in ((P, LEVELS), (C0, SMALL_LEVELS)):
        for k in range(1, levels):
            b = 2 ** k
            first = np.arange(c // 2) // b
            m = np.zeros((P, c // 2), np.float32)
            r = np.arange(c)
            m[:c] = (r[:, None] // (2 * b) == first[None, :]) & (r[:, None] % (2 * b) >= b)
            g.append(m)
    ahead = np.zeros((P, P + C0), np.float32)
    ahead[:, 0:P] = np.where(up, 0, FAR_BELOW)
    ahead[:C0, P:] = np.where(same & up[:C0, :C0], 0, FAR_BELOW)
    g.append(ahead)
    return main, np.concatenate(g, axis=1).astype(np.float32)


def build(nc, x_prompt, x_sample, state_conv_a, state_conv_qkv, state_ssm, meta_tokens, norm_mix, w_in,
          conv_a_w, conv_qkv_w, a_log, dt_bias, gdn_norm, w_out, norm_ffn, w_up, w_down, norm_final,
          c_main, c_gdn, y_prompt, y_sample, new_a_prompt, new_qkv_prompt, new_ssm_prompt,
          new_a_sample, new_qkv_sample, new_ssm_sample):
    ctx = ExitStack()
    with ctx:
        NY = 6
        SLOT = TOK * 4
        R1 = 16512
        RK = R1 + 16 * SLOT
        RYA = RK + 8 * SLOT
        RQ = RK + 16 * SLOT
        RG = RK + 20 * SLOT
        RING = RK + 24 * SLOT
        RZ = RING + 6 * 4096
        ZB = 4448
        RS = RZ + 2 * ZB
        at = {"small": RS}

        def place(name, shape, dt, offset):
            return nc.alloc_sbuf_tensor_at(name, shape, dt, offset=offset)

        def small(name, shape):
            size = 4
            for s in shape[1:]:
                size *= s
            t = place(name, shape, F32, at["small"])
            at["small"] += (size + 31) // 32 * 32
            assert at["small"] <= 229368, name
            return t

        def sem(name):
            return ctx.enter_context(nc.semaphore(name))

        ps = [ctx.enter_context(nc.psum_tensor(f"bank{i}", [P, 512], F32)) for i in range(8)]

        xh = place("xn_high", [P, KT, TOK], F32R, R1)
        xl = place("xn_low", [P, KT, TOK], F32R, R1 + KT * SLOT)
        kf = place("k_feat", [P, NH, TOK], F32, RK)
        vf = place("v_feat", [P, NH, TOK], F32, RK + 4 * SLOT)
        qf = place("q_feat", [P, NH, TOK], F32, RQ)
        gate = place("gate_feat", [P, NH, TOK], F32, RG)
        ya_h = place("ya_high", [P, NH, TOK], F32R, RYA)
        ya_l = place("ya_low", [P, NH, TOK], F32R, RYA + 4 * SLOT)
        yb_h = place("yb_high", [P, NH, TOK], F32R, RK + 4 * SLOT)
        yb_l = place("yb_low", [P, NH, TOK], F32R, RK)
        hT = place("hT", [P, KT, TOK], F32, RQ)
        hg_h = place("hg_high", [P, KT, TOK], F32R, R1)
        hg_l = place("hg_low", [P, KT, TOK], F32R, R1 + KT * SLOT)
        u_h = place("u_high", [P, KT, TOK], F32R, RK)
        u_l = place("u_low", [P, KT, TOK], F32R, RK + KT * SLOT)
        w_raw = [place(f"w_raw{i}", [P, KT, P], F32, RING + 4096 * i) for i in range(2)]
        w_h = [place(f"w_high{i}", [P, KT, P], F32R, RING + 4096 * (2 + i)) for i in range(2)]
        w_l = [place(f"w_low{i}", [P, KT, P], F32R, RING + 4096 * (4 + i)) for i in range(2)]
        z = [place(f"conv_row{i}", [P, ZB // 4], F32, RZ + ZB * i) for i in range(2)]

        x_big = place("x_tok", [P, NT - 1, D], F32, RYA)
        x_small = place("x_tok0", [P, D], F32, RZ)
        square_out = place("square_out", [P, D], F32, RK)
        rows_q = place("rows_q", [28, QKVW], F32, RG)
        rows_a = place("rows_a", [19, CONV], F32, RG + 6144)
        rows_n = place("rows_n", [16, P], F32, RG + 8192)
        ab_raw = place("ab_raw", [P, KT, 8], F32, RG + 3 * SLOT)
        ab_w = place("ab_w", [P, KT, 16], F32R, RG + 3 * SLOT + 256)
        abT = place("abT", [16, TOK], F32, RK + 4 * SLOT)
        sq = [place(f"squares{i}", [P, TOK], F32, RYA + i * SLOT) for i in range(2)]
        sq_h = [place(f"squares_high{i}", [P, TOK], F32R, RYA + (2 + i) * SLOT) for i in range(2)]
        sq_l = [place(f"squares_low{i}", [P, TOK], F32R, RYA + (4 + i) * SLOT) for i in range(2)]
        NROW = 3 * 2 * NH
        pick = place("pick", [P, 2 * NROW], F32R, RYA + 6 * SLOT)
        ssr = place("ss_rows", [NROW, 3 * P], F32, RYA + 7 * SLOT)

        cm = small("c_main", [P, 2 * P + 2 * C0 + 2 * NH])
        eye, upper = cm[:, 0:P], cm[:, P:2 * P]
        upper_s, same_s = cm[0:C0, 2 * P:2 * P + C0], cm[0:C0, 2 * P + C0:2 * P + 2 * C0]
        fold_ab = cm[0:16, 2 * P + 2 * C0:]
        one = small("one", [P, 1])
        mhalf = small("minus_half", [P, 1])
        tq = small("tq", [P, QKVW // P, 28])
        ta = small("ta", [P, CONV // P, 19])
        tn = small("tn", [P, 16])
        gn = small("gdn_norm_col", [P, 1])
        al = small("a_log_b", [P, NH])
        dtb = small("dt_bias_b", [P, NH])
        last_in = [small(f"last_in{i}", [P, 27]) for i in range(2)]
        last_out = [small(f"last_out{i}", [27, P]) for i in range(2)]
        ssx = small("ssx", [P, NT])
        rx = small("rx", [P, NT])
        ab = small("ab", [P, NT, 2 * NH])
        sc = {n: small(n, [P, NT, NH]) for n in
              ("g", "beta", "gneg", "eg", "egl", "eglb", "nk", "rk", "c", "p", "kd_s", "rq_s", "sso", "fo", "tmp")}
        g_seq = small("g_seq", [P, NSEQ, NH])
        eg_seq = small("eg_seq", [P, NSEQ, NH])

        HB = NH * P * 4
        SET = ("Y", "wn", "vn", "kd", "qk")
        gd = [{n: place(f"{n}_{s}", [P, NH * P], F32, R1 + (5 * s + m) * HB) for m, n in enumerate(SET)} for s in range(4)]
        TB = R1 + 20 * HB
        tmpb = [{n: place(f"{n}_{s}", [P, NH * P], F32, TB + (3 * s + m) * HB) for m, n in enumerate(("kg", "At", "X"))}
                for s in range(2)]
        pb = [[place(f"pairs_{s}{i}", [P, NH * P], F32, TB + (6 + 2 * s + i) * HB) for i in range(2)] for s in range(2)]
        HC, T0 = NH * C0 * 4, R1 + 10 * HB
        CG_END = (TB + 11 * HB + 4 * c_gdn.shape[1] + 31) // 32 * 32
        assert CG_END + HB <= RK
        gd.append({**{n: place(f"{n}_t0", [C0, NH * C0], F32, T0 + 2 * HB + m * HC) for m, n in enumerate(("Y", "wn", "qk"))},
                   "vn": place("vn_t0", [C0, NH * P], F32, T0), "kd": place("kd_t0", [C0, NH * P], F32, CG_END)})
        tmpb.append({"kg": place("kg_t0", [C0, NH * P], F32, T0 + HB),
                     **{n: place(f"{n}_t0", [C0, NH * C0], F32, T0 + 2 * HB + (3 + m) * HC) for m, n in enumerate(("At", "X"))}})
        pb.append([place(f"pairs_t0{i}", [C0, NH * C0], F32, T0 + 2 * HB + (5 + i) * HC) for i in range(2)])
        S = place("S", [P, NH * P], F32, TB + 10 * HB)
        cg = place("c_gdn", [P, c_gdn.shape[1]], F32, TB + 11 * HB)
        assert TB + 11 * HB + 4 * c_gdn.shape[1] <= RK
        m0 = cg[:, 0:P]
        off = P
        lev_big = [None]
        for k in range(1, LEVELS):
            lev_big.append(cg[:, off:off + P // 2])
            off += P // 2
        lev_small = [None]
        for k in range(1, SMALL_LEVELS):
            lev_small.append(cg[:, off:off + C0 // 2])
            off += C0 // 2
        ahead_big, ahead_small = cg[:, off:off + P], cg[:, off + P:off + P + C0]
        wq = place("wq_sample", [P, NH, NSEQ, 2 * LSEQ], F32, T0 + 5 * HB)
        wsT = place("ws_feat", [P, NH, C0], F32, T0 + 6 * HB)
        qsT = place("qs_feat", [P, NH, C0], F32, T0 + 6 * HB + HC)
        v_meta = place("v_meta", [C0, NH * P], F32, T0 + 7 * HB)
        SSs = place("S_sample", [P, NH, NSEQ, P], F32, RING)
        vm = [place(f"v_masked{i}", [C0, NSEQ, P], F32, RING + 4096 * (4 + i)) for i in range(2)]
        ob = place("o_tok", [P, NH * P], F32, RZ)
        t1 = place("qs_scaled", [P, NH * P], F32, RZ + HB)
        vnew = place("v_new", [P, NH * P], F32, RZ + 2 * HB)
        ybt = place("yb_full", [P, NH, P], F32, RZ + 3 * HB)

        xs = place("x_slice", [P, NT, P], F32, RZ)
        xs0 = place("x_slice0", [P, NT, P], F32, TB + 6 * HB)
        hsq = place("h_squares", [P, TOK], F32, RZ + NT * P * 4)
        ut = [place(f"u_work{i}", [P, 3 * P], F32, RZ + 3 * P * 4 * i) for i in range(2)]
        nfin = place("norm_final_b", [P, D], F32, R1)
        yt = [place(f"y_tok{i}", [P, D], F32, R1 + 4096 * (1 + i)) for i in range(NY)]

        fin_pair = [0, 6, 2, 0, 4, 6, 2, 0, 4]
        FIRST_FIN = len(GTILES[0])

        s_norm = sem("s_norm"); s_row = sem("s_row"); s_xin = [sem(f"s_xin{i}") for i in range(5)]; s_const = sem("s_const")
        x_sq = sem("x_sq"); x_pow = sem("x_pow"); x_ms = sem("x_ms"); x_scaled = sem("x_scaled")
        x_turned = sem("x_turned"); x_high = sem("x_high"); x_low = sem("x_low")
        set_ones = sem("set_ones"); rows_turned = sem("rows_turned"); rows_kept = sem("rows_kept")
        ab_hi = sem("ab_hi"); ab_lo = sem("ab_lo"); ab_made = sem("ab_made"); ab_kept = sem("ab_kept")
        ab_turned = sem("ab_turned"); ab_tok = sem("ab_tok"); ab_act = sem("ab_act"); g_ready = sem("g_ready")
        g_summed = sem("g_summed"); g_kept = sem("g_kept"); g_exp = sem("g_exp")
        w_load = [sem("w_load0"), sem("w_load1")]
        w_high = sem("w_high"); w_low = sem("w_low"); acc_done = sem("acc_done")
        acc_read_act = sem("acc_read_act"); acc_read_dve = sem("acc_read_dve")
        z_hist = sem("z_hist"); conv_done = sem("conv_done"); silu_done = sem("silu_done")
        last_cols = sem("last_cols"); last_turned = sem("last_turned"); last_kept = sem("last_kept")
        last_sent = [sem("last_sent0"), sem("last_sent1")]
        ya_high_s = sem("ya_high_s")
        ya_low_s = sem("ya_low_s")
        sq_full = sem("sq_full"); sq_high = sem("sq_high"); sq_low = sem("sq_low"); pick_set = sem("pick_set")
        ss_rows = sem("ss_rows"); ss_turned = sem("ss_turned"); ss_done = sem("ss_done"); norms_done = sem("norms_done"); norms_mid = sem("norms_mid")
        s_gdn = sem("s_gdn"); s_states = sem("s_states")
        kv_turned = sem("kv_turned"); kv_kept = sem("kv_kept"); g_rows = sem("g_rows"); g_diff = sem("g_diff")
        d_exp = sem("d_exp"); neighbours = sem("neighbours")
        vn_kept = sem("vn_kept"); qk_kept = sem("qk_kept"); kk_made = sem("kk_made"); kk_kept = sem("kk_kept")
        y_first = sem("y_first"); x_first_t = sem("x_first_t"); x_first = sem("x_first")
        pair_zero = [sem(f"pair_zero{i}") for i in range(3)]
        p_made = [sem(f"p_made{i}") for i in range(3)]; p_kept = [sem(f"p_kept{i}") for i in range(3)]
        xy_made = [sem(f"xy_made{i}") for i in range(3)]; xy_kept = [sem(f"xy_kept{i}") for i in range(3)]
        w_made = sem("w_made"); w_kept = sem("w_kept")
        v_made = sem("v_made"); v_kept = sem("v_kept"); qs_kept = sem("qs_kept")
        os_made = sem("os_made"); s_kept = sem("s_kept"); o_kept = sem("o_kept"); o_sq = sem("o_sq"); o_ms = sem("o_ms")
        o_pow = sem("o_pow"); o_normed = sem("o_normed"); o_turned = sem("o_turned"); yb_full_s = sem("yb_full_s")
        yb_high_s = sem("yb_high_s"); yb_low_s = sem("yb_low_s")
        q_beside = sem("q_beside"); ws_kept = sem("ws_kept")
        ss_decayed = sem("ss_decayed"); vm_made = sem("vm_made"); ss_made = sem("ss_made"); ss_kept = sem("ss_kept")
        x_slice = [sem("x_slice0"), sem("x_slice1")]; x_slice_t = sem("x_slice_t"); x_slice_kept = sem("x_slice_kept")
        hg_high_s = sem("hg_high_s"); hg_low_s = sem("hg_low_s"); h_sq = sem("h_sq")
        h_sum = sem("h_sum"); rstd_b = sem("rstd_b"); rstd_mid = sem("rstd_mid")
        u_full = sem("u_full"); u_high_s = sem("u_high_s"); u_low_s = sem("u_low_s")
        fin_const = sem("fin_const"); fin_turned = sem("fin_turned"); fin_sq = sem("fin_sq"); fin_ms = sem("fin_ms")
        fin_pow = sem("fin_pow"); fin_y = sem("fin_y"); fin_sent = [sem(f"fin_sent{i}") for i in range(NY)]
        out_sent = sem("out_sent"); dve_step = sem("dve_step"); pool_step = sem("pool_step")

        act_reads = [k in ("k", "q", "v", "gate", "C") for k, _, _ in IN_TILES]

        def acc_free(pe, n, g):
            if n < N_IN and act_reads[n]:
                pe.wait_ge(acc_read_act, 3 * sum(act_reads[:n]) + g + 1)
            else:
                pe.wait_ge(acc_read_dve, dve_reads_to(n) + g + 1)

        def dve_reads_to(n):
            return 3 * (sum(not a for a in act_reads[:n]) + max(0, n - N_IN))

        def has_last(n):
            return IN_TILES[n][0] in ("k", "q", "v", "H")

        N_LAST = sum(has_last(n) for n in range(N_IN))

        def last_index(n):
            return sum(has_last(m) for m in range(n))

        def x_tile(t):
            return x_small[0:C0, :] if t == 0 else x_big[:, t - 1, :]

        def x_arrived(eng, t):
            if t == 0:
                eng.wait_ge(s_xin[0], 32)
            elif t <= 2:
                eng.wait_ge(s_xin[t], 16)
            else:
                eng.wait_ge(s_xin[2 + t // 3], 16)

        def turn_bank(g, k):
            m = KT * g + k
            return k if g == 0 else 3 + (m - KT) % 5

        def rows(t):
            return C0 if t == 0 else P

        def heads(tile, c):
            return tile[0:c, 0:NH * c]

        def first(ap, b):
            return ap.rearrange("p (n two b) -> p n two b", two=2, b=b)[:, :, 0, :]

        def second(ap, b):
            return ap.rearrange("p (n two b) -> p n two b", two=2, b=b)[:, :, 1, :]

        def per_head(ap, c, w):
            return ap.unsqueeze(2).to_broadcast([c, NH, w])

        def over_heads(ap, c, w):
            return ap.unsqueeze(1).to_broadcast([c, NH, w])

        def parity(t):
            return 2 if t == 0 else (t - 1) % 2

        def cset(t):
            return 4 if t == 0 else (t - 1) % 4

        def level_at(t, k):
            if t == 0:
                return k
            return (LEVELS - 1) * ((t - 1) // 2) + k

        pairs = [(1 + 2 * i, 2 + 2 * i) for i in range((NT - 1) // 2)]
        w_up_v = w_up.rearrange("l (k p) n -> l p k n", p=P)[0]
        w_down_v = w_down.rearrange("l (k p) n -> l p k n", p=P)[0]
        w_in_v = w_in.rearrange("l (k p) n -> l p k n", p=P)[0]
        w_out_v = w_out.rearrange("l (k p) n -> l p k n", p=P)[0]
        xp_v = x_prompt.rearrange("b (t p) n -> (b p) t n", p=P)
        xs_v = x_sample.rearrange("b s n -> (b s) n")
        ssm_v = state_ssm.rearrange("l b h d e -> l d h b e")[0]
        ssm_out_v = new_ssm_sample.rearrange("l b h d e -> l d h b e")[0]

        block = ctx.enter_context(nc.Block())

        @block.sync
        def _(sp):
            sp.dma_start(x_small[0:NS, :], xs_v).then_inc(s_xin[0], 16)
            sp.dma_start(x_small[NS:C0, :], meta_tokens).then_inc(s_xin[0], 16)
            sp.dma_start(x_big[:, 0:1, :], xp_v[:, 0:1, :]).then_inc(s_xin[1], 16)
            sp.dma_start(x_big[:, 1:2, :], xp_v[:, 1:2, :]).then_inc(s_xin[2], 16)

            def load(n):
                if n >= 2:
                    sp.wait_ge(w_low, n - 1)
                if n < N_IN:
                    c = IN_TILES[n][2]
                    src = w_in_v[:, :, c:c + P]
                elif n < N_MIX:
                    src = w_out_v[:, :, P * (n - N_IN):P * (n - N_IN + 1)]
                sp.dma_start(w_raw[n % 2][:, :, :], src).then_inc(w_load[n % 2], 16)

            def send_last(n):
                kind, i, _ = IN_TILES[n]
                m = last_index(n)
                sp.wait_ge(last_kept, m + 1)
                if kind == "H":
                    sp.dma_start(new_a_sample.rearrange("l b r c -> (l b r) c")[:, P * i:P * i + P],
                                 last_out[m % 2][0:16, :]).then_inc(last_sent[m % 2], 16)
                    sp.dma_start(new_a_prompt.rearrange("l b r c -> (l b r) c")[:, P * i:P * i + P],
                                 last_out[m % 2][16:18, :]).then_inc(last_sent[m % 2], 16)
                else:
                    c = {"q": 0, "k": NH * P, "v": 2 * NH * P}[kind] + P * i
                    sp.dma_start(new_qkv_sample.rearrange("l b r c -> (l b r) c")[:, c:c + P],
                                 last_out[m % 2][0:24, :]).then_inc(last_sent[m % 2], 16)
                    sp.dma_start(new_qkv_prompt.rearrange("l b r c -> (l b r) c")[:, c:c + P],
                                 last_out[m % 2][24:27, :]).then_inc(last_sent[m % 2], 16)

            def slice_x(f):
                if f == 0:
                    for par in range(2):
                        sp.wait_ge(xy_kept[par], level_at(NT - 1, LEVELS - 1))
                elif f == 1:
                    sp.wait_ge(yb_low_s, NT)
                else:
                    sp.wait_ge(x_slice_t, 3 * f)
                cols, dst = slice(P * f, P * f + P), xs if f else xs0
                sp.dma_start(dst[0:NS, 0, :], xs_v[:, cols]).then_inc(x_slice[f % 2], 16)
                sp.dma_start(dst[NS:C0, 0, :], meta_tokens[:, cols]).then_inc(x_slice[f % 2], 16)
                sp.dma_start(dst[:, 1:NT, :], xp_v[:, :, cols]).then_inc(x_slice[f % 2], 16)

            for n in range(N_IN):
                load(n)
                if n == 0:
                    sp.dma_start(x_big[:, 2:5, :], xp_v[:, 2:5, :]).then_inc(s_xin[3], 16)
                    sp.dma_start(x_big[:, 5:8, :], xp_v[:, 5:8, :]).then_inc(s_xin[4], 16)
                if n >= 4 and has_last(n - 4):
                    send_last(n - 4)
            sp.wait_ge(acc_done, 3 * N_IN)
            sp.dma_start(cg[:, :], c_gdn).then_inc(s_gdn, 16)
            for h in range(NH):
                sp.dma_start(SSs[:, h, :, :], ssm_v[:, h, :, :]).then_inc(s_states, 16)
            for n in range(N_IN - 4, N_IN):
                if has_last(n):
                    send_last(n)
            for h in range(NH):
                sp.wait_ge(ss_kept, 2 * (h + 1))
                sp.dma_start(ssm_out_v[:, h, :, :], SSs[:, h, :, :]).then_inc(out_sent, 16)
            sp.wait_ge(out_sent, 16 * NH)
            for n in range(N_IN, N_MIX):
                if n >= N_IN + 3:
                    slice_x(n - N_IN - 3)
                if n == N_IN + 3:
                    sp.wait_ge(s_kept, NT)
                    sp.dma_start(new_ssm_prompt.rearrange("l b h d e -> d (l b h) e"),
                                 S[:, :].rearrange("p (h e) -> p h e", h=NH)).then_inc(out_sent, 16)
                load(n)
            for f in range(N_MIX - N_IN - 3, N_OUT):
                slice_x(f)

            with sp.Fori(0, FG) as g:
                for i in range(2 * KT):
                    n = N_MIX + i
                    sp.wait_ge(w_low, g * (2 * KT) + (n - 1))
                    if i < KT:
                        src = w_up_v[:, :, bass.ds(g * D + P * i, P)]
                    else:
                        src = w_down_v[:, bass.ds(g * KT, KT), P * (i - KT):P * (i - KT) + P]
                    sp.dma_start(w_raw[n % 2][:, :, :], src).then_inc(w_load[n % 2], 16)
            sp.wait_ge(acc_done, 3 * (N_MIX + 2 * KT * FG - KT))
            sp.dma_start(nfin[:, :], norm_final.rearrange("(a n) -> a n", a=1).to_broadcast([P, D])).then_inc(fin_const, 16)
            for t in range(NT):
                sp.wait_ge(fin_y, t + 1)
                if t == 0:
                    sp.dma_start(y_sample.rearrange("b s n -> (b s) n"), yt[0][0:NS, :]).then_inc(fin_sent[0], 16)
                else:
                    sp.dma_start(y_prompt[0, P * (t - 1):P * t, :], yt[t % NY][:, :]).then_inc(fin_sent[t % NY], 16)
            for i in range(NY):
                sp.wait_ge(fin_sent[i], 16 * len(range(i, NT, NY)))
            sp.wait_ge(out_sent, 16 * (NH + 1))
            for i in range(2):
                sp.wait_ge(last_sent[i], 32 * len(range(i, N_LAST, 2)))

        @block.gpsimd
        def _(pool):
            pool.memset(one[:, :], 1.0).then_inc(set_ones, 1)
            pool.memset(mhalf[:, :], -0.5).then_inc(set_ones, 1)
            pool.memset(ab[:, :, :], 0.0).then_inc(set_ones, 1)
            pool.wait_ge(set_ones, 3)
            def x_power(t):
                pool.wait_ge(x_ms, t + 1)
                pool.tensor_tensor(rx[0:rows(t), t:t + 1], ssx[0:rows(t), t:t + 1], mhalf[0:rows(t), :],
                                   ALU.pow).then_inc(x_pow, 1)

            def split_low(n, g=0):
                pool.wait_ge(w_high, g * (2 * KT) + (n + 1))
                if n >= 2:
                    pool.wait_ge(acc_done, g * (6 * KT) + 3 * (n - 1))
                pool.tensor_tensor(w_l[n % 2][:, :, :], w_raw[n % 2][:, :, :], w_h[n % 2][:, :, :].bitcast(F32),
                                   ALU.subtract).then_inc(w_low, 1)

            for t in GTILES[0]:
                x_power(t)
            split_low(0)
            for t in GTILES[1] + GTILES[2]:
                x_power(t)
            pool.wait_ge(ab_hi, 1)
            pool.tensor_tensor(ab_w[:, :, 8:16], ab_raw[:, :, :], ab_w[:, :, 0:8].bitcast(F32),
                               ALU.subtract).then_inc(ab_lo, 1)

            for n in range(N_IN):
                kind, i, _ = IN_TILES[n]
                if kind in ("k", "q", "v"):
                    f = {"q": 0, "k": NH, "v": 2 * NH}[kind] + i
                    if n == 0:
                        pool.wait_ge(x_turned, 24)
                        pool.wait_ge(rows_kept, 3)
                    elif n >= 2:
                        pool.wait_ge(conv_done, n - 1)
                    zb = z[n % 2]
                    pool.tensor_copy(zb[:, 0:56].rearrange("p (b r) -> p b r", r=7)[:, :, 0:3],
                                     tq[:, f, 0:24].rearrange("p (b r) -> p b r", r=3))
                    pool.memset(zb[:, 56:59], 0.0).then_inc(z_hist, 1)
                if n == 3 * NH:
                    pool.wait_ge(x_low, 3 * KT)
                    pool.memset(pick[:, :].bitcast(F32), 0.0).then_inc(pick_set, 1)
                    pool.wait_ge(pick_set, 1)
                    pool.memset(pick[:, NROW:NROW + 1].bitcast(F32), 1.0).then_inc(pick_set, 1)
                if kind == "H":
                    if i:
                        pool.wait_ge(ya_low_s, i)
                    else:
                        pool.wait_ge(conv_done, 3 * NH)
                    pool.tensor_copy(z[1][:, 0:48].rearrange("p (b r) -> p b r", r=6)[:, :, 0:2],
                                     ta[:, i, 0:16].rearrange("p (b r) -> p b r", r=2))
                    pool.memset(z[1][:, 48:50], 0.0).then_inc(z_hist, 1)
                if n + 1 < N_IN:
                    split_low(n + 1)
                if has_last(n):
                    m = last_index(n)
                    if m >= 2:
                        pool.wait_ge(last_turned, m - 1)
                    if kind == "H":
                        pool.wait_ge(acc_read_dve, dve_reads_to(n) + 3)
                        pool.tensor_copy(last_in[m % 2][:, 0:16].rearrange("p (b r) -> p b r", r=2),
                                         z[1][:, 0:48].rearrange("p (b r) -> p b r", r=6)[:, :, 4:6])
                        pool.tensor_copy(last_in[m % 2][:, 16:18], z[1][:, 50 + PRM - 2:50 + PRM]).then_inc(last_cols, 1)
                    else:
                        pool.wait_ge(acc_read_act, 3 * n + 3)
                        pool.tensor_copy(last_in[m % 2][:, 0:24].rearrange("p (b r) -> p b r", r=3),
                                         z[n % 2][:, 0:56].rearrange("p (b r) -> p b r", r=7)[:, :, 4:7])
                        pool.tensor_copy(last_in[m % 2][:, 24:27], z[n % 2][:, 59 + PRM - 3:59 + PRM]).then_inc(last_cols, 1)

            def first_level(t):
                c, st, tb = rows(t), gd[cset(t)], tmpb[parity(t)]
                h3 = lambda ap: ap.rearrange("p (h i) -> p h i", h=NH)
                pool.wait_ge(kk_kept, t + 1)
                if t >= 3:
                    pool.wait_ge(xy_made[parity(t)], level_at(t, 0))
                pool.tensor_tensor(h3(heads(tb["X"], c)), h3(heads(tb["At"], c)), over_heads(m0[0:c, 0:c], c, c),
                                   ALU.mult).then_inc(neighbours, 1)

            def add_diagonal(t):
                c, st, tb = rows(t), gd[cset(t)], tmpb[parity(t)]
                h3 = lambda ap: ap.rearrange("p (h i) -> p h i", h=NH)
                pool.wait_ge(neighbours, t + 1)
                if t >= 5:
                    pool.wait_ge(v_made, t - 4)
                pool.tensor_tensor(h3(heads(st["Y"], c)), over_heads(eye[0:c, 0:c], c, c), h3(heads(tb["X"], c)),
                                   ALU.add).then_inc(y_first, 1)

            def zero_pairs(t, k):
                c, par = rows(t), parity(t)
                at_level = level_at(t, k)
                if at_level >= 3:
                    pool.wait_ge(xy_made[par], at_level - 2)
                pool.memset(heads(pb[par][at_level % 2], c), 0.0).then_inc(pair_zero[par], 1)

            def power(t):
                c = rows(t)
                pool.wait_ge(o_ms, t + 1)
                pool.tensor_tensor(sc["fo"][0:c, t, :], sc["tmp"][0:c, t, :], mhalf[0:c, :].to_broadcast([c, NH]),
                                   ALU.pow).then_inc(o_pow, 1)

            pool.wait_ge(acc_done, 3 * N_IN)
            pool.wait_ge(s_gdn, 16)
            def decay_states(h):
                pool.wait_ge(ss_made, 1)
                pool.tensor_tensor(SSs[:, h, :, :], SSs[:, h, :, :], eg_seq[:, :, h:h + 1].to_broadcast([P, NSEQ, P]),
                                   ALU.mult).then_inc(ss_decayed, 1)

            for n, pr in enumerate(pairs):
                first_tiles = (0, *pr) if n == 0 else pr
                if n == 0:
                    for t in first_tiles:
                        zero_pairs(t, 1)
                        zero_pairs(t, 2)
                for t in first_tiles:
                    first_level(t)
                for t in first_tiles:
                    add_diagonal(t)
                if n == 0:
                    pool.tensor_copy(wq[:, :, :, LSEQ:2 * LSEQ], qf[:, :, 0:NS].rearrange("p h (b r) -> p h b r", r=LSEQ))
                    pool.memset(wsT[:, :, NS:C0], 0.0)
                    pool.memset(qsT[:, :, NS:C0], 0.0).then_inc(q_beside, 1)
                for k in range(1, LEVELS):
                    if n and k == 1:
                        power(pairs[n - 1][0])
                    if n and k == 3:
                        power(pairs[n - 1][1])
                    for t in first_tiles:
                        if k + 2 < (SMALL_LEVELS if t == 0 else LEVELS):
                            zero_pairs(t, k + 2)
                        elif t and pr != pairs[-1]:
                            zero_pairs(t + 2, k + 3 - LEVELS)
                if n >= 2:
                    split_low(N_IN + n - 2)
                if n == 0:
                    decay_states(0)
                    decay_states(1)
                    power(0)
                    decay_states(2)
                    decay_states(3)
            for t in pairs[-1]:
                power(t)

            for n in range(N_IN + 2, N_MIX + 1):
                split_low(n)
            with pool.Fori(0, FG - 1) as g:
                for i in range(2 * KT):
                    split_low(N_MIX + 1 + i, g)
            for i in range(2 * KT - 1):
                split_low(N_MIX + 1 + i, FG - 1)
            for t in range(NT):
                c = rows(t)
                pool.wait_ge(fin_ms, t + 1)
                pool.tensor_tensor(rx[0:c, t:t + 1], ssx[0:c, t:t + 1], mhalf[0:c, :], ALU.pow).then_inc(fin_pow, 1)

        @block.scalar
        def _(act):
            act.dma_start(cm[:, :], c_main).then_inc(s_const, 16)
            act.dma_start(rows_n[0:8, :], norm_mix.rearrange("l (k p) -> (l k) p", p=P)).then_inc(s_norm, 16)
            act.dma_start(rows_n[8:16, :], norm_ffn.rearrange("l (k p) -> (l k) p", p=P)).then_inc(s_norm, 16)
            act.dma_start(ab_raw[:, :, :], w_in_v[:, :, O_A:O_A + 8]).then_inc(s_row, 16)
            act.dma_start(rows_q[0:24, :], state_conv_qkv.rearrange("l b r c -> (l b r) c")).then_inc(s_row, 16)
            act.dma_start(rows_q[24:28, :], conv_qkv_w[0]).then_inc(s_row, 16)
            act.dma_start(rows_a[0:16, :], state_conv_a.rearrange("l b r c -> (l b r) c")).then_inc(s_row, 16)
            act.dma_start(rows_a[16:19, :], conv_a_w[0]).then_inc(s_row, 16)
            act.dma_start(gn[:, :], gdn_norm.rearrange("l (p a) -> (l p) a", a=1)).then_inc(s_row, 16)
            act.dma_start(al[:, :], a_log.to_broadcast([P, NH])).then_inc(s_row, 16)
            act.dma_start(dtb[:, :], dt_bias.to_broadcast([P, NH])).then_inc(s_row, 16)
            def split_high(n, g=0):
                act.wait_ge(w_load[n % 2], g * (16 * KT) + 16 * (n // 2 + 1))
                if n >= 2:
                    act.wait_ge(acc_done, g * (6 * KT) + 3 * (n - 1))
                act.activation(w_h[n % 2][:, :, :], w_raw[n % 2][:, :, :], ACT.Copy).then_inc(w_high, 1)

            for g, (c0, w) in enumerate(GROUPS):
                for t in GTILES[g]:
                    x_arrived(act, t)
                    if t:
                        act.wait_ge(x_sq, t)
                    act.activation(square_out[0:rows(t), :], x_tile(t), ACT.Square,
                                   accum_out=ssx[0:rows(t), t:t + 1]).then_inc(x_sq, 1)
                if g == 0:
                    split_high(0)
                    act.wait_ge(rows_kept, 1)
                for k in range(KT):
                    act.wait_ge(x_turned, KT * g + k + 1)
                    act.activation(xh[:, k, c0:c0 + w], ps[turn_bank(g, k)][:, 0:w], ACT.Copy,
                                   scale=tn[:, k:k + 1]).then_inc(x_high, 1)
            act.wait_ge(s_row, 128)
            act.activation(ab_w[:, :, 0:8], ab_raw[:, :, :], ACT.Copy).then_inc(ab_hi, 1)
            split_high(1)
            for g, (c0, w) in enumerate(GROUPS):
                act.wait_ge(ab_made, g + 1)
                act.activation(abT[:, c0:c0 + w], ps[6 + g % 2][0:16, 0:w], ACT.Copy).then_inc(ab_kept, 1)

            def ab_exps():
                act.wait_ge(ab_tok, 2)
                act.activation(sc["tmp"][:, :, :], sc["eg"][:, :, :], ACT.Exp, scale=-1.0).then_inc(ab_act, 1)
                act.activation(sc["beta"][:, :, :], ab[:, :, NH:2 * NH], ACT.Exp, scale=-1.0).then_inc(ab_act, 1)
                act.activation(al[:, :], al[:, :], ACT.Exp).then_inc(ab_act, 1)
                act.wait_ge(ab_act, 3)
                act.activation(sc["tmp"][:, :, :], sc["tmp"][:, :, :], ACT.Ln, bias=one[:, 0:1]).then_inc(ab_act, 1)

            def silu(n):
                kind, i, _ = IN_TILES[n]
                dst = {"k": kf, "q": qf, "v": vf}[kind][:, i, :]
                act.wait_ge(conv_done, n + 1)
                act.activation(dst, dst, ACT.Silu).then_inc(silu_done, 1)

            def square_high(j):
                act.wait_ge(sq_full, j + 1)
                if j >= 2:
                    act.wait_ge(ss_done, j - 1)
                act.activation(sq_h[j % 2][:, :], sq[j % 2][:, :], ACT.Copy).then_inc(sq_high, 1)

            for n in range(N_IN):
                kind, i, _ = IN_TILES[n]
                if 0 < n and n + 1 < N_IN:
                    split_high(n + 1)
                if n == 2:
                    ab_exps()
                if kind in ("k", "q", "v"):
                    zb = z[n % 2]
                    if n == 0:
                        act.wait_ge(x_turned, 24)
                    elif n >= 2:
                        act.wait_ge(conv_done, n - 1)
                        act.wait_ge(last_cols, n - 1)
                    for g, (c0, w) in enumerate(GROUPS):
                        act.wait_ge(acc_done, 3 * n + g + 1)
                        bank = ps[(n % 2) * 3 + g]
                        if g == 0:
                            act.activation(zb[:, 0:56].rearrange("p (b r) -> p b r", r=7)[:, :, 3:7],
                                           bank[:, 0:NS].rearrange("p (b r) -> p b r", r=LSEQ), ACT.Copy)
                            act.activation(zb[:, 59:59 + w - NS], bank[:, NS:w], ACT.Copy).then_inc(acc_read_act, 1)
                        else:
                            act.activation(zb[:, 59 + c0 - NS:59 + c0 - NS + w], bank[:, 0:w],
                                           ACT.Copy).then_inc(acc_read_act, 1)
                    if n:
                        silu(n - 1)
                if kind == "gate":
                    for g, (c0, w) in enumerate(GROUPS):
                        act.wait_ge(acc_done, 3 * n + g + 1)
                        if i == 0 and g == 0:
                            act.wait_ge(rows_kept, 3)
                            act.wait_ge(ab_made, 3)
                        act.activation(gate[:, i, c0:c0 + w], ps[(n % 2) * 3 + g][:, 0:w], ACT.Silu).then_inc(acc_read_act, 1)
                    if i == 0:
                        silu(n - 1)
                    square_high(2 * i)
                    square_high(2 * i + 1)
                if kind == "C":
                    if i == 0:
                        act.wait_ge(conv_done, 3 * NH)
                        act.wait_ge(last_cols, 3 * NH)
                    else:
                        act.wait_ge(acc_read_dve, dve_reads_to(n))
                    for g, (c0, w) in enumerate(GROUPS):
                        act.wait_ge(acc_done, 3 * n + g + 1)
                        act.activation(z[0][:, c0:c0 + w], ps[(n % 2) * 3 + g][:, 0:w], ACT.Copy).then_inc(acc_read_act, 1)
                if kind == "B":
                    for g, (c0, w) in enumerate(GROUPS):
                        act.wait_ge(acc_read_dve, dve_reads_to(n) + g + 1)
                        act.activation(ya_h[:, i, c0:c0 + w], z[1][:, c0:c0 + w], ACT.Copy).then_inc(ya_high_s, 1)
                if n == 4:
                    act.wait_ge(g_kept, 4)
                    act.activation(sc["eg"][:, :, :], sc["gneg"][:, :, :], ACT.Exp, scale=-1.0).then_inc(g_exp, 1)
                    act.activation(sc["egl"][:, :, :], sc["egl"][:, :, :], ACT.Exp).then_inc(g_exp, 1)
                    act.activation(sc["eglb"][:, :, :], sc["eglb"][:, :, :], ACT.Exp).then_inc(g_exp, 1)
                    act.activation(eg_seq[:, :, :], eg_seq[:, :, :], ACT.Exp).then_inc(g_exp, 1)
                if n == 4 * NH + 1:
                    act.wait_ge(norms_mid, 1)
                    act.activation(sc["nk"][:, :, :], sc["nk"][:, :, :], ACT.Sqrt).then_inc(norms_mid, 1)
                    act.activation(sc["rq_s"][:, :, :], sc["rq_s"][:, :, :], ACT.Sqrt).then_inc(norms_mid, 1)

            def decay_exp(t):
                c, st = rows(t), gd[cset(t)]
                act.wait_ge(g_diff, t + 1)
                act.activation(heads(st["wn"], c), heads(st["wn"], c), ACT.Exp).then_inc(d_exp, 1)

            def keep_v_scaled(t):
                c, st = rows(t), gd[cset(t)]
                act.wait_ge(kv_turned, t + 1)
                if t >= 5:
                    act.wait_ge(v_made, t - 4)
                for h in range(NH):
                    hs = slice(P * h, P * h + P)
                    ins = act.activation(st["vn"][0:c, hs], ps[2 * parity(t) + 1][0:c, hs], ACT.Copy,
                                         scale=sc["nk"][0:c, t, h:h + 1])
                ins.then_inc(vn_kept, 1)

            def keep_x(t):
                c, tb = rows(t), tmpb[parity(t)]
                act.wait_ge(x_first_t, t + 1)
                act.wait_ge(y_first, t + 1)
                act.activation(heads(tb["X"], c), ps[2 * parity(t)][0:c, 0:NH * c], ACT.Copy).then_inc(x_first, 1)

            def keep_w(t):
                c, st = rows(t), gd[cset(t)]
                act.wait_ge(w_made, t + 1)
                made = ps[2 * parity(t)][:, 0:NH * c]
                if t == 0:
                    made = made.rearrange("p (h i) -> p h i", h=NH)[:, :, 0:NS].rearrange("p h (b r) -> p h b r", r=LSEQ)
                act.activation(wq[:, :, :, 0:LSEQ] if t == 0 else st["wn"][:, :], made, ACT.Copy, scale=-1.0).then_inc(w_kept, 1)

            def o_square(t):
                c = rows(t)
                act.wait_ge(o_kept, t + 1)
                for h in range(NH):
                    ins = act.activation(t1[0:c, P * h:P * h + P], ob[0:c, P * h:P * h + P], ACT.Square,
                                         scale=sc["rq_s"][0:c, t, h:h + 1], accum_out=sc["sso"][0:c, t, h:h + 1])
                ins.then_inc(o_sq, 1)

            def yb_high(t):
                c0, c = tile_cols(t)
                act.wait_ge(yb_full_s, t + 1)
                act.activation(yb_h[:, :, c0:c0 + c], ybt[:, :, 0:c], ACT.Copy).then_inc(yb_high_s, 1)

            for n, pr in enumerate(pairs):
                first_tiles = (0, *pr) if n == 0 else pr
                for t in first_tiles:
                    keep_v_scaled(t)
                for t in first_tiles:
                    decay_exp(t)
                for t in first_tiles:
                    keep_x(t)
                if n == 0:
                    keep_w(0)
                    o_square(0)
                    yb_high(0)
                else:
                    for t in pairs[n - 1]:
                        o_square(t)
                        yb_high(t)
                for t in pr:
                    keep_w(t)
                if n in (1, 2):
                    split_high(N_IN + n - 1)
            for t in pairs[-1]:
                o_square(t)
                yb_high(t)

            for f in range(N_OUT):
                n = N_IN + f
                if f:
                    split_high(n + 1)
                for g, (c0, w) in enumerate(GROUPS):
                    act.wait_ge(acc_read_dve, dve_reads_to(n) + g + 1)
                    act.activation(hg_h[:, f, c0:c0 + w], hT[:, f, c0:c0 + w], ACT.Copy,
                                   scale=tn[:, 8 + f:9 + f]).then_inc(hg_high_s, 1)

            act.wait_ge(rstd_mid, 3)
            act.activation(hsq[:, :], hsq[:, :], ACT.Sqrt).then_inc(rstd_b, 1)

            def up_high(g, i):
                for m, (c0, w) in enumerate(GROUPS):
                    act.wait_ge(u_full, g * (3 * KT) + 3 * i + m + 1)
                    if i == 0 and m == 0:
                        act.wait_ge(acc_done, g * (6 * KT) + 3 * N_MIX)
                    act.activation(u_h[:, i, c0:c0 + w], ut[(3 * i + m) % 2][:, 0:w], ACT.Copy).then_inc(u_high_s, 1)

            with act.Fori(0, FG - 1) as g:
                for i in range(KT):
                    split_high(N_MIX + 1 + i, g)
                    up_high(g, i)
                for i in range(KT):
                    split_high(N_MIX + KT + 1 + i, g)
            for i in range(KT):
                split_high(N_MIX + 1 + i, FG - 1)
                up_high(FG - 1, i)
            for i in range(KT - 1):
                split_high(N_MIX + KT + 1 + i, FG - 1)
            for t in range(NT):
                c = rows(t)
                act.wait_ge(fin_turned, t + 1)
                if t == 0:
                    act.wait_ge(acc_done, 3 * (N_MIX + 2 * KT * FG - KT))
                if t >= NY:
                    act.wait_ge(fin_sent[t % NY], 16 * (t // NY))
                for half in range(2):
                    ins = act.activation(yt[t % NY][0:c, 512 * half:512 * half + 512], ps[fin_pair[t] + half][0:c, :],
                                         ACT.Square, accum_out=sc["sso"][0:c, t, half:half + 1])
                ins.then_inc(fin_sq, 1)

        @block.tensor
        def _(pe):
            def dense_part(n, g, rhs, ks):
                c0, w = GROUPS[g]
                bank = ps[(n % 2) * 3 + g]
                for k in ks:
                    hi, lo = rhs(k)
                    pe.matmul(bank[:, 0:w], w_h[n % 2][:, k, :], hi[:, c0:c0 + w], start=(k == 0), stop=False)
                    pe.matmul(bank[:, 0:w], w_h[n % 2][:, k, :], lo[:, c0:c0 + w], start=False, stop=False)
                    ins = pe.matmul(bank[:, 0:w], w_l[n % 2][:, k, :], hi[:, c0:c0 + w], start=False, stop=(k == KT - 1))
                    if k == KT - 1:
                        ins.then_inc(acc_done, 1)

            def dense(n, rhs, g0=0, prepare=None, ready=(0, 0, 0)):
                for g in range(3):
                    if g == 0:
                        pe.wait_ge(w_low, g0 * (2 * KT) + (n + 1))
                    if prepare:
                        prepare(g)
                    dense_part(n, g, rhs, range(ready[g], KT))

            pe.wait_ge(s_const, 16)
            pe.wait_ge(s_norm, 32)
            pe.transpose(ps[0][:, 0:16], rows_n[:, :], eye[0:16, 0:16]).then_inc(rows_turned, 1)

            def normed(k):
                return xh[:, k, :], xl[:, k, :]

            for g, (c0, w) in enumerate(GROUPS):
                for k in range(KT):
                    if g == 0 and k == 0:
                        pe.wait_ge(rows_kept, 1)
                    m = KT * g + k
                    if g:
                        pe.wait_ge(x_low, m - 4 if m >= KT + 5 else m - KT + 4)
                    for t in GTILES[g]:
                        o, c = tile_cols(t)
                        if k == 0:
                            pe.wait_ge(x_scaled, t + 1)
                        ins = pe.transpose(ps[turn_bank(g, k)][:, o - c0:o - c0 + c], x_tile(t)[:, P * k:P * k + P],
                                           eye[0:c, 0:c])
                    ins.then_inc(x_turned, 1)
                if g == 0:
                    pe.wait_ge(w_low, 1)
                pe.wait_ge(x_low, KT * (g + 1))
                dense_part(0, g, normed, range(KT))
            pe.wait_ge(s_row, 128)
            for f in range(QKVW // P):
                ins = pe.transpose(ps[3][:, 28 * f:28 * f + 28], rows_q[:, P * f:P * f + P], eye[0:28, 0:28])
            for f in range(CONV // P):
                ins = pe.transpose(ps[4][:, 19 * f:19 * f + 19], rows_a[:, P * f:P * f + P], eye[0:19, 0:19])
            ins.then_inc(rows_turned, 1)
            pe.wait_ge(ab_lo, 1)
            for g, (c0, w) in enumerate(GROUPS):
                if g == 2:
                    pe.wait_ge(ab_kept, 1)
                for k in range(KT):
                    pe.matmul(ps[6 + g % 2][0:16, 0:w], ab_w[:, k, 0:16], xh[:, k, c0:c0 + w], start=(k == 0), stop=False)
                for k in range(KT):
                    ins = pe.matmul(ps[6 + g % 2][0:16, 0:w], ab_w[:, k, 0:16], xl[:, k, c0:c0 + w], start=False,
                                    stop=(k == KT - 1))
                ins.then_inc(ab_made, 1)

            def turn_last(n):
                m = last_index(n)
                r = 18 if IN_TILES[n][0] == "H" else 27
                pe.wait_ge(last_cols, m + 1)
                if m:
                    pe.wait_ge(last_kept, m)
                pe.transpose(ps[6][0:r, 0:P], last_in[m % 2][:, 0:r], eye).then_inc(last_turned, 1)

            def sum_squares(j):
                pe.wait_ge(pick_set, 2)
                pe.wait_ge(sq_low, j + 1)
                for m, g in enumerate((1, 0, 2)):
                    c0, w = GROUPS[g]
                    row = 2 * NH * g + j
                    for part in (sq_h, sq_l):
                        ins = pe.matmul(ps[7][0:NROW, 0:w], pick[:, NROW - row:2 * NROW - row], part[j % 2][:, c0:c0 + w],
                                        start=(j == 0 and m == 0 and part is sq_h),
                                        stop=(j == 2 * NH - 1 and m == 2 and part is sq_l))
                ins.then_inc(ss_done, 1)

            def turn_squares():
                pe.wait_ge(ss_rows, 1)
                for t in range(NT):
                    o, c = tile_cols(t)
                    g = [t in x for x in GTILES].index(True)
                    o -= GROUPS[g][0]
                    ins = pe.transpose(ps[7][0:c, NROW * t:NROW * t + NROW], ssr[:, o:o + c], eye[0:NROW, 0:NROW])
                ins.then_inc(ss_turned, 1)

            for n in range(N_IN):
                def prepare(g, n=n):
                    if n >= 2:
                        acc_free(pe, n - 2, g)
                    elif g == 0:
                        pe.wait_ge(rows_kept, 3)
                if n:
                    dense(n, normed, prepare=prepare)
                if n == 1:
                    pe.wait_ge(ab_kept, 3)
                    for t in range(NT):
                        o, c = tile_cols(t)
                        ins = pe.matmul(ps[7][0:c, 8 * t:8 * t + 8], abT[:, o:o + c], fold_ab, start=True, stop=True)
                    ins.then_inc(ab_turned, 1)
                if n == 2:
                    pe.wait_ge(g_ready, 2)
                    big = sc["g"][:, 1:NT, :]
                    small_g = sc["g"][0:C0, 0, :]
                    pe.matmul(ps[7][:, 0:32], upper, big, start=True, stop=True)
                    pe.matmul(ps[7][0:C0, 32:36], upper_s, small_g, start=True, stop=True)
                    pe.matmul(ps[7][:, 64:96], one[:, 0:1].to_broadcast([P, P]), big, start=True, stop=True)
                    pe.matmul(ps[7][0:C0, 96:100], same_s, small_g, start=True, stop=True)
                    pe.matmul(ps[7][:, 128:160], one[0:C0, 0:1].to_broadcast([C0, P]), g_seq[0:C0, :, :],
                              start=True, stop=True).then_inc(g_summed, 1)
                if n and has_last(n - 1):
                    turn_last(n - 1)
                if IN_TILES[n][0] == "gate" and IN_TILES[n][1]:
                    sum_squares(2 * IN_TILES[n][1] - 2)
                    sum_squares(2 * IN_TILES[n][1] - 1)
                if n == 4 * NH:
                    sum_squares(2 * NH - 2)
                    sum_squares(2 * NH - 1)
                if n == 4 * NH + 1:
                    turn_squares()

            def turn_kv(t):
                o, c = tile_cols(t)
                b = ps[2 * parity(t)], ps[2 * parity(t) + 1]
                if t >= 3:
                    pe.wait_ge(w_kept, t - 1)
                for i, src in enumerate((kf, vf)):
                    for h in range(NH):
                        ins = pe.transpose(b[i][0:c, P * h:P * h + P], src[:, h, o:o + c], eye)
                ins.then_inc(kv_turned, 1)

            def decay_rows(t):
                c = rows(t)
                pe.wait_ge(kv_kept, t + 1)
                if t == 0:
                    pe.wait_ge(s_gdn, 16)
                u, ahead = (upper_s, ahead_small) if t == 0 else (upper, ahead_big)
                for h in range(NH):
                    out = ps[2 * parity(t)][0:c, c * h:c * h + c]
                    pe.matmul(out, eye[0:c, 0:c], ahead[0:c, :], start=True, stop=False)
                    ins = pe.matmul(out, sc["g"][0:c, t, h:h + 1].to_broadcast([c, c]), u, start=False, stop=True)
                ins.then_inc(g_rows, 1)

            def products(t):
                o, c = tile_cols(t)
                pe.wait_ge(g_diff, t + 1)
                pe.wait_ge(vn_kept, t + 1)
                for i, rhs in enumerate((kf, qf)):
                    for h in range(NH):
                        ins = pe.matmul(ps[2 * parity(t) + i][0:c, c * h:c * h + c], kf[:, h, o:o + c],
                                        rhs[:, h, o:o + c], start=True, stop=True)
                ins.then_inc(kk_made, 1)

            def turn_y(t):
                c, tb = rows(t), tmpb[parity(t)]
                pe.wait_ge(neighbours, t + 1)
                for h in range(NH):
                    hs = slice(c * h, c * h + c)
                    pe.matmul(ps[2 * parity(t)][0:c, hs], eye[0:c, 0:c], eye[0:c, 0:c], start=True, stop=False)
                    ins = pe.matmul(ps[2 * parity(t)][0:c, hs], tb["X"][0:c, hs], eye[0:c, 0:c], start=False, stop=True)
                ins.then_inc(x_first_t, 1)

            def sample_products(j):
                if j == 0:
                    pe.wait_ge(s_states, 16 * NH)
                    pe.wait_ge(w_kept, 1)
                    pe.wait_ge(q_beside, 1)
                for i in (2 * j, 2 * j + 1):
                    h, b = i // NSEQ, i % NSEQ
                    ins = pe.matmul(ps[6][:, 2 * LSEQ * i:2 * LSEQ * (i + 1)], SSs[:, h, b, :], wq[:, h, b, :],
                                    start=True, stop=True)
                if 2 * j + 2 == NH * NSEQ:
                    ins.then_inc(ss_made, 1)

            def level_p(t, k):
                c, tb, par = rows(t), tmpb[parity(t)], parity(t)
                if k == 1:
                    pe.wait_ge(x_first, t + 1)
                else:
                    pe.wait_ge(xy_kept[par], level_at(t, k) - 1)
                for h in range(NH):
                    hs = slice(c * h, c * h + c)
                    ins = pe.matmul(ps[2 * par][0:c, hs], tb["At"][0:c, hs], tb["X"][0:c, hs], start=True, stop=True)
                    if h == NH - 1:
                        ins.then_inc(p_made[par], 1)
                    if (t, k) in ((1, 5), (2, 5)):
                        sample_products(NH * t + h)

            def level_xy(t, k):
                c, tb, st, par = rows(t), tmpb[parity(t)], gd[cset(t)], parity(t)
                at_level, last = level_at(t, k), k == (SMALL_LEVELS if t == 0 else LEVELS) - 1
                pk = pb[par][at_level % 2]
                pe.wait_ge(p_kept[par], at_level)
                if k == 1:
                    pe.wait_ge(qk_kept, t + 1)
                for h in range(NH):
                    hs = slice(c * h, c * h + c)
                    if not last:
                        pe.matmul(ps[2 * par + 1][0:c, hs], st["Y"][0:c, hs], pk[0:c, hs], start=True, stop=False)
                    ins = pe.matmul(ps[2 * par + 1][0:c, hs], pk[0:c, hs], st["Y"][0:c, hs], start=last, stop=True)
                    if h == NH - 1:
                        ins.then_inc(xy_made[par], 1)
                    if (t, k) in ((2, 4), (1, 5)):
                        sample_products(h if k == 4 else 3 * NH + h)

            def make_w(t):
                c, st, tb = rows(t), gd[cset(t)], tmpb[parity(t)]
                pe.wait_ge(xy_kept[parity(t)], level_at(t, (SMALL_LEVELS if t == 0 else LEVELS) - 1))
                for h in range(NH):
                    ins = pe.matmul(ps[2 * parity(t)][:, c * h:c * h + c], tb["kg"][0:c, P * h:P * h + P],
                                    st["Y"][0:c, c * h:c * h + c], start=True, stop=True)
                ins.then_inc(w_made, 1)

            def use_state(t):
                o, c = tile_cols(t)
                st = gd[cset(t)]
                pe.wait_ge(w_kept, t + 1)
                pe.wait_ge(s_kept, t)
                pe.wait_ge(v_kept, t)
                pe.wait_ge(qs_kept, t)
                pe.wait_ge(yb_full_s, t - 1 + t % 2)
                if t == 1:
                    pe.wait_ge(ss_kept, 2 * NH)
                for h in range(NH):
                    hs = slice(P * h, P * h + P)
                    pe.matmul(ps[4][:, hs], st["Y"][:, hs], st["vn"][:, hs], start=True, stop=False)
                    pe.matmul(ps[4][:, hs], st["wn"][:, hs], S[:, hs], start=False, stop=True)
                for h in range(NH):
                    hs = slice(P * h, P * h + P)
                    ins = pe.matmul(ps[5][:, hs], qf[:, h, o:o + c], S[:, hs], start=True, stop=True)
                ins.then_inc(v_made, 1)

            def next_state(t):
                c, st = rows(t), gd[cset(t)]
                pe.wait_ge(v_kept, t + 1)
                pe.wait_ge(o_kept, t)
                for h in range(NH):
                    hs = slice(P * h, P * h + P)
                    pe.matmul(ps[7][:, hs], st["kd"][0:c, hs], vnew[0:c, hs],
                              start=True, stop=True)
                for h in range(NH):
                    ins = pe.matmul(ps[6][0:c, P * h:P * h + P], st["qk"][0:c, c * h:c * h + c],
                                    vnew[0:c, P * h:P * h + P], start=True, stop=True)
                ins.then_inc(os_made, 1)

            def turn_o(t):
                c = rows(t)
                pe.wait_ge(o_normed, t + 1)
                if t:
                    pe.wait_ge(qs_kept, t + 1 + (t % 2))
                    pe.wait_ge(yb_full_s, t)
                else:
                    pe.wait_ge(ss_kept, 2)
                for h in range(NH):
                    ins = pe.transpose(ps[5 if t else 4][:, c * h:c * h + c], ob[0:c, P * h:P * h + P], eye[0:c, 0:c])
                ins.then_inc(o_turned, 1)

            def chain_step(k, a, b):
                if k == 1:
                    use_state(a)
                if k == 2:
                    next_state(a)
                if k == 3:
                    use_state(b)
                if k == 4:
                    turn_o(a)
                    next_state(b)
                if k == 6:
                    turn_o(b)

            def sample_states(h):
                pe.wait_ge(vm_made, h + 1)
                if h == 2:
                    pe.wait_ge(yb_full_s, 1)
                if h == 3:
                    pe.wait_ge(ss_kept, 4)
                for half in range(2):
                    ins = pe.matmul(ps[4 + 2 * (h % 2) + half][:, :], gd[4]["kd"][0:C0, P * h:P * h + P],
                                    vm[h % 2][:, 4 * half:4 * half + 4, :], start=True, stop=True)
                ins.then_inc(ss_made, 1)

            def tile0_step(m):
                st = gd[4]
                if m == 0:
                    make_w(0)
                if m == 3:
                    pe.wait_ge(ws_kept, 2)
                    for h in range(NH):
                        hs, cs = slice(P * h, P * h + P), slice(C0 * h, C0 * h + C0)
                        pe.matmul(ps[4][0:C0, hs], st["Y"][0:C0, cs], st["vn"][0:C0, hs], start=True, stop=False)
                        pe.matmul(ps[4][0:C0, hs], wsT[:, h, :], eye, start=False, stop=True)
                    for h in range(NH):
                        ins = pe.matmul(ps[5][0:C0, P * h:P * h + P], qsT[:, h, :], eye, start=True, stop=True)
                    ins.then_inc(ss_made, 1)
                if m == 4:
                    sample_states(0)
                    for h in range(NH):
                        hs, cs = slice(P * h, P * h + P), slice(C0 * h, C0 * h + C0)
                        pe.matmul(ps[7][:, hs], st["kd"][0:C0, hs], v_meta[0:C0, hs], start=True, stop=True)
                        ins = pe.matmul(ps[6][0:C0, hs], st["qk"][0:C0, cs], vnew[0:C0, hs], start=True, stop=True)
                    ins.then_inc(os_made, 1)
                if m == 5:
                    pe.wait_ge(s_kept, 1)
                    pe.wait_ge(o_kept, 1)
                    sample_states(1)
                    turn_o(0)

            pe.wait_ge(norms_done, 1)
            acc_free(pe, N_IN - 1, 2)
            for n, pr in enumerate(pairs):
                first_tiles = (0, *pr) if n == 0 else pr
                for step in (turn_kv, decay_rows, products, turn_y):
                    for t in first_tiles:
                        step(t)
                    if n == 1 and step in (turn_kv, decay_rows):
                        sample_states(2 if step == turn_kv else 3)
                    if n and step in (products, turn_y):
                        chain_step(1 if step == products else 2, *pairs[n - 1])
                for k in range(1, LEVELS):
                    now = first_tiles if k < SMALL_LEVELS else pr
                    for t in now:
                        level_p(t, k)
                    if n:
                        chain_step(k + 2, *pairs[n - 1])
                    elif k >= SMALL_LEVELS:
                        tile0_step(2 * (k - SMALL_LEVELS))
                    for t in now:
                        level_xy(t, k)
                    if n == 0 and k >= SMALL_LEVELS:
                        tile0_step(2 * (k - SMALL_LEVELS) + 1)
                for t in pr:
                    make_w(t)
            def mixed(k):
                return (ya_h[:, k, :], ya_l[:, k, :]) if k < NH else (yb_h[:, k - NH, :], yb_l[:, k - NH, :])

            ready = {N_IN: (KT, KT, NH), N_IN + 1: (KT - 1, 0, 0)}
            early = [(n, g, k) for n, g in ((N_IN, 0), (N_IN, 1), (N_IN, 2), (N_IN + 1, 0)) for k in range(ready[n][g])]
            pe.wait_ge(w_low, N_IN + 2)
            pe.wait_ge(ya_low_s, NH)
            pe.wait_ge(yb_low_s, GTILES[1][-1] + 1)
            for k in range(1, LEVELS):
                chain_step(k, *pairs[-1])
                if k == 1:
                    pe.wait_ge(w_kept, NT)
                per = -(-len(early) // (LEVELS - 1))
                for n, g, kk in early[per * (k - 1):per * k]:
                    dense_part(n, g, mixed, [kk])

            for f in range(N_OUT):
                n = N_IN + f

                def prepare(g, f=f, n=n):
                    m = 3 * f + g
                    if m == 0:
                        pe.wait_ge(o_kept, NT)
                    if m == 1:
                        pe.wait_ge(s_kept, NT)
                    if m == 2:
                        pe.wait_ge(yb_low_s, NT)
                    pe.wait_ge(x_slice[f % 2], 48 * (f // 2 + 1))
                    if m >= 2:
                        pe.wait_ge(h_sq, m - 1)
                    for t in GTILES[g]:
                        o, c = tile_cols(t)
                        ins = pe.transpose(ps[6 + m % 2][:, o - GROUPS[g][0]:o - GROUPS[g][0] + c],
                                           (xs if f else xs0)[0:c, t, :], eye[0:c, 0:c])
                    ins.then_inc(x_slice_t, 1)
                    if f >= 2:
                        acc_free(pe, n - 2, g)

                dense(n, mixed, prepare=prepare, ready=ready.get(n, (0, 0, 0)))
            pe.wait_ge(h_sq, 3 * N_OUT)
            for g, (c0, w) in enumerate(GROUPS):
                if g == 0:
                    pe.wait_ge(x_slice_kept, 3 * N_OUT)
                if g == 2:
                    pe.wait_ge(rstd_mid, 1)
                pe.matmul(ps[6 + g % 2][:, 0:w], one[:, 0:1].to_broadcast([P, P]), hsq[:, c0:c0 + w], start=True,
                          stop=True).then_inc(h_sum, 1)

            def up(g, i):
                n = N_MIX + i

                def prepare(m):
                    pe.wait_ge(acc_read_dve, g * (6 * KT) + dve_reads_to(n - 2) + m + 1)
                    if i == 0:
                        pe.wait_ge(hg_low_s, 3 * N_OUT)
                dense(n, lambda k: (hg_h[:, k, :], hg_l[:, k, :]), g0=g, prepare=prepare)

            def down(g, i, between=None):
                n = N_MIX + KT + i

                def prepare(m):
                    pe.wait_ge(acc_read_dve, g * (6 * KT) + dve_reads_to(n - 2) + m + 1)
                    if i == 0:
                        pe.wait_ge(u_low_s, g * (3 * KT) + 3 * (KT - 1) + m + 1)
                    if m == 2 and between:
                        between()
                dense(n, lambda k: (u_h[:, k, :], u_l[:, k, :]), g0=g, prepare=prepare)

            def turn_h(t):
                o, c = tile_cols(t)
                if t in GTILES[0]:
                    unread = 2
                elif t in GTILES[2] or fin_pair[t] == 4:
                    unread = 0
                else:
                    unread = 1
                pe.wait_ge(acc_read_dve, dve_reads_to(N_MIX + 2 * KT * FG) - unread)
                if fin_pair[t] in fin_pair[:t]:
                    before = max(s for s in range(t) if fin_pair[s] == fin_pair[t])
                    pe.wait_ge(fin_y, before + 1)
                for k in range(KT):
                    ins = pe.transpose(ps[fin_pair[t] + k // 4][0:c, P * (k % 4):P * (k % 4) + P], hT[:, k, o:o + c], eye)
                ins.then_inc(fin_turned, 1)

            def turn_first():
                for t in range(FIRST_FIN):
                    turn_h(t)

            with pe.Fori(0, FG - 1) as g:
                for i in range(KT):
                    up(g, i)
                for i in range(KT):
                    down(g, i)
            for i in range(KT):
                up(FG - 1, i)
            for i in range(KT):
                down(FG - 1, i, turn_first if i == KT - 1 else None)
            for t in range(FIRST_FIN, NT):
                turn_h(t)

        @block.vector
        def _(dve):
            steps = [0]

            def link(ins):
                steps[0] += 1
                ins.then_inc(dve_step, 1)
                dve.wait_ge(dve_step, steps[0])

            for g, (c0, w) in enumerate(GROUPS):
                for t in GTILES[g]:
                    dve.wait_ge(x_sq, t + 1)
                    dve.tensor_scalar(ssx[0:rows(t), t:t + 1], ssx[0:rows(t), t:t + 1], 1.0 / D, EPS, ALU.mult,
                                      ALU.add).then_inc(x_ms, 1)
                    if t == 0:
                        dve.wait_ge(rows_turned, 1)
                        dve.tensor_copy(tn[:, :], ps[0][:, 0:16]).then_inc(rows_kept, 1)
                    dve.wait_ge(x_pow, t + 1)
                    dve.tensor_scalar(x_tile(t), x_tile(t), rx[0:rows(t), t:t + 1], None, ALU.mult).then_inc(x_scaled, 1)
                for k in range(KT):
                    dve.wait_ge(x_high, KT * g + k + 1)
                    dve.scalar_tensor_tensor(out=xl[:, k, c0:c0 + w], in0=ps[turn_bank(g, k)][:, 0:w], scalar=tn[:, k:k + 1],
                                             in1=xh[:, k, c0:c0 + w].bitcast(F32), op0=ALU.mult,
                                             op1=ALU.subtract).then_inc(x_low, 1)
            dve.wait_ge(rows_turned, 2)
            dve.tensor_copy(tq[:, :, :], ps[3][:, 0:336].rearrange("p (f r) -> p f r", r=28)).then_inc(rows_kept, 1)
            dve.tensor_copy(ta[:, :, :], ps[4][:, 0:76].rearrange("p (f r) -> p f r", r=19)).then_inc(rows_kept, 1)

            def conv(zr, r, samp_w, pre, wt, taps, dst):
                zs = zr[:, 0:NSEQ * samp_w].rearrange("p (b r) -> p b r", r=samp_w)
                ds = dst[:, 0:NS].rearrange("p (b r) -> p b r", r=LSEQ)
                for j in range(taps):
                    w = wt[:, j:j + 1]
                    main = zr[:, pre + j:pre + j + PRM]
                    if j == 0:
                        dve.tensor_scalar(dst[:, NS:TOK], main, w, None, ALU.mult)
                        link(dve.tensor_scalar(ds, zs[:, :, j:j + LSEQ], w, None, ALU.mult))
                    else:
                        dve.scalar_tensor_tensor(out=dst[:, NS:TOK], in0=main, scalar=w, in1=dst[:, NS:TOK],
                                                 op0=ALU.mult, op1=ALU.add)
                        ins = dve.scalar_tensor_tensor(out=ds, in0=zs[:, :, j:j + LSEQ], scalar=w, in1=ds,
                                                       op0=ALU.mult, op1=ALU.add)
                        if j < taps - 1:
                            link(ins)
                return ins

            def keep_last(m, r):
                dve.wait_ge(last_turned, m + 1)
                if m >= 2:
                    dve.wait_ge(last_sent[m % 2], 32 * (m // 2))
                dve.tensor_copy(last_out[m % 2][0:r, :], ps[6][0:r, 0:P]).then_inc(last_kept, 1)

            def ab_first():
                dve.wait_ge(ab_turned, 1)
                dve.wait_ge(set_ones, 3)
                dve.tensor_copy(ab[0:C0, 0, :], ps[7][0:C0, 0:8])
                dve.tensor_copy(ab[:, 1:NT, :], ps[7][:, 8:8 * NT].rearrange("p (t j) -> p t j", j=8)).then_inc(ab_tok, 1)
                dve.wait_ge(ab_tok, 1)
                link(dve.tensor_tensor(sc["g"][:, :, :], ab[:, :, 0:NH], dtb[:, :].unsqueeze(1).to_broadcast([P, NT, NH]), ALU.add))
                link(dve.tensor_scalar(sc["eg"][:, :, :], sc["g"][:, :, :], -1.0, None, ALU.mult))
                dve.tensor_tensor(sc["eg"][:, :, :], sc["eg"][:, :, :], sc["g"][:, :, :], ALU.max).then_inc(ab_tok, 1)

            def ab_second():
                dve.wait_ge(ab_act, 4)
                link(dve.tensor_scalar(sc["g"][:, :, :], sc["g"][:, :, :], 0.0, None, ALU.max))
                link(dve.tensor_tensor(sc["g"][:, :, :], sc["g"][:, :, :], sc["tmp"][:, :, :], ALU.add))
                link(dve.tensor_tensor(sc["g"][:, :, :], sc["g"][:, :, :], al[:, :].unsqueeze(1).to_broadcast([P, NT, NH]), ALU.mult))
                link(dve.tensor_scalar(sc["g"][:, :, :], sc["g"][:, :, :], -1.0, None, ALU.mult))
                link(dve.tensor_scalar(sc["beta"][:, :, :], sc["beta"][:, :, :], 1.0, None, ALU.add))
                dve.reciprocal(sc["beta"][:, :, :], sc["beta"][:, :, :]).then_inc(g_ready, 1)
                dve.tensor_tensor(g_seq[0:C0, :, :], sc["g"][0:C0, 0, :].unsqueeze(1).to_broadcast([C0, NSEQ, NH]),
                                  same_s[:, 0:NS:LSEQ].unsqueeze(2).to_broadcast([C0, NSEQ, NH]), ALU.mult).then_inc(g_ready, 1)

            nk, rk, c_, p_ = sc["nk"], sc["rk"], sc["c"], sc["p"]

            def square(j):
                src = (kf if j < NH else qf)[:, j % NH, :]
                dve.wait_ge(silu_done, j + 1)
                if j >= 2:
                    dve.wait_ge(sq_low, j - 1)
                dve.tensor_tensor(sq[j % 2][:, :], src, src, ALU.mult).then_inc(sq_full, 1)

            def square_low(j):
                dve.wait_ge(sq_high, j + 1)
                if j >= 2:
                    dve.wait_ge(ss_done, j - 1)
                dve.tensor_tensor(sq_l[j % 2][:, :], sq[j % 2][:, :], sq_h[j % 2][:, :].bitcast(F32),
                                  ALU.subtract).then_inc(sq_low, 1)

            def keep_norms():
                dve.wait_ge(ss_turned, 1)
                for dst, j in ((nk, 0), (sc["rq_s"], NH)):
                    link(dve.memset(dst[:, 0, :], 1.0))
                    for g, ts in enumerate(GTILES):
                        turned = ps[7][:, 0:NROW * NT].rearrange("p (t r) -> p t r", r=NROW)
                        r0 = 2 * NH * g + j
                        if g == 0:
                            dve.tensor_scalar(dst[0:C0, 0, :], turned[0:C0, 0, r0:r0 + NH], EPS, None, ALU.add)
                            ts = ts[1:]
                        ins = dve.tensor_scalar(dst[:, ts[0]:ts[-1] + 1, :], turned[:, ts[0]:ts[-1] + 1, r0:r0 + NH],
                                                EPS, None, ALU.add)
                ins.then_inc(norms_mid, 1)

            def scale_norms():
                dve.wait_ge(norms_mid, 3)
                dve.wait_ge(g_exp, 4)
                dve.reciprocal(rk[:, :, :], nk[:, :, :])
                link(dve.reciprocal(sc["rq_s"][:, :, :], sc["rq_s"][:, :, :]))
                dve.tensor_scalar(sc["rq_s"][:, :, :], sc["rq_s"][:, :, :], float(P) ** -0.5, None, ALU.mult)
                dve.tensor_tensor(sc["kd_s"][:, :, :], rk[:, :, :], sc["egl"][:, :, :], ALU.mult)
                link(dve.tensor_tensor(c_[:, :, :], rk[:, :, :], sc["beta"][:, :, :], ALU.mult))
                dve.tensor_tensor(p_[:, :, :], c_[:, :, :], rk[:, :, :], ALU.mult).then_inc(norms_done, 1)

            for n in range(N_IN):
                kind, i, _ = IN_TILES[n]
                if kind == "gate":
                    for j in (2 * i, 2 * i + 1):
                        square(j)
                    for j in (2 * i, 2 * i + 1):
                        square_low(j)
                if n == 4 * NH:
                    dve.wait_ge(ss_done, 2 * NH)
                    dve.tensor_copy(ssr[:, :], ps[7][0:NROW, 0:3 * P]).then_inc(ss_rows, 1)
                if n == 2:
                    ab_second()
                if kind in ("k", "q", "v"):
                    f = {"q": 0, "k": NH, "v": 2 * NH}[kind] + i
                    dst = {"k": kf, "q": qf, "v": vf}[kind][:, i, :]
                    dve.wait_ge(acc_read_act, 3 * n + 3)
                    dve.wait_ge(z_hist, n + 1)
                    if n == 0:
                        dve.wait_ge(x_sq, NT)
                    conv(z[n % 2], 3, 7, 56, tq[:, f, 24:28], 4, dst).then_inc(conv_done, 1)
                if kind == "H":
                    bank = [ps[(n % 2) * 3 + g] for g in range(3)]
                    dve.wait_ge(z_hist, 3 * NH + i + 1)
                    for g, (c0, w) in enumerate(GROUPS):
                        dve.wait_ge(acc_done, 3 * n + g + 1)
                        dve.wait_ge(acc_read_act, 3 * sum(act_reads[:n]))
                        if i and g == 0:
                            dve.wait_ge(last_cols, 3 * NH + i)
                        if g == 0:
                            dve.tensor_tensor(z[1][:, 0:48].rearrange("p (b r) -> p b r", r=6)[:, :, 2:6],
                                              bank[0][:, 0:NS].rearrange("p (b r) -> p b r", r=LSEQ),
                                              z[0][:, 0:NS].rearrange("p (b r) -> p b r", r=LSEQ), ALU.mult)
                            dve.tensor_tensor(z[1][:, 50:50 + w - NS], bank[0][:, NS:w], z[0][:, NS:w],
                                              ALU.mult).then_inc(acc_read_dve, 1)
                        else:
                            ins = dve.tensor_tensor(z[1][:, 50 + c0 - NS:50 + c0 - NS + w], bank[g][:, 0:w],
                                                    z[0][:, c0:c0 + w], ALU.mult)
                            ins.then_inc(acc_read_dve, 1)
                    dve.wait_ge(acc_read_dve, dve_reads_to(n) + 3)
                    conv(z[1], 2, 6, 48, ta[:, i, 16:19], 3, z[0]).then_inc(conv_done, 1)
                if kind == "B":
                    dve.wait_ge(conv_done, 3 * NH + i + 1)
                    dve.wait_ge(last_cols, 3 * NH + i + 1)
                    for g, (c0, w) in enumerate(GROUPS):
                        dve.wait_ge(acc_done, 3 * n + g + 1)
                        dve.tensor_tensor(z[1][:, c0:c0 + w], ps[(n % 2) * 3 + g][:, 0:w], z[0][:, c0:c0 + w],
                                          ALU.mult).then_inc(acc_read_dve, 1)
                    dve.wait_ge(ya_high_s, 3 * i + 3)
                    dve.tensor_tensor(ya_l[:, i, :], z[1][:, 0:TOK], ya_h[:, i, :].bitcast(F32),
                                      ALU.subtract).then_inc(ya_low_s, 1)
                if n == 1:
                    ab_first()
                if n == 3:
                    dve.wait_ge(g_summed, 1)
                    dve.memset(sc["gneg"][:, 0, :], 0.0)
                    link(dve.memset(sc["egl"][:, 0, :], 0.0))
                    dve.memset(sc["eglb"][:, 0, :], 0.0)
                    g3 = lambda ap: ap.rearrange("p (t h) -> p t h", h=NH)
                    dve.tensor_scalar(sc["gneg"][:, 1:NT, :], g3(ps[7][:, 0:32]), -1.0, None, ALU.mult)
                    link(dve.tensor_scalar(sc["gneg"][0:C0, 0, :], ps[7][0:C0, 32:36], -1.0, None, ALU.mult))
                    dve.tensor_tensor(sc["egl"][:, 1:NT, :], g3(ps[7][:, 64:96]), sc["gneg"][:, 1:NT, :],
                                      ALU.add).then_inc(g_kept, 1)
                    dve.tensor_tensor(sc["egl"][0:C0, 0, :], ps[7][0:C0, 96:100], sc["gneg"][0:C0, 0, :],
                                      ALU.add).then_inc(g_kept, 1)
                    dve.tensor_copy(sc["eglb"][:, 1:NT, :], g3(ps[7][:, 64:96])).then_inc(g_kept, 1)
                    dve.tensor_copy(eg_seq[:, :, :], ps[7][:, 128:160].rearrange("p (b h) -> p b h", h=NH)).then_inc(g_kept, 1)
                if n == 4 * NH + 1:
                    keep_norms()
                if n == 4 * NH + 2:
                    scale_norms()
                if n and has_last(n - 1):
                    keep_last(last_index(n - 1), 18 if IN_TILES[n - 1][0] == "H" else 27)

            dve.wait_ge(norms_done, 1)

            h3 = lambda ap: ap.rearrange("p (h i) -> p h i", h=NH)

            def keep_kv(t):
                c, st, tb = rows(t), gd[cset(t)], tmpb[parity(t)]
                b0 = ps[2 * parity(t)][0:c, :]
                dve.wait_ge(kv_turned, t + 1)
                if t >= 3:
                    dve.wait_ge(w_made, t - 1)
                if t >= 5:
                    dve.wait_ge(os_made, t - 3)
                dve.tensor_tensor(h3(tb["kg"][0:c, :]), h3(b0), per_head(sc["eg"][0:c, t, :], c, P), ALU.mult)
                dve.tensor_tensor(h3(st["kd"][0:c, :]), h3(b0), per_head(sc["kd_s"][0:c, t, :], c, P), ALU.mult).then_inc(kv_kept, 1)

            def decay_diff(t):
                c, st = rows(t), gd[cset(t)]
                dve.wait_ge(g_rows, t + 1)
                for h in range(NH):
                    ins = dve.tensor_scalar(st["wn"][0:c, c * h:c * h + c], ps[2 * parity(t)][0:c, c * h:c * h + c],
                                            sc["gneg"][0:c, t, h:h + 1], 0.0, ALU.add, ALU.min)
                ins.then_inc(g_diff, 1)

            def keep_products(t, i=0):
                c, st, tb = rows(t), gd[cset(t)], tmpb[parity(t)]
                if i == 0:
                    dve.wait_ge(kk_made, t + 1)
                    dve.wait_ge(d_exp, t + 1)
                dst, s = ((tb["At"], p_), (st["qk"], rk))[i]
                for h in range(NH):
                    cs = slice(c * h, c * h + c)
                    ins = dve.scalar_tensor_tensor(out=dst[0:c, cs], in0=ps[2 * parity(t) + i][0:c, cs],
                                                   scalar=s[0:c, t, h:h + 1], in1=st["wn"][0:c, cs], op0=ALU.mult,
                                                   op1=ALU.mult)
                ins.then_inc((kk_kept, qk_kept)[i], 1)

            def keep_qk(t):
                keep_products(t, 1)

            def keep_p(t, k):
                c, par, b = rows(t), parity(t), 2 ** k
                at_level = level_at(t, k)
                dve.wait_ge(p_made[par], at_level)
                dve.wait_ge(pair_zero[par], at_level)
                m = (lev_small if t == 0 else lev_big)[k][0:c, :]
                src = ps[2 * par][0:c, 0:NH * c].rearrange("p (h n two b) -> p h n two b", h=NH, two=2, b=b)[:, :, :, 0, :]
                dst = heads(pb[par][at_level % 2], c).rearrange("p (h n two b) -> p h n two b", h=NH, two=2, b=b)[:, :, :, 0, :]
                mask = m.rearrange("p (n b) -> p n b", b=b).unsqueeze(1).to_broadcast([c, NH, c // 2 // b, b])
                dve.tensor_tensor(dst, src, mask, ALU.mult).then_inc(p_kept[par], 1)

            def keep_xy(t, k):
                c, st, tb, par, b = rows(t), gd[cset(t)], tmpb[parity(t)], parity(t), 2 ** k
                at_level, last = level_at(t, k), k == (SMALL_LEVELS if t == 0 else LEVELS) - 1
                dve.wait_ge(xy_made[par], at_level)
                made = ps[2 * par + 1][0:c, 0:NH * c]
                if not last:
                    xf = first(heads(tb["X"], c), b)
                    dve.tensor_tensor(xf, xf, first(made, b), ALU.subtract)
                ys = second(heads(st["Y"], c), b)
                dve.tensor_tensor(ys, ys, second(made, b), ALU.subtract).then_inc(xy_kept[par], 1)

            def keep_v(t):
                c = rows(t)
                dve.wait_ge(v_made, t)
                dve.wait_ge(os_made, t)
                dve.tensor_tensor(h3(vnew[0:c, :]), h3(ps[4][0:c, :]), per_head(c_[0:c, t, :], c, P),
                                  ALU.mult).then_inc(v_kept, 1)
                if t:
                    dve.wait_ge(o_sq, t)
                dve.tensor_tensor(h3(t1[0:c, :]), h3(ps[5][0:c, :]), per_head(sc["eg"][0:c, t, :], c, P),
                                  ALU.mult).then_inc(qs_kept, 1)

            def keep_state(t):
                dve.wait_ge(os_made, t + 1)
                for h in range(NH):
                    hs = slice(P * h, P * h + P)
                    ins = dve.scalar_tensor_tensor(out=S[:, hs], in0=S[:, hs], scalar=sc["eglb"][:, t, h:h + 1],
                                                   in1=ps[7][:, hs], op0=ALU.mult, op1=ALU.add)
                ins.then_inc(s_kept, 1)

            def keep_o(t):
                c = rows(t)
                dve.wait_ge(qs_kept, t + 1)
                if t:
                    dve.wait_ge(o_turned, t)
                dve.tensor_tensor(ob[0:c, :], ps[6][0:c, :], t1[0:c, :], ALU.add).then_inc(o_kept, 1)

            def norm_o(t):
                c = rows(t)
                dve.wait_ge(o_sq, t + 1)
                dve.tensor_scalar(sc["tmp"][0:c, t, :], sc["sso"][0:c, t, :], 1.0 / P, EPS, ALU.mult,
                                  ALU.add).then_inc(o_ms, 1)
                dve.wait_ge(o_pow, t + 1)
                link(dve.tensor_tensor(sc["fo"][0:c, t, :], sc["fo"][0:c, t, :], sc["rq_s"][0:c, t, :], ALU.mult))
                dve.tensor_tensor(h3(ob[0:c, :]), h3(ob[0:c, :]), per_head(sc["fo"][0:c, t, :], c, P),
                                  ALU.mult).then_inc(o_normed, 1)

            def gate_o(t):
                o, c = tile_cols(t)
                dve.wait_ge(o_turned, t + 1)
                dve.scalar_tensor_tensor(out=ybt[:, :, 0:c], in0=h3(ps[5 if t else 4][:, 0:NH * c]), scalar=gn[:, 0:1],
                                         in1=gate[:, :, o:o + c], op0=ALU.mult, op1=ALU.mult).then_inc(yb_full_s, 1)
                dve.wait_ge(yb_high_s, t + 1)
                dve.tensor_tensor(yb_l[:, :, o:o + c], ybt[:, :, 0:c], yb_h[:, :, o:o + c].bitcast(F32),
                                  ALU.subtract).then_inc(yb_low_s, 1)

            def chain_step(k, a, b):
                if k == 1:
                    keep_v(a)
                if k == 2:
                    keep_state(a)
                    keep_o(a)
                if k == 3:
                    keep_v(b)
                    norm_o(a)
                if k == 4:
                    gate_o(a)
                    keep_state(b)
                    keep_o(b)
                if k == 5:
                    norm_o(b)
                if k == 6:
                    gate_o(b)

            def mask_v(h):
                if h >= 2:
                    dve.wait_ge(ss_made, h + 1)
                dve.tensor_tensor(vm[h % 2][:, :, :], vnew[0:C0, P * h:P * h + P].unsqueeze(1).to_broadcast([C0, NSEQ, P]),
                                  same_s[:, 0:NS:LSEQ].unsqueeze(2).to_broadcast([C0, NSEQ, P]), ALU.mult).then_inc(vm_made, 1)

            def keep_sample_states(h):
                dve.wait_ge(ss_made, h + 3)
                dve.wait_ge(ss_decayed, h + 1)
                for half in range(2):
                    sh = SSs[:, h, 4 * half:4 * half + 4, :]
                    dve.tensor_tensor(sh, sh, ps[4 + 2 * (h % 2) + half][:, :].rearrange("p (b e) -> p b e", b=4),
                                      ALU.add).then_inc(ss_kept, 1)

            def tile0_step(m):
                if m == 2:
                    dve.wait_ge(ss_made, 1)
                    both = ps[6][:, 0:2 * NH * NS].rearrange("p (h b r) -> p h b r", h=NH, r=2 * LSEQ)
                    for i, dst in enumerate((wsT, qsT)):
                        dve.tensor_copy(dst[:, :, 0:NS].rearrange("p h (b r) -> p h b r", r=LSEQ),
                                        both[:, :, :, LSEQ * i:LSEQ * i + LSEQ]).then_inc(ws_kept, 1)
                if m == 3:
                    dve.wait_ge(ss_made, 2)
                    dve.tensor_tensor(h3(vnew[0:C0, :]), h3(ps[4][0:C0, :]), per_head(c_[0:C0, 0, :], C0, P),
                                      ALU.mult).then_inc(v_kept, 1)
                    dve.tensor_tensor(h3(t1[0:C0, :]), h3(ps[5][0:C0, :]), per_head(sc["eg"][0:C0, 0, :], C0, P),
                                      ALU.mult).then_inc(qs_kept, 1)
                    dve.wait_ge(v_kept, 1)
                    dve.tensor_scalar(v_meta[:, :], vnew[0:C0, :], same_s[:, NS:NS + 1], None, ALU.mult)
                    mask_v(0)
                if m == 4:
                    mask_v(1)
                    dve.wait_ge(os_made, 1)
                    keep_o(0)
                    dve.tensor_copy(S[:, :], ps[7][:, :]).then_inc(s_kept, 1)
                    keep_sample_states(0)
                    norm_o(0)
                if m == 5:
                    mask_v(2)
                    keep_sample_states(1)
                    mask_v(3)
                    gate_o(0)

            dve.wait_ge(acc_done, 3 * N_IN)
            for n, pr in enumerate(pairs):
                first_tiles = (0, *pr) if n == 0 else pr
                for step in (keep_kv, decay_diff, keep_products, keep_qk):
                    for t in first_tiles:
                        step(t)
                    if n == 1 and step in (keep_kv, decay_diff):
                        keep_sample_states(2 if step == keep_kv else 3)
                    if n and step in (keep_products, keep_qk):
                        chain_step(1 if step == keep_products else 2, *pairs[n - 1])
                for k in range(1, LEVELS):
                    now = first_tiles if k < SMALL_LEVELS else pr
                    for t in now:
                        keep_p(t, k)
                    if n:
                        chain_step(k + 2, *pairs[n - 1])
                    elif k >= SMALL_LEVELS:
                        tile0_step(2 * (k - SMALL_LEVELS))
                    for t in now:
                        keep_xy(t, k)
                    if n == 0 and k >= SMALL_LEVELS:
                        tile0_step(2 * (k - SMALL_LEVELS) + 1)
            for k in range(1, LEVELS):
                chain_step(k, *pairs[-1])

            for f in range(N_OUT):
                n = N_IN + f
                for g, (c0, w) in enumerate(GROUPS):
                    m = 3 * f + g
                    hc = hT[:, f, c0:c0 + w]
                    dve.wait_ge(x_slice_t, m + 1)
                    dve.tensor_copy(hc, ps[6 + m % 2][:, 0:w]).then_inc(x_slice_kept, 1)
                    dve.wait_ge(acc_done, 3 * n + g + 1)
                    dve.wait_ge(x_slice_kept, m + 1)
                    dve.tensor_tensor(hc, hc, ps[(n % 2) * 3 + g][:, 0:w], ALU.add).then_inc(acc_read_dve, 1)
                    dve.wait_ge(acc_read_dve, dve_reads_to(n) + g + 1)
                    hs_ = hsq[:, c0:c0 + w]
                    if f == 0:
                        dve.tensor_tensor(hs_, hc, hc, ALU.mult).then_inc(h_sq, 1)
                    else:
                        square = ps[6 + m % 2][:, 0:w]
                        link(dve.tensor_tensor(square, hc, hc, ALU.mult))
                        dve.tensor_tensor(hs_, hs_, square, ALU.add).then_inc(h_sq, 1)
                    dve.wait_ge(hg_high_s, m + 1)
                    if m == 0:
                        dve.wait_ge(out_sent, 16 * (NH + 1))
                    dve.scalar_tensor_tensor(out=hg_l[:, f, c0:c0 + w], in0=hc, scalar=tn[:, 8 + f:9 + f],
                                             in1=hg_h[:, f, c0:c0 + w].bitcast(F32), op0=ALU.mult,
                                             op1=ALU.subtract).then_inc(hg_low_s, 1)
            for g, (c0, w) in enumerate(GROUPS):
                dve.wait_ge(h_sum, g + 1)
                dve.tensor_scalar(hsq[:, c0:c0 + w], ps[6 + g % 2][:, 0:w], 1.0 / D, EPS, ALU.mult,
                                  ALU.add).then_inc(rstd_mid, 1)
            dve.wait_ge(rstd_b, 1)
            link(dve.reciprocal(hsq[:, :], hsq[:, :]))

            def up_rows(g, i):
                n = N_MIX + i
                for m, (c0, w) in enumerate(GROUPS):
                    j = 3 * i + m
                    dve.wait_ge(acc_done, g * (6 * KT) + 3 * n + m + 1)
                    ub = ut[j % 2][:, 0:w]
                    dve.tensor_tensor(ub, ps[(n % 2) * 3 + m][:, 0:w], hsq[:, c0:c0 + w], ALU.mult).then_inc(acc_read_dve, 1)
                    dve.wait_ge(acc_read_dve, g * (6 * KT) + dve_reads_to(n) + m + 1)
                    dve.scalar_tensor_tensor(out=ub, in0=ub, scalar=0.0, in1=ub, op0=ALU.max, op1=ALU.mult).then_inc(u_full, 1)
                    dve.wait_ge(u_high_s, g * (3 * KT) + j + 1)
                    dve.tensor_tensor(u_l[:, i, c0:c0 + w], ub, u_h[:, i, c0:c0 + w].bitcast(F32),
                                      ALU.subtract).then_inc(u_low_s, 1)

            def down_rows(g, i, groups=range(3)):
                n = N_MIX + KT + i
                for m in groups:
                    c0, w = GROUPS[m]
                    hc = hT[:, i, c0:c0 + w]
                    dve.wait_ge(acc_done, g * (6 * KT) + 3 * n + m + 1)
                    dve.tensor_tensor(hc, hc, ps[(n % 2) * 3 + m][:, 0:w], ALU.add)\
                       .then_inc(acc_read_dve, 1)

            with dve.Fori(0, FG - 1) as g:
                for i in range(KT):
                    up_rows(g, i)
                for i in range(KT):
                    down_rows(g, i)
            for i in range(KT):
                up_rows(FG - 1, i)
            for i in range(KT - 1):
                down_rows(FG - 1, i)
            down_rows(FG - 1, KT - 1, range(2))
            dve.wait_ge(fin_const, 16)

            def mean_square(t):
                c = rows(t)
                dve.wait_ge(fin_sq, t + 1)
                link(dve.tensor_tensor(ssx[0:c, t:t + 1], sc["sso"][0:c, t, 0:1], sc["sso"][0:c, t, 1:2], ALU.add))
                dve.tensor_scalar(ssx[0:c, t:t + 1], ssx[0:c, t:t + 1], 1.0 / D, EPS, ALU.mult, ALU.add).then_inc(fin_ms, 1)

            mean_square(0)
            for t in range(NT):
                c = rows(t)
                if t == FIRST_FIN - 1:
                    down_rows(FG - 1, KT - 1, [2])
                if t + 1 < NT:
                    mean_square(t + 1)
                dve.wait_ge(fin_pow, t + 1)
                for half in range(2):
                    ins = dve.scalar_tensor_tensor(out=yt[t % NY][0:c, 512 * half:512 * half + 512],
                                                   in0=ps[fin_pair[t] + half][0:c, :], scalar=rx[0:c, t:t + 1],
                                                   in1=nfin[0:c, 512 * half:512 * half + 512], op0=ALU.mult, op1=ALU.mult)
                ins.then_inc(fin_y, 1)


_INS = ["x_prompt", "x_sample", "state_conv_a", "state_conv_qkv", "state_ssm", "meta_tokens", "norm_mix", "w_in",
        "conv_a_w", "conv_qkv_w", "a_log", "dt_bias", "gdn_norm", "w_out", "norm_ffn", "w_up", "w_down", "norm_final"]
_OUTS = [(1, SEQ, D), (NSEQ, LSEQ, D), (1, 1, 2, CONV), (1, 1, 3, QKVW), (1, 1, NH, P, P),
         (1, NSEQ, 2, CONV), (1, NSEQ, 3, QKVW), (1, NSEQ, NH, P, P)]


def kernel(**inputs):
    import concourse.bacc as bacc
    from concourse.bass_utils import run_bass_kernel_spmd

    nc = bacc.Bacc("TRN2", target_bir_lowering=False, num_devices=1)
    arrays, args = {}, []
    tables = dict(zip(("c_main", "c_gdn"), constants()))
    for name in _INS + list(tables):
        a = np.ascontiguousarray(tables[name] if name in tables else inputs[name])
        arrays[f"in_{name}"] = a
        args.append(nc.dram_tensor(f"in_{name}", a.shape, mybir.dt.from_np(a.dtype), kind="ExternalInput").ap())
    for i, shape in enumerate(_OUTS):
        args.append(nc.dram_tensor(f"out_{i}", shape, F32, kind="ExternalOutput").ap())
    build(nc, *args)
    got = run_bass_kernel_spmd(nc, [arrays], core_ids=[0])
    return tuple(got.results[0][f"out_{i}"] for i in range(len(_OUTS)))
```
